# Optimizing a Trainium2 kernel written in Bass

```python
import math
import jax, jax.numpy as jnp
from jax import lax
import numpy as np

D_MODEL = 1024
BATCH = 1
SEQ = 1024
DEPTH = 1

SSM_WIDTH = 512
SSM_GROUP = 16
SSM_GROUPS = SSM_WIDTH // SSM_GROUP
SSM_STATE = 64
MLSTM_HEADS = 4
MLSTM_HEAD_DIM = 128
MLSTM_WIDTH = MLSTM_HEADS * MLSTM_HEAD_DIM
MLSTM_CHUNK = 64
CONV_WIDTH = 4
ATTN_HEADS = 4
ATTN_HEAD_DIM = 128
ATTN_WIDTH = ATTN_HEADS * ATTN_HEAD_DIM
Q_LORA_RANK = 256
IDX_HEADS = 8
IDX_HEAD_DIM = 64
TOPK_MAX = 256
Q_BLOCK = 128
N_BRANCH = 3
BRANCH_WIDTH = 512
EPS = 1e-6

SPLITS = (SSM_WIDTH, SSM_WIDTH,
          MLSTM_WIDTH, MLSTM_WIDTH, MLSTM_WIDTH, MLSTM_HEADS, MLSTM_HEADS, MLSTM_WIDTH,
          Q_LORA_RANK, ATTN_HEAD_DIM, ATTN_HEAD_DIM, IDX_HEAD_DIM, IDX_HEADS, ATTN_WIDTH,
          N_BRANCH * D_MODEL)
IN_WIDTH = sum(SPLITS)


def rmsnorm(x, g):
    xf = x.astype(jnp.float32)
    y = xf * lax.rsqrt(jnp.mean(xf * xf, axis=-1, keepdims=True) + EPS)
    return (y * g.astype(jnp.float32)).astype(x.dtype)

def layernorm(x, g, b):
    xf = x.astype(jnp.float32)
    mu = jnp.mean(xf, axis=-1, keepdims=True)
    xc = xf - mu
    y = xc * lax.rsqrt(jnp.mean(xc * xc, axis=-1, keepdims=True) + EPS)
    return (y * g.astype(jnp.float32) + b.astype(jnp.float32)).astype(x.dtype)

def causal_depthwise_conv(x, w, b):
    k_w, ch = w.shape
    y = lax.conv_general_dilated(x, w[:, None, :], window_strides=(1,), padding=[(k_w - 1, 0)],
                                 dimension_numbers=('NWC', 'WIO', 'NWC'), feature_group_count=ch)
    return y + b

def s5_mixer(u, a_re, a_im, b_re, b_im, c_re, c_im, log_dt, d_skip, glu_w, glu_b):
    bsz, seq, _ = u.shape
    f32 = jnp.float32
    uf = u.astype(f32).reshape(bsz, seq, SSM_GROUPS, SSM_GROUP)
    dt = jnp.exp(log_dt.astype(f32))[:, None]
    ar = a_re.astype(f32)
    ai = a_im.astype(f32)
    mag = jnp.exp(ar * dt)
    ang = ai * dt
    abar_re = mag * jnp.cos(ang)
    abar_im = mag * jnp.sin(ang)
    den = ar * ar + ai * ai
    fr = ((abar_re - 1.0) * ar + abar_im * ai) / den
    fi = (abar_im * ar - (abar_re - 1.0) * ai) / den
    br = b_re.astype(f32)
    bi = b_im.astype(f32)
    bb_re = fr[..., None] * br - fi[..., None] * bi
    bb_im = fr[..., None] * bi + fi[..., None] * br
    bu_re = jnp.einsum('blgp,gnp->blgn', uf, bb_re)
    bu_im = jnp.einsum('blgp,gnp->blgn', uf, bb_im)
    a_seq_re = jnp.broadcast_to(abar_re, bu_re.shape)
    a_seq_im = jnp.broadcast_to(abar_im, bu_im.shape)

    def combine(e1, e2):
        a1r, a1i, b1r, b1i = e1
        a2r, a2i, b2r, b2i = e2
        return (a2r * a1r - a2i * a1i, a2r * a1i + a2i * a1r,
                a2r * b1r - a2i * b1i + b2r, a2r * b1i + a2i * b1r + b2i)

    _, _, h_re, h_im = lax.associative_scan(combine, (a_seq_re, a_seq_im, bu_re, bu_im), axis=1)
    y = (jnp.einsum('blgn,gpn->blgp', h_re, c_re.astype(f32))
         - jnp.einsum('blgn,gpn->blgp', h_im, c_im.astype(f32)))
    y = y.reshape(bsz, seq, SSM_WIDTH) + d_skip.astype(f32) * u.astype(f32)
    g = jax.nn.gelu(y)
    out = g * jax.nn.sigmoid(g @ glu_w.astype(f32) + glu_b.astype(f32))
    return out.astype(u.dtype)

def mlstm_mixer(q, k, v, i_pre, f_pre, conv_w, conv_b, igate_b, fgate_b, mh_norm_g):
    bsz, seq, _ = q.shape
    f32 = jnp.float32
    qk = jax.nn.silu(causal_depthwise_conv(jnp.concatenate([q, k], axis=-1), conv_w, conv_b))
    q, k = jnp.split(qk, 2, axis=-1)
    nc = seq // MLSTM_CHUNK

    def to_chunks(t):
        t = t.astype(f32).reshape(bsz, nc, MLSTM_CHUNK, MLSTM_HEADS, -1)
        return t.transpose(1, 0, 3, 2, 4)

    def gates_to_chunks(t):
        return t.reshape(bsz, nc, MLSTM_CHUNK, MLSTM_HEADS).transpose(1, 0, 3, 2)

    qc = to_chunks(q)
    kc = to_chunks(k) * (MLSTM_HEAD_DIM ** -0.5)
    vc = to_chunks(v)
    ig = gates_to_chunks(i_pre.astype(f32) + igate_b.astype(f32))
    lf = gates_to_chunks(jax.nn.log_sigmoid(f_pre.astype(f32) + fgate_b.astype(f32)))
    causal = jnp.tril(jnp.ones((MLSTM_CHUNK, MLSTM_CHUNK), dtype=bool))

    def step(carry, xs):
        c_prev, n_prev, m_prev = carry
        qb, kb, vb, ib, fb = xs
        bcum = jnp.cumsum(fb, axis=-1)
        dmat = bcum[..., :, None] - bcum[..., None, :] + ib[..., None, :]
        dmat = jnp.where(causal, dmat, -jnp.inf)
        inter = bcum + m_prev[..., None]
        m = jnp.maximum(inter, jnp.max(dmat, axis=-1))
        dexp = jnp.exp(dmat - m[..., None])
        inter_w = jnp.exp(inter - m)
        s = jnp.einsum('bhtd,bhsd->bhts', qb, kb) * dexp
        num = (jnp.einsum('bhts,bhse->bhte', s, vb)
               + inter_w[..., None] * jnp.einsum('bhtd,bhde->bhte', qb, c_prev))
        den = jnp.sum(s, axis=-1) + inter_w * jnp.einsum('bhtd,bhd->bht', qb, n_prev)
        h = num / jnp.maximum(jnp.abs(den), jnp.exp(-m))[..., None]
        b_last = bcum[..., -1]
        g_end = b_last[..., None] - bcum + ib
        m_next = jnp.maximum(b_last + m_prev, jnp.max(g_end, axis=-1))
        w_s = jnp.exp(g_end - m_next[..., None])
        decay = jnp.exp(b_last + m_prev - m_next)
        c_next = decay[..., None, None] * c_prev + jnp.einsum('bhs,bhsd,bhse->bhde', w_s, kb, vb)
        n_next = decay[..., None] * n_prev + jnp.einsum('bhs,bhsd->bhd', w_s, kb)
        return (c_next, n_next, m_next), h

    init = (jnp.zeros((bsz, MLSTM_HEADS, MLSTM_HEAD_DIM, MLSTM_HEAD_DIM), f32),
            jnp.zeros((bsz, MLSTM_HEADS, MLSTM_HEAD_DIM), f32),
            jnp.zeros((bsz, MLSTM_HEADS), f32))
    _, hs = lax.scan(step, init, (qc, kc, vc, ig, lf))
    h = hs.transpose(1, 0, 3, 2, 4).reshape(bsz, seq, MLSTM_HEADS, MLSTM_HEAD_DIM)
    h = h * lax.rsqrt(jnp.mean(h * h, axis=-1, keepdims=True) + EPS)
    h = h.reshape(bsz, seq, MLSTM_WIDTH) * mh_norm_g.astype(f32)
    return h.astype(q.dtype)

def dsa_mixer(cq, k, v, kidx, widx, q_norm_g, w_uq, w_qidx, kidx_norm_g, kidx_norm_b):
    bsz, seq, _ = cq.shape
    f32 = jnp.float32
    cqn = rmsnorm(cq, q_norm_g)
    q = (cqn @ w_uq).reshape(bsz, seq, ATTN_HEADS, ATTN_HEAD_DIM)
    qi = (cqn @ w_qidx).reshape(bsz, seq, IDX_HEADS, IDX_HEAD_DIM)
    ki = layernorm(kidx, kidx_norm_g, kidx_norm_b).astype(f32)
    wi = widx.astype(f32) * (IDX_HEADS ** -0.5) * (IDX_HEAD_DIM ** -0.5)
    topk = min(TOPK_MAX, seq // 4)
    nb = seq // Q_BLOCK
    q_blk = q.reshape(bsz, nb, Q_BLOCK, ATTN_HEADS, ATTN_HEAD_DIM).transpose(1, 0, 2, 3, 4)
    qi_blk = qi.reshape(bsz, nb, Q_BLOCK, IDX_HEADS, IDX_HEAD_DIM).transpose(1, 0, 2, 3, 4)
    wi_blk = wi.reshape(bsz, nb, Q_BLOCK, IDX_HEADS).transpose(1, 0, 2, 3)
    starts = jnp.arange(nb, dtype=jnp.int32) * Q_BLOCK
    s_pos = jnp.arange(seq, dtype=jnp.int32)
    gather = jax.vmap(lambda kb_, ib_: kb_[ib_])

    def block(args):
        start, qb, qib, wb = args
        t = start + jnp.arange(Q_BLOCK, dtype=jnp.int32)
        rel = jax.nn.relu(jnp.einsum('bthd,bsd->bths', qib.astype(f32), ki))
        score = jnp.einsum('bth,bths->bts', wb, rel)
        causal = s_pos[None, :] <= t[:, None]
        score = jnp.where(causal[None], score, -jnp.inf)
        _, sel = lax.top_k(score, topk)
        valid = sel <= t[None, :, None]
        kg = gather(k, sel).astype(f32)
        vg = gather(v, sel).astype(f32)
        logits = jnp.einsum('bthd,btkd->bthk', qb.astype(f32), kg) * (ATTN_HEAD_DIM ** -0.5)
        logits = jnp.where(valid[:, :, None, :], logits, -jnp.inf)
        p = jax.nn.softmax(logits, axis=-1)
        return jnp.einsum('bthk,btkd->bthd', p, vg)

    o = lax.map(block, (starts, q_blk, qi_blk, wi_blk))
    o = o.transpose(1, 0, 2, 3, 4).reshape(bsz, seq, ATTN_WIDTH)
    return o.astype(cq.dtype)

def hybrid_layer(x, norm_g, w_in, ssm_a_re, ssm_a_im, ssm_b_re, ssm_b_im, ssm_c_re, ssm_c_im,
                 ssm_log_dt, ssm_d, glu_w, glu_b, qk_conv_w, qk_conv_b, igate_b, fgate_b,
                 mh_norm_g, q_norm_g, w_uq, w_qidx, kidx_norm_g, kidx_norm_b, w_branch, w_out):
    bsz, seq, _ = x.shape
    h = rmsnorm(x, norm_g)
    proj = h @ w_in
    idx = np.cumsum(np.array(SPLITS))[:-1].tolist()
    (u_a, z_a, q_b, k_b, v_b, i_b, f_b, z_b,
     cq_c, k_c, v_c, kidx_c, widx_c, z_c, gate_pre) = jnp.split(proj, idx, axis=-1)
    y_a = s5_mixer(u_a, ssm_a_re, ssm_a_im, ssm_b_re, ssm_b_im, ssm_c_re, ssm_c_im,
                   ssm_log_dt, ssm_d, glu_w, glu_b) * jax.nn.silu(z_a)
    y_b = mlstm_mixer(q_b, k_b, v_b, i_b, f_b, qk_conv_w, qk_conv_b, igate_b, fgate_b,
                      mh_norm_g) * jax.nn.silu(z_b)
    y_c = dsa_mixer(cq_c, k_c, v_c, kidx_c, widx_c, q_norm_g, w_uq, w_qidx,
                    kidx_norm_g, kidx_norm_b) * jax.nn.silu(z_c)
    ys = jnp.stack([y_a, y_b, y_c], axis=2)
    branch = jnp.einsum('blnw,nwd->blnd', ys, w_branch)
    gates = jax.nn.sigmoid(gate_pre.reshape(bsz, seq, N_BRANCH, D_MODEL))
    merged = jnp.sum(gates * branch, axis=2)
    return x + merged @ w_out

def first_inputs(seed: int = 0) -> dict:
    key = jax.random.key(seed)
    ks = jax.random.split(key, 32)
    f32 = jnp.float32
    L_, D_ = DEPTH, D_MODEL
    G, N, P = SSM_GROUPS, SSM_STATE, SSM_GROUP

    def nrm(k, shape, scale):
        return jax.random.normal(k, shape, f32) * scale

    n_idx = jnp.arange(N, dtype=f32)
    inp = {}
    inp['x'] = jax.random.normal(ks[0], (BATCH, SEQ, D_), f32)
    inp['norm_g'] = 1.0 + nrm(ks[1], (L_, D_), 0.02)
    inp['w_in'] = nrm(ks[2], (L_, D_, IN_WIDTH), D_ ** -0.5)
    inp['ssm_a_re'] = -0.5 + nrm(ks[3], (L_, G, N), 0.01)
    inp['ssm_a_im'] = math.pi * n_idx + nrm(ks[4], (L_, G, N), 0.01)
    inp['ssm_b_re'] = nrm(ks[5], (L_, G, N, P), (2.0 * P) ** -0.5)
    inp['ssm_b_im'] = nrm(ks[6], (L_, G, N, P), (2.0 * P) ** -0.5)
    inp['ssm_c_re'] = nrm(ks[7], (L_, G, P, N), (2.0 * N) ** -0.5)
    inp['ssm_c_im'] = nrm(ks[8], (L_, G, P, N), (2.0 * N) ** -0.5)
    inp['ssm_log_dt'] = jax.random.uniform(ks[9], (L_, G), f32, math.log(1e-3), math.log(1e-1))
    inp['ssm_d'] = nrm(ks[10], (L_, SSM_WIDTH), 1.0)
    inp['glu_w'] = nrm(ks[11], (L_, SSM_WIDTH, SSM_WIDTH), SSM_WIDTH ** -0.5)
    inp['glu_b'] = nrm(ks[12], (L_, SSM_WIDTH), 0.02)
    inp['qk_conv_w'] = nrm(ks[13], (L_, CONV_WIDTH, 2 * MLSTM_WIDTH), CONV_WIDTH ** -0.5)
    inp['qk_conv_b'] = nrm(ks[14], (L_, 2 * MLSTM_WIDTH), 0.02)
    inp['igate_b'] = nrm(ks[15], (L_, MLSTM_HEADS), 0.1)
    inp['fgate_b'] = jnp.linspace(3.0, 6.0, MLSTM_HEADS, dtype=f32) + nrm(ks[16], (L_, MLSTM_HEADS), 0.1)
    inp['mh_norm_g'] = 1.0 + nrm(ks[17], (L_, MLSTM_WIDTH), 0.02)
    inp['q_norm_g'] = 1.0 + nrm(ks[18], (L_, Q_LORA_RANK), 0.02)
    inp['w_uq'] = nrm(ks[19], (L_, Q_LORA_RANK, ATTN_WIDTH), Q_LORA_RANK ** -0.5)
    inp['w_qidx'] = nrm(ks[20], (L_, Q_LORA_RANK, IDX_HEADS * IDX_HEAD_DIM), Q_LORA_RANK ** -0.5)
    inp['kidx_norm_g'] = 1.0 + nrm(ks[21], (L_, IDX_HEAD_DIM), 0.02)
    inp['kidx_norm_b'] = nrm(ks[22], (L_, IDX_HEAD_DIM), 0.02)
    inp['w_branch'] = nrm(ks[23], (L_, N_BRANCH, BRANCH_WIDTH, D_), BRANCH_WIDTH ** -0.5)
    inp['w_out'] = nrm(ks[24], (L_, D_, D_), D_ ** -0.5)
    inp['final_norm_g'] = 1.0 + nrm(ks[25], (D_,), 0.02)
    return inp

def first_block(x, norm_g, w_in, ssm_a_re, ssm_a_im, ssm_b_re, ssm_b_im, ssm_c_re, ssm_c_im,
              ssm_log_dt, ssm_d, glu_w, glu_b, qk_conv_w, qk_conv_b, igate_b, fgate_b,
              mh_norm_g, q_norm_g, w_uq, w_qidx, kidx_norm_g, kidx_norm_b, w_branch, w_out,
              final_norm_g):
    for l in range(DEPTH):
        x = hybrid_layer(x, norm_g[l], w_in[l], ssm_a_re[l], ssm_a_im[l], ssm_b_re[l], ssm_b_im[l],
                         ssm_c_re[l], ssm_c_im[l], ssm_log_dt[l], ssm_d[l], glu_w[l], glu_b[l],
                         qk_conv_w[l], qk_conv_b[l], igate_b[l], fgate_b[l], mh_norm_g[l],
                         q_norm_g[l], w_uq[l], w_qidx[l], kidx_norm_g[l], kidx_norm_b[l],
                         w_branch[l], w_out[l])
    return rmsnorm(x, final_norm_g)


_first_inputs = first_inputs


def first_inputs(seed=0):
    import zlib

    import numpy as np

    out = dict(_first_inputs(seed))
    spreads = {}
    factors = {'norm_g': 3.931,
     'ssm_a_re': 64.0,
     'ssm_a_im': 64.0,
     'ssm_b_re': 64.0,
     'ssm_b_im': 64.0,
     'ssm_c_re': 64.0,
     'ssm_c_im': 64.0,
     'ssm_log_dt': 64.0,
     'glu_b': 59.636,
     'qk_conv_b': 59.687,
     'igate_b': 64.0,
     'mh_norm_g': 26.978,
     'q_norm_g': 8.0,
     'w_qidx': 2.74,
     'kidx_norm_g': 8.0,
     'kidx_norm_b': 8.0,
     'final_norm_g': 7.858}
    for name, (base, spread) in spreads.items():
        noise = np.random.default_rng([zlib.crc32(name.encode()), seed]).standard_normal(out[name].shape)
        drawn = base * np.exp(spread * noise) if base else spread * noise
        out[name] = __import__('jax').numpy.asarray(drawn.astype(out[name].dtype))
    for name, factor in factors.items():
        out[name] = (out[name] * factor).astype(out[name].dtype)
    return out


_narrow_inputs = first_inputs


def first_inputs(seed=0):
    out = dict(_narrow_inputs(seed))
    wider = {'glu_b': 3.66,
     'igate_b': 12.0,
     'mh_norm_g': 3.41,
     'kidx_norm_g': 4.12,
     'kidx_norm_b': 4.35,
     'final_norm_g': 3.15}
    for name, times in wider.items():
        mean = out[name].mean()
        out[name] = (mean + times * (out[name] - mean)).astype(out[name].dtype)
    return out


SB_HEADS = 8
SB_HEAD_DIM = 64
SB_WIDTH = SB_HEADS * SB_HEAD_DIM
SB_BLOCK = 128
SSD_WIDTH = D_MODEL
SSD_HEAD_DIM = 64
SSD_HEADS = SSD_WIDTH // SSD_HEAD_DIM
SSD_GROUPS = 2
SSD_STATE = 64
SSD_CONV = 4
SSD_CHUNK = 128
SSD_CONV_CH = SSD_WIDTH + 2 * SSD_GROUPS * SSD_STATE
RW_HEAD_DIM = 64
RW_WIDTH = D_MODEL // 2
RW_HEADS = RW_WIDTH // RW_HEAD_DIM
RW_DECAY_RANK = 64
RW_ICLR_RANK = 64
SB_COLS = 4 * SB_WIDTH
SSD_COLS = SSD_WIDTH + SSD_CONV_CH + SSD_HEADS
RW_COLS = 4 * RW_WIDTH + RW_DECAY_RANK + RW_ICLR_RANK
GATE_COLS = N_BRANCH * D_MODEL
N_IN = SB_COLS + SSD_COLS + RW_COLS + GATE_COLS
RMS_EPS = 1e-6
GN_EPS = 64e-5


def _split(x, sizes):
    idx = np.cumsum(sizes)[:-1].tolist()
    return jnp.split(x, idx, axis=-1)

def rms_norm(x, g):
    xf = x.astype(jnp.float32)
    y = xf * lax.rsqrt(jnp.mean(xf * xf, axis=-1, keepdims=True) + RMS_EPS)
    return (y * g.astype(jnp.float32)).astype(x.dtype)

def stick_breaking_attention(q, k, v):
    b, s, h, dh = q.shape
    scale = dh ** -0.5
    outs = []
    for i in range(s // SB_BLOCK):
        q0 = i * SB_BLOCK
        end = q0 + SB_BLOCK
        qb, kb, vb = q[:, q0:end], k[:, :end], v[:, :end]
        z = jnp.einsum('bqhd,bkhd->bhqk', qb, kb).astype(jnp.float32) * scale
        t_idx = q0 + jnp.arange(SB_BLOCK)
        s_idx = jnp.arange(end)
        mask = s_idx[None, :] < t_idx[:, None]
        log_beta = jax.nn.log_sigmoid(z)
        log_keep = jnp.where(mask, jax.nn.log_sigmoid(-z), 0.0)
        after = lax.cumsum(log_keep, axis=3, reverse=True) - log_keep
        att = jnp.where(mask, jnp.exp(log_beta + after), 0.0)
        outs.append(jnp.einsum('bhqk,bkhd->bqhd', att.astype(v.dtype), vb))
    return jnp.concatenate(outs, axis=1).reshape(b, s, h * dh)

def causal_depthwise_conv_2(x, w, bias):
    kw, ch = w.shape
    y = lax.conv_general_dilated(x, w[:, None, :], window_strides=(1,), padding=[(kw - 1, 0)],
                                 dimension_numbers=('NWC', 'WIO', 'NWC'), feature_group_count=ch)
    return y + bias

def segsum(a):
    t = a.shape[-1]
    rep = jnp.broadcast_to(a[..., None], a.shape + (t,))
    strict = jnp.tril(jnp.ones((t, t), dtype=bool), -1)
    cs = jnp.cumsum(jnp.where(strict, rep, 0), axis=-2)
    return jnp.where(jnp.tril(jnp.ones((t, t), dtype=bool)), cs, -jnp.inf)

def ssd_mixer(xbc_raw, dt_raw, conv_w, conv_b, dt_bias, a_log, d_skip):
    b, s, _ = xbc_raw.shape
    c, l, g = s // SSD_CHUNK, SSD_CHUNK, SSD_GROUPS
    j, p, n = SSD_HEADS // SSD_GROUPS, SSD_HEAD_DIM, SSD_STATE
    xbc = jax.nn.silu(causal_depthwise_conv_2(xbc_raw, conv_w, conv_b))
    xs, bm, cm = _split(xbc, [SSD_WIDTH, g * n, g * n])
    xs = xs.reshape(b, c, l, g, j, p)
    bm = bm.reshape(b, c, l, g, n)
    cm = cm.reshape(b, c, l, g, n)
    dt = jax.nn.softplus(dt_raw + dt_bias).reshape(b, c, l, g, j)
    a_head = -jnp.exp(a_log).reshape(g, j)
    da = jnp.moveaxis(dt * a_head, 2, -1)
    x_dt = xs * dt[..., None]
    a_cs = jnp.cumsum(da, axis=-1)
    decay_in = jnp.exp(segsum(da))
    cb = jnp.einsum('bclgn,bcsgn->bcgls', cm, bm)
    y_diag = jnp.einsum('bcgls,bcgjls,bcsgjp->bclgjp', cb, decay_in, x_dt)
    decay_states = jnp.exp(a_cs[..., -1:] - a_cs)
    states = jnp.einsum('bclgn,bcgjl,bclgjp->bcgjpn', bm, decay_states, x_dt)
    last = jnp.pad(jnp.moveaxis(a_cs[..., -1], 1, -1), [(0, 0), (0, 0), (0, 0), (1, 0)])
    decay_chunk = jnp.exp(segsum(last))
    states_p = jnp.concatenate([jnp.zeros_like(states[:, :1]), states], axis=1)
    new_states = jnp.einsum('bgjzc,bcgjpn->bzgjpn', decay_chunk, states_p)
    prev_states = new_states[:, :-1]
    y_off = jnp.einsum('bclgn,bcgjpn,bcgjl->bclgjp', cm, prev_states, jnp.exp(a_cs))
    y = y_diag + y_off + xs * d_skip.reshape(g, j)[:, :, None]
    return y.reshape(b, s, SSD_WIDTH)

def _rwkv7_step(state, inp):
    r_t, w_t, k_t, v_t, kk_t, a_t = inp
    sa = jnp.einsum('bhij,bhj->bhi', state, -kk_t)
    state = (state * w_t[:, :, None, :] + sa[..., None] * (kk_t * a_t)[:, :, None, :]
             + v_t[..., None] * k_t[:, :, None, :])
    y_t = jnp.einsum('bhij,bhj->bhi', state, r_t)
    return state, y_t

def rwkv7_mixer(slab, mu, w0, w_up, a0, a_up, k_k, k_a, r_k, ln_g, ln_b):
    b, s, _ = slab.shape
    hh, nn = RW_HEADS, RW_HEAD_DIM
    prev = jnp.pad(slab[:, :-1], [(0, 0), (1, 0), (0, 0)])
    mixed = slab + (prev - slab) * mu
    r, k, v, gate, w_lo, a_lo = _split(mixed, [RW_WIDTH] * 4 + [RW_DECAY_RANK, RW_ICLR_RANK])
    w = -jax.nn.softplus(-(w0 + jnp.tanh(w_lo) @ w_up)) - 0.5
    decay = jnp.exp(-jnp.exp(w.astype(jnp.float32)))
    a = jax.nn.sigmoid(a0 + a_lo @ a_up)
    kk = (k * k_k).reshape(b, s, hh, nn).astype(jnp.float32)
    kk = kk / jnp.maximum(jnp.sqrt(jnp.sum(kk * kk, axis=-1, keepdims=True)), 1e-12)
    k = k * (1 + (a - 1) * k_a)
    heads = lambda t: t.reshape(b, s, hh, nn).astype(jnp.float32)
    r4, k4, v4, a4, w4 = heads(r), heads(k), heads(v), heads(a), heads(decay)
    seq_first = lambda t: jnp.moveaxis(t, 1, 0)
    state0 = jnp.zeros((b, hh, nn, nn), jnp.float32)
    _, ys = lax.scan(_rwkv7_step, state0,
                     (seq_first(r4), seq_first(w4), seq_first(k4), seq_first(v4), seq_first(kk), seq_first(a4)))
    y = jnp.moveaxis(ys, 0, 1)
    mean = jnp.mean(y, axis=-1, keepdims=True)
    var = jnp.mean(jnp.square(y - mean), axis=-1, keepdims=True)
    y = ((y - mean) * lax.rsqrt(var + GN_EPS)).reshape(b, s, RW_WIDTH) * ln_g + ln_b
    bonus = jnp.sum(r4 * k4 * r_k, axis=-1, keepdims=True) * v4
    y = y + bonus.reshape(b, s, RW_WIDTH)
    return y.astype(slab.dtype), gate

def hybrid_layer_2(x, norm_g, w_in, conv_w, conv_b, dt_bias, a_log, d_skip, ssd_norm_g,
                 rw_mu, rw_w0, rw_w_up, rw_a0, rw_a_up, rw_k_k, rw_k_a, rw_r_k, rw_ln_g, rw_ln_b,
                 w_out_sb, w_out_ssd, w_out_rw, w_o):
    b, s, _ = x.shape
    h = rms_norm(x, norm_g)
    proj = h @ w_in
    sb_cols, ssd_cols, rw_cols, gate_cols = _split(proj, [SB_COLS, SSD_COLS, RW_COLS, GATE_COLS])
    q, k, v, sb_gate = _split(sb_cols, [SB_WIDTH] * 4)
    shp = (b, s, SB_HEADS, SB_HEAD_DIM)
    y_sb = stick_breaking_attention(q.reshape(shp), k.reshape(shp), v.reshape(shp)) * jax.nn.silu(sb_gate)
    z, xbc, dt_raw = _split(ssd_cols, [SSD_WIDTH, SSD_CONV_CH, SSD_HEADS])
    y_ssd = ssd_mixer(xbc, dt_raw, conv_w, conv_b, dt_bias, a_log, d_skip)
    y_ssd = rms_norm(y_ssd * jax.nn.silu(z), ssd_norm_g)
    y_rw, rw_gate = rwkv7_mixer(rw_cols, rw_mu, rw_w0, rw_w_up, rw_a0, rw_a_up, rw_k_k, rw_k_a,
                                rw_r_k, rw_ln_g, rw_ln_b)
    y_rw = y_rw * jax.nn.silu(rw_gate)
    g_sb, g_ssd, g_rw = _split(jax.nn.sigmoid(gate_cols), [D_MODEL] * N_BRANCH)
    merged = g_sb * (y_sb @ w_out_sb) + g_ssd * (y_ssd @ w_out_ssd) + g_rw * (y_rw @ w_out_rw)
    return x + merged @ w_o

def second_inputs(seed: int = 0) -> dict:
    key = jax.random.key(seed)
    ks = jax.random.split(key, 24)
    f32 = jnp.float32
    nrm = lambda k, shp, sc: jax.random.normal(k, shp, f32) * sc
    dt0 = jnp.exp(jax.random.uniform(ks[5], (DEPTH, SSD_HEADS), f32, np.log(1e-3), np.log(1e-1)))
    return {
        "x": nrm(ks[0], (BATCH, SEQ, D_MODEL), 1.0),
        "norm_g": 1.0 + nrm(ks[1], (DEPTH, D_MODEL), 0.02),
        "w_in": nrm(ks[2], (DEPTH, D_MODEL, N_IN), D_MODEL ** -0.5),
        "conv_w": nrm(ks[3], (DEPTH, SSD_CONV, SSD_CONV_CH), SSD_CONV ** -0.5),
        "conv_b": nrm(ks[4], (DEPTH, SSD_CONV_CH), 0.02),
        "dt_bias": dt0 + jnp.log(-jnp.expm1(-dt0)),
        "a_log": jnp.log(jax.random.uniform(ks[6], (DEPTH, SSD_HEADS), f32, 1.0, 16.0)),
        "d_skip": 1.0 + nrm(ks[7], (DEPTH, SSD_HEADS), 0.02),
        "ssd_norm_g": 1.0 + nrm(ks[8], (DEPTH, SSD_WIDTH), 0.02),
        "rw_mu": jax.random.uniform(ks[9], (DEPTH, RW_COLS), f32, 0.0, 1.0),
        "rw_w0": jax.random.uniform(ks[10], (DEPTH, RW_WIDTH), f32, -6.0, -1.0),
        "rw_w_up": nrm(ks[11], (DEPTH, RW_DECAY_RANK, RW_WIDTH), 0.1),
        "rw_a0": nrm(ks[12], (DEPTH, RW_WIDTH), 0.1),
        "rw_a_up": nrm(ks[13], (DEPTH, RW_ICLR_RANK, RW_WIDTH), 0.1),
        "rw_k_k": 0.85 + nrm(ks[14], (DEPTH, RW_WIDTH), 0.02),
        "rw_k_a": 1.0 + nrm(ks[15], (DEPTH, RW_WIDTH), 0.02),
        "rw_r_k": nrm(ks[16], (DEPTH, RW_HEADS, RW_HEAD_DIM), 0.1),
        "rw_ln_g": 1.0 + nrm(ks[17], (DEPTH, RW_WIDTH), 0.02),
        "rw_ln_b": nrm(ks[18], (DEPTH, RW_WIDTH), 0.02),
        "w_out_sb": nrm(ks[19], (DEPTH, SB_WIDTH, D_MODEL), SB_WIDTH ** -0.5),
        "w_out_ssd": nrm(ks[20], (DEPTH, SSD_WIDTH, D_MODEL), SSD_WIDTH ** -0.5),
        "w_out_rw": nrm(ks[21], (DEPTH, RW_WIDTH, D_MODEL), RW_WIDTH ** -0.5),
        "w_o": nrm(ks[22], (DEPTH, D_MODEL, D_MODEL), D_MODEL ** -0.5),
        "final_g": 1.0 + nrm(ks[23], (D_MODEL,), 0.02),
    }

def second_block(x, norm_g, w_in, conv_w, conv_b, dt_bias, a_log, d_skip, ssd_norm_g,
              rw_mu, rw_w0, rw_w_up, rw_a0, rw_a_up, rw_k_k, rw_k_a, rw_r_k, rw_ln_g, rw_ln_b,
              w_out_sb, w_out_ssd, w_out_rw, w_o, final_g):
    for i in range(DEPTH):
        x = hybrid_layer_2(x, norm_g[i], w_in[i], conv_w[i], conv_b[i], dt_bias[i], a_log[i], d_skip[i],
                         ssd_norm_g[i], rw_mu[i], rw_w0[i], rw_w_up[i], rw_a0[i], rw_a_up[i], rw_k_k[i],
                         rw_k_a[i], rw_r_k[i], rw_ln_g[i], rw_ln_b[i], w_out_sb[i], w_out_ssd[i],
                         w_out_rw[i], w_o[i])
    return rms_norm(x, final_g)


_first_inputs_2 = second_inputs


def second_inputs(seed=0):
    import zlib

    import numpy as np

    out = dict(_first_inputs_2(seed))
    spreads = {}
    factors = {'norm_g': 2.904,
     'conv_b': 40.76,
     'd_skip': 64.0,
     'ssd_norm_g': 53.968,
     'rw_w_up': 6.82,
     'rw_a0': 6.952,
     'rw_k_k': 64.0,
     'rw_k_a': 8.0,
     'rw_ln_g': 64.0,
     'rw_ln_b': 64.0,
     'final_g': 8.442}
    for name, (base, spread) in spreads.items():
        noise = np.random.default_rng([zlib.crc32(name.encode()), seed]).standard_normal(out[name].shape)
        drawn = base * np.exp(spread * noise) if base else spread * noise
        out[name] = __import__('jax').numpy.asarray(drawn.astype(out[name].dtype))
    for name, factor in factors.items():
        out[name] = (out[name] * factor).astype(out[name].dtype)
    return out


_narrow_inputs_2 = second_inputs


def second_inputs(seed=0):

    out = dict(_narrow_inputs_2(seed))
    wider = {'d_skip': 12.0,
     'ssd_norm_g': 8.26,
     'rw_k_k': 11.72,
     'rw_ln_g': 4.29,
     'rw_ln_b': 4.36,
     'final_g': 3.27}
    for name, times in wider.items():
        mean = out[name].mean()
        out[name] = (mean + times * (out[name] - mean)).astype(out[name].dtype)
    return out


def setup_inputs(seed=0):
    out = dict(first_inputs(seed))
    for name, value in second_inputs(seed + 1).items():
        if name != "x":
            out[name + "_2"] = value
    return out


def reference(
    x, norm_g, w_in, ssm_a_re, ssm_a_im, ssm_b_re, ssm_b_im, ssm_c_re, ssm_c_im, ssm_log_dt,
    ssm_d, glu_w, glu_b, qk_conv_w, qk_conv_b, igate_b, fgate_b, mh_norm_g, q_norm_g, w_uq,
    w_qidx, kidx_norm_g, kidx_norm_b, w_branch, w_out, final_norm_g, norm_g_2, w_in_2, conv_w_2,
    conv_b_2, dt_bias_2, a_log_2, d_skip_2, ssd_norm_g_2, rw_mu_2, rw_w0_2, rw_w_up_2, rw_a0_2,
    rw_a_up_2, rw_k_k_2, rw_k_a_2, rw_r_k_2, rw_ln_g_2, rw_ln_b_2, w_out_sb_2, w_out_ssd_2,
    w_out_rw_2, w_o_2, final_g_2,
):
    x = first_block(
        x, norm_g, w_in, ssm_a_re, ssm_a_im, ssm_b_re, ssm_b_im, ssm_c_re, ssm_c_im, ssm_log_dt,
        ssm_d, glu_w, glu_b, qk_conv_w, qk_conv_b, igate_b, fgate_b, mh_norm_g, q_norm_g, w_uq,
        w_qidx, kidx_norm_g, kidx_norm_b, w_branch, w_out, final_norm_g,
    )
    return second_block(
        x, norm_g_2, w_in_2, conv_w_2, conv_b_2, dt_bias_2, a_log_2, d_skip_2, ssd_norm_g_2,
        rw_mu_2, rw_w0_2, rw_w_up_2, rw_a0_2, rw_a_up_2, rw_k_k_2, rw_k_a_2, rw_r_k_2,
        rw_ln_g_2, rw_ln_b_2, w_out_sb_2, w_out_ssd_2, w_out_rw_2, w_o_2, final_g_2,
    )


_drawn_inputs = setup_inputs


def setup_inputs(seed=0):
    import zlib

    import numpy as np

    out = dict(_drawn_inputs(seed))
    spreads = {}
    factors = {}
    for name, (base, spread) in spreads.items():
        noise = np.random.default_rng([zlib.crc32(name.encode()), seed]).standard_normal(out[name].shape)
        drawn = base * np.exp(spread * noise) if base else spread * noise
        out[name] = __import__('jax').numpy.asarray(drawn.astype(out[name].dtype))
    for name, factor in factors.items():
        out[name] = (out[name] * factor).astype(out[name].dtype)
    return out
```

```python
import math
from contextlib import ExitStack

import numpy as np

import concourse.bass as bass
from concourse import mybir

F32 = mybir.dt.float32
I32 = mybir.dt.int32
ALU = mybir.AluOpType
ACT = mybir.ActivationFunctionType
AX = mybir.AxisListType

P = 128
BANK = 512
D = 1024
T = 1024
KD = D // P
NB = T // P
HALVES = T // BANK
EPS = 1e-6
TAKEN = -3.0e38
FUTURE = -1.0e38
DROP = -1.0e30


class Step:
    __slots__ = ("queue", "needed", "count")

    def __init__(self, queue):
        self.queue, self.needed, self.count = queue, False, None


class Landed:
    __slots__ = ("sem", "value")

    def __init__(self, sem, value):
        self.sem, self.value = sem, value


def flatten(producers):
    flat = []
    for x in producers:
        if isinstance(x, (list, tuple)):
            flat.extend(flatten(x))
        elif x is not None:
            flat.append(x)
    return flat


class Queue:

    def __init__(self, engine, sem):
        self.engine, self.sem, self.items, self.last = engine, sem, [], None

    def __call__(self, emit, *producers):
        flat = flatten(producers)
        for x in flat:
            if isinstance(x, Step):
                x.needed = True
        step = Step(self)
        self.items.append((emit, flat, step))
        self.last = step
        return step

    def number(self):
        n = 0
        for _, _, step in self.items:
            if step.needed:
                n += 1
                step.count = n

    def play(self):
        reached = {}
        for emit, producers, step in self.items:
            wanted = {}
            for x in producers:
                sem, value = (x.queue.sem, x.count) if isinstance(x, Step) else (x.sem, x.value)
                wanted[sem.name] = (sem, max(value, wanted.get(sem.name, (sem, 0))[1]))
            for name, (sem, value) in wanted.items():
                if value > reached.get(name, 0):
                    self.engine.wait_ge(sem, value)
                    reached[name] = value
            if emit is None:
                continue
            done = emit(self.engine)
            if step.needed:
                done.then_inc(self.sem, 1)


class Slot:

    def __init__(self, view, sem):
        self.view, self.sem, self.filled, self.readers = view, sem, 0, []

    def fill(self, queue, pieces, *producers):
        waits = [self.readers, list(producers)]
        for out, src in pieces:
            self.filled += 16
            last = queue.last
            queue(lambda e, out=out, src=src: e.dma_start(out, src).then_inc(self.sem, 16), *waits)
            queue.last = last
            waits = []
        self.readers = []
        return Landed(self.sem, self.filled)


class Bank:

    def __init__(self, view):
        self.view, self.readers = view, []


class Machine:

    def __init__(self, nc, ctx):
        self.nc, self.ctx = nc, ctx
        self.pe = Queue(nc.tensor, self.sem("pe_done"))
        self.act = Queue(nc.scalar, self.sem("act_done"))
        self.dve = Queue(nc.vector, self.sem("dve_done"))
        self.pool = Queue(nc.gpsimd, self.sem("pool_done"))
        self.sp = Queue(nc.sync, self.sem("sp_done"))
        self.banks = [Bank(ctx.enter_context(nc.psum_tensor(f"bank{i}", [P, BANK], F32))[:, :]) for i in range(8)]
        self.next_bank = 0
        self.ring = list(range(6))
        self.held = self.banks[6:8]
        self.arena = ctx.enter_context(nc.sbuf_tensor("arena", [P, 53200], F32))
        self.top = 0
        self.peak = 0

    def sem(self, name):
        return self.ctx.enter_context(self.nc.semaphore(name))

    def take(self, *shape):
        n = int(np.prod(shape))
        view = self.arena[:, self.top:self.top + n]
        self.top += n
        self.peak = max(self.peak, self.top)
        assert self.top <= 53200, self.top
        if len(shape) == 2:
            view = view.rearrange("p (a b) -> p a b", a=shape[0])
        elif len(shape) == 3:
            view = view.rearrange("p (a b c) -> p a b c", a=shape[0], b=shape[1])
        elif len(shape) == 4:
            view = view.rearrange("p (a b c d) -> p a b c d", a=shape[0], b=shape[1], c=shape[2])
        return view

    def slot(self, name, *shape):
        return Slot(self.take(*shape), self.sem(name))

    def bank(self):
        b = self.banks[self.ring[self.next_bank % len(self.ring)]]
        self.next_bank += 1
        return b

    def fence(self, queues=None):
        return [q.last for q in (self.pe, self.act, self.dve, self.pool) if q.last is not None]

    def play(self):
        for q in (self.pe, self.act, self.dve, self.pool, self.sp):
            q.number()
        for q in (self.pe, self.act, self.dve, self.pool, self.sp):
            q.play()


def bc(ap, shape):
    return ap.to_broadcast(shape)



def make_constants(m, c):
    c.ident = m.take(P)
    c.ones = m.take(P)
    c.zero = m.take(1)
    c.upper = m.take(P)
    c.tail_t = m.take(P)
    c.pair_ones = m.take(P)
    pool = m.pool

    def fill(view, value):
        return pool(lambda e: e.memset(view, value))

    def keep(view, cmp, pattern, base, channel, value, after):
        return pool(lambda e: e.affine_select(out=view, in_=view, compare_op=cmp, fill=value, base=base,
                                              pattern=pattern, channel_multiplier=channel), after)

    s = fill(c.ident, 0.0)
    c.ident_ready = keep(c.ident, ALU.not_equal, [[-1, P]], 0, 1, 1.0, s)
    fill(c.zero, 0.0)
    s = fill(c.upper, 1.0)
    keep(c.upper, ALU.is_ge, [[1, P]], 0, -1, 0.0, s)
    s = fill(c.tail_t, 1.0)
    keep(c.tail_t, ALU.is_ge, [[-1, P]], 0, 1, 0.0, s)
    s = m.dve(lambda e: e.memset(c.pair_ones, 0.0))
    m.dve(lambda e: e.memset(c.pair_ones[0:64, 0:64], 1.0), s)
    c.pair_ready = m.dve(lambda e: e.memset(c.pair_ones[64:128, 64:128], 1.0), s)
    c.stacked_ident = m.take(64)
    s = fill(c.stacked_ident, 0.0)
    s = keep(c.stacked_ident, ALU.not_equal, [[-1, 64]], 0, 1, 1.0, s)
    c.stacked_ready = keep(c.stacked_ident, ALU.not_equal, [[-1, 64]], -64, 1, 1.0, s)
    c.ready = fill(c.ones, 1.0)


def root_of_inverse(m, view, *ready):
    s = m.dve(lambda e: e.reciprocal(view, view), *ready)
    return m.act(lambda e: e.activation(view, view, ACT.Sqrt), s)


def rms_rows(m, c, src, ready, square_tmp, out):
    banks = [m.bank() for _ in range(HALVES)]
    free = [None, None]
    step = None
    for k in range(KD):
        sq = m.act(lambda e, k=k: e.activation(square_tmp[:, k % 2, :], src[:, k, :], ACT.Square),
                   ready(k), free[k % 2])
        for n in range(HALVES):
            cols = slice(n * BANK, (n + 1) * BANK)
            step = m.pe(lambda e, k=k, n=n, cols=cols: e.matmul(banks[n].view, c.ones, square_tmp[:, k % 2, cols],
                                                                start=(k == 0), stop=(k == KD - 1)),
                        sq, c.ready, banks[n].readers if k == 0 else None)
        free[k % 2] = step
    for n in range(HALVES):
        cols = slice(n * BANK, (n + 1) * BANK)
        s = m.dve(lambda e, n=n, cols=cols: e.tensor_scalar(out[:, cols], banks[n].view, 1.0 / D, EPS,
                                                            ALU.mult, ALU.add), step)
        banks[n].readers = [s]
    return root_of_inverse(m, out, s)


def load_weights(m, w, n0, n1, kt=KD):
    slot = m.weights[m.next_weight % len(m.weights)]
    m.next_weight += 1
    n = n1 - n0
    view = slot.view[:, 0:kt * n].rearrange("p (k n) -> p k n", k=kt)
    landed = slot.fill(m.sp, [(view, w.rearrange("(k p) n -> p k n", p=P)[:, :, n0:n1])])
    return slot, view, landed


def project_channels(m, src, ready, slot, w, landed, cols, evacuate, kt=KD, halves=HALVES, bank=BANK):
    for i, (c0, c1) in enumerate(cols):
        for n in range(halves):
            b = m.bank()
            step = None
            for k in range(kt):
                step = m.pe(lambda e, k=k, n=n, b=b, c0=c0, c1=c1: e.matmul(b.view[0:c1 - c0, 0:bank], w[:, k, c0:c1],
                                                              src[:, k, n * bank:(n + 1) * bank],
                                                              start=(k == 0), stop=(k == kt - 1)),
                            landed, ready, b.readers if k == 0 else None)
            b.readers = [evacuate(i, n, b.view[0:c1 - c0, 0:bank], step)]
            slot.readers = [step]


def project_tokens(m, src, ready, slot, w, landed, c0, c1, evacuate, kt=KD):
    for blk in range(NB):
        b = m.bank()
        step = None
        for k in range(kt):
            step = m.pe(lambda e, k=k, b=b, blk=blk: e.matmul(b.view[:, 0:c1 - c0], src[:, k, blk * P:(blk + 1) * P],
                                                              w[:, k, c0:c1], start=(k == 0), stop=(k == kt - 1)),
                        landed, ready, b.readers if k == 0 else None)
        b.readers = [evacuate(blk, b.view[:, 0:c1 - c0], step)]
        slot.readers = [step]


TILES4 = [(i * P, (i + 1) * P) for i in range(4)]


class Merge:

    def __init__(self, m, c):
        self.merged = m.take(KD, T)
        self.sig = m.take(3, BANK)
        self.sig_free = [None] * 3
        self.written = {}
        self.turn = 0
        self.branch = 0
        self.last = None

    def add(self, m, hT, h_ready, w_in, gate0, w_branch, y, y_ready, kt):
        for half in range(2):
            gslot, gw, gl = load_weights(m, w_in, gate0 + half * BANK, gate0 + (half + 1) * BANK)
            bslot, bw, bl = load_weights(m, w_branch, half * BANK, (half + 1) * BANK, kt)
            for i in range(4):
                d = half * 4 + i
                for n in range(HALVES):
                    cols = slice(n * BANK, (n + 1) * BANK)
                    j = self.turn % 3
                    self.turn += 1
                    g = m.bank()
                    for k in range(KD):
                        gs = m.pe(lambda e, k=k, g=g, gw=gw, i=i, cols=cols: e.matmul(
                            g.view, gw[:, k, i * P:(i + 1) * P], hT[:, k, cols], start=(k == 0), stop=(k == KD - 1)),
                            gl, h_ready, g.readers if k == 0 else None)
                    b = m.bank()
                    for k in range(kt):
                        bs = m.pe(lambda e, k=k, b=b, bw=bw, i=i, cols=cols: e.matmul(
                            b.view, bw[:, k, i * P:(i + 1) * P], y[:, k, cols], start=(k == 0), stop=(k == kt - 1)),
                            bl, y_ready, b.readers if k == 0 else None)
                    sig = m.act(lambda e, g=g, j=j: e.activation(self.sig[:, j, :], g.view, ACT.Sigmoid),
                                gs, self.sig_free[j])
                    g.readers = [sig]
                    dst = self.merged[:, d, cols]
                    if self.branch == 0:
                        s = m.dve(lambda e, b=b, j=j, dst=dst: e.tensor_tensor(dst, b.view, self.sig[:, j, :], ALU.mult),
                                  sig, bs)
                        b.readers = [s]
                    else:
                        s = m.dve(lambda e, b=b, j=j: e.tensor_tensor(self.sig[:, j, :], b.view, self.sig[:, j, :], ALU.mult),
                                  sig, bs)
                        b.readers = [s]
                        s = m.pool(lambda e, j=j, dst=dst: e.tensor_tensor(dst, dst, self.sig[:, j, :], ALU.add),
                                   s, self.written[d, n])
                    self.sig_free[j] = s
                    self.written[d, n] = s
            gslot.readers, bslot.readers = [gs], [bs]
        self.branch += 1
        self.last = bs


def gate_with_silu(m, hT, h_ready, w_in, c0, y, y_ready, kt=4):
    done = []
    tmp = m.silu_tmp
    for g in range(kt // 4):
        slot, w, landed = load_weights(m, w_in, c0 + g * BANK, c0 + (g + 1) * BANK)

        def evacuate(i, n, ps, step):
            j = m.silu_turn % 2
            m.silu_turn += 1
            cols = slice(n * BANK, (n + 1) * BANK)
            a = m.act(lambda e: e.activation(tmp[:, j, :], ps, ACT.Silu), step, m.silu_free[j])
            s = m.dve(lambda e: e.tensor_tensor(y[:, g * 4 + i, cols], y[:, g * 4 + i, cols], tmp[:, j, :], ALU.mult),
                      a, y_ready)
            m.silu_free[j] = s
            done.append(s)
            return a

        project_channels(m, hT, h_ready, slot, w, landed, TILES4, evacuate)
    return done[-1]



TOPK = 256
AH, AD = 4, 128
IH, ID = 8, 64
QR = 256


def dsa(m, c, io, hT, h_ready, y, fence):
    w_in = io["w_in"]
    C0 = 2 * 512 + 3 * 512 + 8 + 512
    K0 = C0 + QR
    V0 = K0 + AD
    NTOK = QR + AD + ID + IH
    tok = m.take(NB, NTOK)
    kT = m.take(T)
    kiT = m.take(T)
    cqT = m.take(2, T)
    qT = m.take(4, T)
    qiT = m.take(4, T)
    score = [m.take((b + 1) * P) for b in range(NB)]
    ki2 = m.take(NB, 2, ID)
    sq = m.take(NB, ID)
    stat = m.take(6, NB)
    wi = m.take(NB, IH)
    best = m.take(8)
    relu = m.take(2, BANK)
    prob = m.take(2, T)
    probT = m.take(2, T)
    small = m.take(2, 8)
    att = m.take(2, BANK)

    slot = m.weights[m.next_weight % len(m.weights)]
    m.next_weight += 1
    w = slot.view[:, 0:KD * NTOK].rearrange("p (k n) -> p k n", k=KD)
    src = w_in.rearrange("(k p) n -> p k n", p=P)
    landed = slot.fill(m.sp, [(w[:, :, 0:QR], src[:, :, C0:C0 + QR]), (w[:, :, QR:NTOK], src[:, :, V0:V0 + NTOK - QR])])
    tok_done = []

    def evac_tok(blk, ps, step):
        s = m.act(lambda e: e.activation(tok[:, blk, :], ps, ACT.Copy), step, fence)
        tok_done.append(s)
        return s

    project_tokens(m, hT, h_ready, slot, w, landed, 0, NTOK, evac_tok)
    slot, w, landed = load_weights(m, w_in, K0, K0 + AD)
    k_done = []

    def evac_k(i, n, ps, step):
        s = m.act(lambda e: e.activation(kT[:, n * BANK:(n + 1) * BANK], ps, ACT.Copy), step, fence)
        k_done.append(s)
        return s

    project_channels(m, hT, h_ready, slot, w, landed, [(0, AD)], evac_k)

    junk = prob[:, 0, 0:QR]
    s = None
    for blk in range(NB):
        s = m.act(lambda e, blk=blk: e.activation(junk, tok[:, blk, 0:QR], ACT.Square, accum_out=stat[:, 0, blk:blk + 1]),
                  tok_done[blk], s)
    s = m.dve(lambda e: e.tensor_scalar(stat[:, 1, :], stat[:, 0, :], 1.0 / QR, EPS, ALU.mult, ALU.add), s, fence)
    s = root_of_inverse(m, stat[:, 1, :], s)
    s = m.dve(lambda e: e.tensor_tensor(tok[:, :, 0:QR], tok[:, :, 0:QR],
                                        stat[:, 1, :].unsqueeze(2).to_broadcast([P, NB, QR]), ALU.mult), s)
    cq_done = []
    for j in range(2):
        for g in range(2):
            b = m.bank()
            for i in range(4):
                blk = g * 4 + i
                t = m.pe(lambda e, b=b, i=i, blk=blk, j=j: e.transpose(
                    b.view[:, i * P:(i + 1) * P], tok[:, blk, j * P:(j + 1) * P], c.ident), s, c.ready,
                    b.readers if i == 0 else None)
            t = m.act(lambda e, b=b, j=j, g=g: e.activation(cqT[:, j, g * BANK:(g + 1) * BANK], b.view, ACT.Copy,
                                                            scale=c.vec("q_norm_g", j)), t)
            b.readers = [t]
            cq_done.append(t)

    KI = slice(QR + AD, QR + AD + ID)
    s = m.dve(lambda e: e.tensor_reduce(stat[:, 2, :], tok[:, :, KI], AX.X, ALU.add), tok_done)
    s = m.dve(lambda e: e.tensor_scalar(stat[:, 2, :], stat[:, 2, :], 1.0 / ID, None, ALU.mult), s)
    s = m.dve(lambda e: e.tensor_tensor(tok[:, :, KI], tok[:, :, KI],
                                        stat[:, 2, :].unsqueeze(2).to_broadcast([P, NB, ID]), ALU.subtract), s)
    s = m.dve(lambda e: e.tensor_tensor(sq, tok[:, :, KI], tok[:, :, KI], ALU.mult), s)
    s = m.dve(lambda e: e.tensor_reduce(stat[:, 3, :], sq, AX.X, ALU.add), s)
    s = m.dve(lambda e: e.tensor_scalar(stat[:, 3, :], stat[:, 3, :], 1.0 / ID, EPS, ALU.mult, ALU.add), s)
    s = root_of_inverse(m, stat[:, 3, :], s)
    for r in range(2):
        s2 = m.dve(lambda e, r=r: e.tensor_tensor(ki2[:, :, r, :], tok[:, :, KI],
                                                  stat[:, 3, :].unsqueeze(2).to_broadcast([P, NB, ID]), ALU.mult), s)
    ki_done = []
    for g in range(2):
        b = m.bank()
        for i in range(4):
            t = m.pe(lambda e, b=b, i=i, g=g: e.transpose(
                b.view[:, i * P:(i + 1) * P], ki2[:, g * 4 + i, :, :].rearrange("p r d -> p (r d)"), c.ident), s2,
                b.readers if i == 0 else None)
        t = m.dve(lambda e, b=b, g=g: e.tensor_scalar(kiT[:, g * BANK:(g + 1) * BANK], b.view,
                                                      c.vec("kidx_norm_g"), c.vec("kidx_norm_b"), ALU.mult, ALU.add), t)
        b.readers = [t]
        ki_done.append(t)
    wi_done = m.dve(lambda e: e.tensor_scalar(wi, tok[:, :, NTOK - IH:NTOK], float(IH) ** -0.5, float(ID) ** -0.5,
                                              ALU.mult, ALU.mult), tok_done)

    q_done = {}
    for name, dst in (("w_qidx", qiT), ("w_uq", qT)):
        slot, w, landed = load_weights(m, io[name], 0, 512, 2)

        def evac_q(i, n, ps, step, name=name, dst=dst):
            s = m.act(lambda e: e.activation(dst[:, i, n * BANK:(n + 1) * BANK], ps, ACT.Copy), step, fence)
            q_done[name] = s
            return s

        project_channels(m, cqT, cq_done, slot, w, landed, TILES4, evac_q, kt=2)

    relu_free = [None, None]
    turn = 0
    score_done = [None] * NB
    for b in range(NB):
        for c0 in range(0, (b + 1) * P, BANK):
            c1 = min(c0 + BANK, (b + 1) * P)
            prev = None
            for h in range(IH):
                r0 = ID * (h % 2)
                pb = m.bank()
                s = m.pe(lambda e, b=b, c0=c0, c1=c1, h=h, r0=r0, pb=pb: e.matmul(
                    pb.view[:, 0:c1 - c0], qiT[r0:r0 + ID, h // 2, b * P:(b + 1) * P], kiT[r0:r0 + ID, c0:c1],
                    start=True, stop=True), q_done["w_qidx"], ki_done, pb.readers)
                j = turn % 2
                turn += 1
                s = m.act(lambda e, pb=pb, j=j, n=c1 - c0: e.activation(relu[:, j, 0:n], pb.view[:, 0:n], ACT.Relu),
                          s, relu_free[j])
                pb.readers = [s]
                dst = score[b][:, c0:c1]
                if h == 0:
                    prev = m.dve(lambda e, j=j, b=b, h=h, dst=dst, n=c1 - c0: e.tensor_scalar(
                        dst, relu[:, j, 0:n], wi[:, b, h:h + 1], None, ALU.mult), s, wi_done)
                else:
                    prev = m.dve(lambda e, j=j, b=b, h=h, dst=dst, n=c1 - c0: e.scalar_tensor_tensor(
                        out=dst, in0=relu[:, j, 0:n], scalar=wi[:, b, h:h + 1], in1=dst, op0=ALU.mult, op1=ALU.add),
                        s, prev)
                relu_free[j] = prev
        diag = score[b][:, b * P:(b + 1) * P]
        score_done[b] = m.pool(lambda e, diag=diag: e.affine_select(
            out=diag, in_=diag, compare_op=ALU.is_ge, fill=FUTURE, base=0, pattern=[[-1, P]], channel_multiplier=1), prev)

    for b in range(NB):
        s = score_done[b]
        if (b + 1) * P > TOPK:
            for _ in range(TOPK // 8):
                s = m.dve(lambda e, b=b: e.max(best, score[b]), s)
                s = m.dve(lambda e, b=b: e.match_replace(score[b], best, score[b], TAKEN), s)
            s = m.dve(lambda e, b=b: e.tensor_scalar(score[b], score[b], TAKEN, DROP, ALU.not_equal, ALU.mult), s)
        else:
            s = m.dve(lambda e, b=b: e.tensor_scalar(score[b], score[b], 0.5 * FUTURE, DROP, ALU.is_lt, ALU.mult), s)
        score_done[b] = s

    SC = float(AD) ** -0.5
    y_done = []
    pfree, tfree, afree = [None, None], [None, None], [None, None]
    turn = 0
    for b in range(NB):
        N = (b + 1) * P
        out_bank = m.held[b % 2]
        first = True
        sums = small[:, b % 2, 0:AH]
        for h in range(AH):
            j = turn % 2
            turn += 1
            parts = []
            for c0 in range(0, N, BANK):
                c1 = min(c0 + BANK, N)
                pb = m.bank()
                s = m.pe(lambda e, pb=pb, c0=c0, c1=c1, h=h, b=b: e.matmul(
                    pb.view[:, 0:c1 - c0], qT[:, h, b * P:(b + 1) * P], kT[:, c0:c1], start=True, stop=True),
                    q_done["w_uq"], k_done, pb.readers)
                i = len(parts)
                s = m.dve(lambda e, pb=pb, c0=c0, c1=c1, b=b, j=j, i=i: e.tensor_tensor_reduce(
                    out=prob[:, j, c0:c1], in0=pb.view[:, 0:c1 - c0], in1=score[b][:, c0:c1], scale=1.0, scalar=-3e38,
                    op0=ALU.add, op1=ALU.max, accum_out=stat[:, 4, 2 * j + i:2 * j + i + 1]),
                    s, score_done[b], pfree[j])
                pb.readers = [s]
                parts.append(s)
            top = stat[:, 4, 2 * j:2 * j + 1]
            if len(parts) == 2:
                s = m.dve(lambda e, j=j: e.tensor_tensor(stat[:, 4, 2 * j:2 * j + 1], stat[:, 4, 2 * j:2 * j + 1],
                                                         stat[:, 4, 2 * j + 1:2 * j + 2], ALU.max), parts)
            s = m.dve(lambda e, j=j: e.tensor_scalar(stat[:, 5, j:j + 1], stat[:, 4, 2 * j:2 * j + 1], -SC, None, ALU.mult), s)
            s = m.act(lambda e, j=j, N=N, b=b, h=h: e.activation(
                prob[:, j, 0:N], prob[:, j, 0:N], ACT.Exp, bias=stat[:, 5, j:j + 1], scale=SC,
                accum_out=small[:, b % 2, h:h + 1]), s)
            last_exp = s
            for g in range(0, b + 1, 4):
                tb = m.bank()
                n = min(4, b + 1 - g)
                for i in range(n):
                    s2 = m.pe(lambda e, tb=tb, i=i, g=g, j=j: e.transpose(
                        tb.view[:, i * P:(i + 1) * P], prob[:, j, (g + i) * P:(g + i + 1) * P], c.ident), s,
                        tb.readers if i == 0 else None)
                pfree[j] = s2
                cp = m.act(lambda e, tb=tb, g=g, n=n, j=j: e.activation(
                    probT[:, j, g * P:(g + n) * P], tb.view[:, 0:n * P], ACT.Copy), s2, tfree[j])
                tb.readers = [cp]
            for i in range(b + 1):
                pv = m.pe(lambda e, i=i, j=j, h=h, b=b, ob=out_bank: e.matmul(
                    ob.view[:, h * P:(h + 1) * P], probT[:, j, i * P:(i + 1) * P], tok[:, i, QR:QR + AD],
                    start=(i == 0), stop=(i == b)), cp, out_bank.readers if first else None)
                first = False
            tfree[j] = pv
        a = b % 2
        s = m.dve(lambda e, a=a: e.reciprocal(small[:, a, 4:8], small[:, a, 0:4]), last_exp)
        s = m.dve(lambda e, a=a, ob=out_bank: e.tensor_tensor(
            att[:, a, :].rearrange("p (h d) -> p h d", h=AH), ob.view.rearrange("p (h d) -> p h d", h=AH),
            small[:, a, 4:8].unsqueeze(2).to_broadcast([P, AH, AD]), ALU.mult), s, pv, afree[a])
        out_bank.readers = [s]
        tb = m.bank()
        for h in range(AH):
            s2 = m.pe(lambda e, a=a, h=h, tb=tb: e.transpose(tb.view[:, h * P:(h + 1) * P],
                                                            att[:, a, h * P:(h + 1) * P], c.ident), s,
                      tb.readers if h == 0 else None)
        afree[a] = s2
        s = m.act(lambda e, b=b, tb=tb: e.activation(y[:, :, b * P:(b + 1) * P],
                                                     tb.view.rearrange("p (h t) -> p h t", h=AH), ACT.Copy), s2, fence)
        tb.readers = [s]
        y_done.append(s)
    return gate_with_silu(m, hT, h_ready, w_in, V0 + AD + ID + IH, y, y_done[-1])



def vector_columns(names):
    at, n = {}, 0
    for name, width in names:
        at[name] = (n, width)
        n += width
    return at, n


VECS = [("norm_g", 8), ("ssm_d", 4), ("glu_b", 4), ("qk_conv_w", 32), ("qk_conv_b", 8), ("mh_norm_g", 4),
        ("q_norm_g", 2), ("kidx_norm_g", 1), ("kidx_norm_b", 1), ("final_norm_g", 8), ("igate_b", 1), ("fgate_b", 1),
        ("norm_g_2", 8), ("conv_w_2", 40), ("conv_b_2", 10), ("dt_bias_2", 1), ("a_log_2", 1), ("ssd_norm_g_2", 8),
        ("rw_mu_2", 17), ("rw_w0_2", 4), ("rw_a0_2", 4), ("rw_k_k_2", 4), ("rw_k_a_2", 4), ("rw_r_k_2", 4),
        ("rw_ln_g_2", 4), ("rw_ln_b_2", 4), ("final_g_2", 8), ("ssm_a_re", 16), ("ssm_a_im", 16), ("ssm_log_dt", 16),
        ("d_skip_2", 16)]
VEC_AT, VEC_N = vector_columns(VECS)


class Constants:

    def row_picker(self, heads, h):
        return self.ident[0:heads, h:h + 1].to_broadcast([heads, P])

    def vec(self, name, i=0):
        c0, n = VEC_AT[name]
        return self.vectors[:, c0 + i:c0 + i + 1]

    def vecs(self, name):
        c0, n = VEC_AT[name]
        return self.vectors[:, c0:c0 + n]


def setup(nc, ctx, io):
    m = Machine(nc, ctx)
    c = Constants()
    c.vectors = m.take(VEC_N)
    vs = Slot(c.vectors, m.sem("vectors_in"))
    c.landed = vs.fill(m.sp, [(c.vectors, io["vectors"])])
    make_constants(m, c)
    m.weights = [m.slot(f"weights{i}", 8 * BANK) for i in range(2)]
    m.next_weight = 0
    m.silu_tmp = m.take(2, BANK)
    m.silu_free = [None, None]
    m.silu_turn = 0
    for q in (m.act, m.dve, m.pe, m.pool):
        m_wait(q, [c.landed, c.ready] if q is not m.pool else [c.landed])
    return m, c


def m_wait(queue, producers):
    flat = flatten(producers)
    for x in flat:
        if isinstance(x, Step):
            x.needed = True
    queue.items.append((None, flat, Step(queue)))


SCRATCH = [("s5_scratch", (512, T)), ("y_first0", (512, T)), ("y_first1", (512, T)), ("y_first2", (512, T)),
           ("y_second0", (512, T)), ("y_second1", (1024, T)), ("y_second2", (512, T)), ("x_middle", (D, T)), ("h_second", (D, T)),
           ("gates_first", (3 * D, T)), ("gates_second", (3 * D, T))]



MH, MD = 4, 128


def depthwise_conv(m, c, src, dst, i, tiles, wname, bname, ready, free):
    def tap(k):
        return c.vec(wname, k * tiles + i)

    s = m.dve(lambda e: e.tensor_scalar(dst, src[:, 3:3 + T], tap(3), c.vec(bname, i), ALU.mult, ALU.add), ready, free)
    for k in range(3):
        s = m.dve(lambda e, k=k: e.scalar_tensor_tensor(out=dst, in0=src[:, k:k + T], scalar=tap(k), in1=dst,
                                                        op0=ALU.mult, op1=ALU.add), s)
    return s


def log_sigmoid_rows(m, x, tmp, s):
    a = m.act(lambda e: e.activation(tmp, x, ACT.Abs), s)
    a = m.act(lambda e: e.activation(tmp, tmp, ACT.Exp, scale=-1.0), a)
    a = m.act(lambda e: e.activation(tmp, tmp, ACT.Ln, bias=1.0), a)
    s = m.dve(lambda e: e.tensor_scalar(x, x, 0.0, None, ALU.min), a)
    return m.dve(lambda e: e.tensor_tensor(x, x, tmp, ALU.subtract), s)


def mlstm(m, c, io, hT, h_ready, y, fence):
    w_in = io["w_in"]
    Q0 = 2 * 512
    V0 = Q0 + 2 * 512
    I0 = V0 + 512
    Z0 = I0 + 8
    qk = m.take(8, T)
    v1 = m.take(NB, MH, MD + 1)
    weight = m.take(NB * (NB + 1) // 2 * P)
    negM = m.take(T)
    raw = m.take(2, T + 3)
    ig = m.take(T)
    F = m.take(T)
    M = m.take(T)
    hnum = m.take(NB, MD + 1)
    tokg = m.take(2, NB, MH)
    small = m.take(3, NB)
    E = m.take(2, BANK)
    SC = float(MD) ** -0.5

    for j in range(2):
        pad = m.pool(lambda e, j=j: e.memset(raw[:, j, 0:3], 0.0), fence)
    raw_free = [None, None]
    qk_done = {}
    for g in range(2):
        slot, w, landed = load_weights(m, w_in, Q0 + g * BANK, Q0 + (g + 1) * BANK)
        halves = {}

        def evac(i, n, ps, step, g=g, halves=halves):
            t = g * 4 + i
            j = t % 2
            s = m.act(lambda e: e.activation(raw[:, j, 3 + n * BANK:3 + (n + 1) * BANK], ps, ACT.Copy),
                      step, raw_free[j], fence)
            if n == 1:
                cv = depthwise_conv(m, c, raw[:, j, :], qk[:, t, :], t, 8, "qk_conv_w", "qk_conv_b", [s, pad], fence)
                raw_free[j] = cv
                qk_done[t] = m.act(lambda e, t=t: e.activation(qk[:, t, :], qk[:, t, :], ACT.Silu), cv)
            return s

        project_channels(m, hT, h_ready, slot, w, landed, TILES4, evac)

    one = m.pool(lambda e: e.memset(v1[:, :, :, MD:MD + 1], 1.0), fence)
    slot, w, landed = load_weights(m, w_in, V0, V0 + 512)
    v_done = [one]

    def evac_v(blk, ps, step):
        s = m.act(lambda e: e.activation(v1[:, blk, :, 0:MD], ps.rearrange("p (h d) -> p h d", h=MH), ACT.Copy), step, fence)
        v_done.append(s)
        return s

    project_tokens(m, hT, h_ready, slot, w, landed, 0, 512, evac_v)

    slot, w, landed = load_weights(m, w_in, I0, I0 + 8)
    rows = {}

    def evac_g(i, n, ps, step):
        dst = (ig if i == 0 else F)[0:MH, n * BANK:(n + 1) * BANK]
        bias = c.vec("igate_b" if i == 0 else "fgate_b")[0:MH]
        s = m.dve(lambda e: e.tensor_scalar(dst, ps, bias, None, ALU.add), step, fence)
        rows[i] = s
        return s

    project_channels(m, hT, h_ready, slot, w, landed, [(0, 4), (4, 8)], evac_g)
    R = slice(0, MH)
    s = log_sigmoid_rows(m, F[R], M[R], rows[1])
    s = m.dve(lambda e: e.tensor_tensor_scan(F[R], c.zero[R].to_broadcast([MH, T]), F[R], 0.0, ALU.add, ALU.add), s)
    a = m.dve(lambda e: e.tensor_tensor(ig[R], ig[R], F[R], ALU.subtract), s, rows[0])
    s = m.dve(lambda e: e.tensor_tensor_scan(M[R], ig[R], ig[R], 0.0, ALU.max, ALU.max), a)
    mr = m.dve(lambda e: e.tensor_tensor(F[R], F[R], M[R], ALU.add), s)
    nm = m.dve(lambda e: e.tensor_scalar(M[R], M[R], -1.0, None, ALU.mult), mr)
    b = m.bank()
    first = True
    for r, (row, dep) in enumerate(((ig, a), (F, mr))):
        for blk in range(NB):
            o = (r * NB + blk) * MH
            t = m.pe(lambda e, row=row, blk=blk, o=o, b=b: e.transpose(
                b.view[:, o:o + MH], row[R, blk * P:(blk + 1) * P], c.ident[R, 0:MH]), dep, b.readers if first else None)
            first = False
    s = m.dve(lambda e, b=b: e.tensor_copy(tokg[:, 0].rearrange("p b h -> p (b h)"), b.view[:, 0:NB * MH]), t)
    s2 = m.act(lambda e, b=b: e.activation(tokg[:, 1].rearrange("p b h -> p (b h)"), b.view[:, NB * MH:2 * NB * MH],
                                           ACT.Exp, scale=-1.0), t, s)
    b.readers = [s2]
    tok_ready = [s, s2]

    def at(j):
        return sum((NB - i) * P for i in range(j))

    E_free = [None, None]
    turn = 0
    nm_free, w_free, hn_free = None, None, None
    y_done = []
    for h in range(MH):
        for n in range(HALVES):
            b = m.bank()
            s = m.pe(lambda e, b=b, h=h, n=n: e.matmul(b.view, c.row_picker(MH, h), M[R, n * BANK:(n + 1) * BANK],
                                                       start=True, stop=True), nm, b.readers)
            s = m.dve(lambda e, b=b, n=n: e.tensor_copy(negM[:, n * BANK:(n + 1) * BANK], b.view), s, nm_free)
            b.readers = [s]
        neg_ready = s
        wdone = {}
        for j in range(NB):
            for t0 in range(j * P, T, BANK):
                t1 = min(t0 + BANK, T)
                n = t1 - t0
                b = m.bank()
                s = m.pe(lambda e, b=b, h=h, j=j, t0=t0, t1=t1, n=n: e.matmul(
                    b.view[:, 0:n], qk[:, 4 + h, j * P:(j + 1) * P], qk[:, h, t0:t1], start=True, stop=True),
                    qk_done[h], qk_done[4 + h], b.readers)
                k = turn % 2
                turn += 1
                bias = tokg[:, 0, j, h:h + 1]
                diag = t0 == j * P
                deps = [neg_ready, tok_ready]
                if diag:
                    d = m.dve(lambda e, k=k, bias=bias, t0=t0: e.tensor_scalar(
                        E[:, k, 0:P], negM[:, t0:t0 + P], bias, 0.0, ALU.add, ALU.min), deps, E_free[k])
                    x = m.act(lambda e, k=k: e.activation(E[:, k, 0:P], E[:, k, 0:P], ACT.Exp), d)
                    mask = m.pool(lambda e, k=k: e.affine_select(out=E[:, k, 0:P], in_=E[:, k, 0:P], compare_op=ALU.is_ge,
                                                                 fill=0.0, base=0, pattern=[[1, P]],
                                                                 channel_multiplier=-1), x)
                    if n > P:
                        x = m.act(lambda e, k=k, bias=bias, t0=t0, n=n, t1=t1: e.activation(
                            E[:, k, P:n], negM[:, t0 + P:t1], ACT.Exp, bias=bias))
                    x = [x, mask]
                else:
                    x = m.act(lambda e, k=k, bias=bias, t0=t0, n=n, t1=t1: e.activation(
                        E[:, k, 0:n], negM[:, t0:t1], ACT.Exp, bias=bias), deps, E_free[k])
                o = at(j) + t0 - j * P
                s = m.dve(lambda e, b=b, k=k, n=n, o=o: e.scalar_tensor_tensor(
                    out=weight[:, o:o + n], in0=b.view[:, 0:n], scalar=SC, in1=E[:, k, 0:n], op0=ALU.mult, op1=ALU.mult),
                    s, x, w_free)
                b.readers = [s]
                E_free[k] = s
        nm_free = x
        for g in range(0, NB, 3):
            b = m.bank()
            nblk = min(3, NB - g)
            for i in range(nblk):
                for j in range(g + i + 1):
                    o = at(j) + (g + i - j) * P
                    t = m.pe(lambda e, b=b, i=i, j=j, o=o, h=h, g=g: e.matmul(
                        b.view[:, i * (MD + 1):(i + 1) * (MD + 1)], weight[:, o:o + P], v1[:, j, h, :],
                        start=(j == 0), stop=(j == g + i)), s, v_done, b.readers if i == 0 and j == 0 else None)
            cp = m.act(lambda e, b=b, g=g, nblk=nblk: e.activation(
                hnum[:, g:g + nblk, :].rearrange("p b d -> p (b d)"), b.view[:, 0:nblk * (MD + 1)], ACT.Copy), t, hn_free)
            b.readers = [cp]
        w_free = t
        den = hnum[:, :, MD]
        s = m.act(lambda e, den=den: e.activation(small[:, 0, :], den, ACT.Abs), cp)
        s = m.dve(lambda e, h=h: e.tensor_tensor(small[:, 0, :], small[:, 0, :], tokg[:, 1, :, h], ALU.max), s, tok_ready)
        s = m.dve(lambda e: e.reciprocal(small[:, 0, :], small[:, 0, :]), s)
        num = hnum[:, :, 0:MD]
        s = m.dve(lambda e, num=num: e.tensor_tensor(num, num, small[:, 0, :].unsqueeze(2).to_broadcast([P, NB, MD]), ALU.mult), s)
        junk = E[:, 0, 0:P]
        q = [s, E_free]
        for blk in range(NB):
            q = m.act(lambda e, blk=blk, junk=junk: e.activation(junk, hnum[:, blk, 0:MD], ACT.Square,
                                                                accum_out=small[:, 1, blk:blk + 1]), q)
        s = m.dve(lambda e: e.tensor_scalar(small[:, 1, :], small[:, 1, :], 1.0 / MD, EPS, ALU.mult, ALU.add), q)
        s = root_of_inverse(m, small[:, 1, :], s)
        s = m.dve(lambda e, num=num: e.tensor_tensor(num, num, small[:, 1, :].unsqueeze(2).to_broadcast([P, NB, MD]), ALU.mult), s)
        E_free = [s, s]
        for g in range(2):
            b = m.bank()
            for i in range(4):
                t = m.pe(lambda e, b=b, i=i, g=g: e.transpose(b.view[:, i * P:(i + 1) * P], hnum[:, g * 4 + i, 0:MD], c.ident),
                         s, b.readers if i == 0 else None)
            cp = m.act(lambda e, b=b, g=g, h=h: e.activation(y[:, h, g * BANK:(g + 1) * BANK], b.view, ACT.Copy,
                                                             scale=c.vec("mh_norm_g", h)), t, fence)
            b.readers = [cp]
            y_done.append(cp)
        hn_free = t
    return gate_with_silu(m, hT, h_ready, w_in, Z0, y, y_done)



SG, SN, SP_ = 32, 64, 16
SL = 8
SC_ = T // SL
NP_ = SG // 2


def s5_parameters(m, c, io, S):
    par = m.take(24, NP_)
    bmat = m.take(2, NP_, SP_)
    cmat = m.take(2, NP_, SP_)
    bb = m.take(2, NP_, SP_)
    pw = m.take(2, SL + 1, NP_)
    tmp = m.take(2, NP_ * SC_ // 2)
    slot = Slot(bmat, m.sem("ssm_params_in"))
    landed = slot.fill(m.sp, [(bmat, io["ssm_b"].rearrange("p (r j q) -> p r j q", r=2, j=NP_)),
                              (cmat, io["ssm_c"].rearrange("p (r j q) -> p r j q", r=2, j=NP_))])
    dt, mag, ang, k, r, sn, hs, cm1, are, aim, den, fr, fi, am1, zr, zi, m8, u1, u2, u3 = [par[:, i, :] for i in range(20)]
    ar, ai, ldt = c.vecs("ssm_a_re"), c.vecs("ssm_a_im"), c.vecs("ssm_log_dt")
    TT = lambda o, a, b, op, *d: m.dve(lambda e: e.tensor_tensor(o, a, b, op), m.dve.last, *d)
    TS = lambda o, a, s1, s2, o1, o2, *d: m.dve(lambda e: e.tensor_scalar(o, a, s1, s2, o1, o2), m.dve.last, *d)

    def cmul(o_re, o_im, a_re, a_im, b_re, b_im, t1, t2):
        TT(o_re, a_re, b_re, ALU.mult)
        TT(t1, a_im, b_im, ALU.mult)
        TT(o_re, o_re, t1, ALU.subtract)
        TT(o_im, a_re, b_im, ALU.mult)
        TT(t2, a_im, b_re, ALU.mult)
        return TT(o_im, o_im, t2, ALU.add)

    bits = m.take(NP_).bitcast(I32)
    accurate_exp(m, dt, ldt, (u2, u3), bits)
    TT(u1, ar, dt, ALU.mult)
    accurate_exp(m, mag, u1, (u2, u3), bits)
    TT(ang, ai, dt, ALU.mult)
    TS(k, ang, 1.0 / (2 * np.pi), 12582912.0, ALU.mult, ALU.add)
    TS(k, k, 12582912.0, None, ALU.subtract, ALU.bypass)
    two_pi = 2 * np.pi
    p1 = float(np.float32(6.28125))
    p2 = float(np.float32(np.round((two_pi - p1) * 2.0 ** 21) / 2.0 ** 21))
    p3 = float(np.float32(two_pi - p1 - p2))
    src = ang
    for part in (p1, p2, p3):
        m.dve(lambda e, part=part, src=src: e.scalar_tensor_tensor(out=r, in0=k, scalar=-part, in1=src, op0=ALU.mult,
                                                                   op1=ALU.add), m.dve.last)
        src = r
    TS(r, r, 0.5, None, ALU.mult, ALU.bypass)
    TT(k, r, r, ALU.mult)
    polynomial(m, hs, k, [(-1.0) ** n / math.factorial(2 * n + 1) for n in range(8)])
    TT(hs, hs, r, ALU.mult)
    polynomial(m, cm1, k, [(-1.0) ** n / math.factorial(2 * n) for n in range(9)])
    TT(sn, hs, cm1, ALU.mult)
    TS(sn, sn, 2.0, None, ALU.mult, ALU.bypass)
    TT(cm1, hs, hs, ALU.mult)
    TS(cm1, cm1, -2.0, None, ALU.mult, ALU.bypass)
    TT(u1, mag, cm1, ALU.mult)
    TT(are, mag, u1, ALU.add)
    TT(aim, mag, sn, ALU.mult)
    TS(am1, mag, -1.0, None, ALU.add, ALU.bypass)
    TT(am1, am1, u1, ALU.add)
    TT(den, ar, ar, ALU.mult)
    TT(u1, ai, ai, ALU.mult)
    TT(den, den, u1, ALU.add)
    m.dve(lambda e: e.reciprocal(den, den), m.dve.last)
    TT(fr, am1, ar, ALU.mult)
    TT(u1, aim, ai, ALU.mult)
    TT(fr, fr, u1, ALU.add)
    TT(fr, fr, den, ALU.mult)
    TT(fi, aim, ar, ALU.mult)
    TT(u1, am1, ai, ALU.mult)
    TT(fi, fi, u1, ALU.subtract)
    TT(fi, fi, den, ALU.mult)
    wide = lambda v: v.unsqueeze(2).to_broadcast([P, NP_, SP_])
    t1 = tmp[:, 0, 0:NP_ * SP_].rearrange("p (j q) -> p j q", j=NP_)
    t2 = tmp[:, 1, 0:NP_ * SP_].rearrange("p (j q) -> p j q", j=NP_)
    m_wait(m.dve, [landed])
    cmul(bb[:, 0], bb[:, 1], bmat[:, 0], bmat[:, 1], wide(fr), wide(fi), t1, t2)
    m.dve(lambda e: e.memset(pw[:, 0, 0, :], 1.0))
    m.dve(lambda e: e.memset(pw[:, 1, 0, :], 0.0))
    TS(pw[:, 0, 1, :], are, 0.0, None, ALU.add, ALU.bypass)
    TS(pw[:, 1, 1, :], aim, 0.0, None, ALU.add, ALU.bypass)
    n = 1
    while n < SL:
        rows = lambda r_, a, b: pw[:, r_, a:b, :]
        top = lambda r_, n=n: pw[:, r_, n:n + 1, :].to_broadcast([P, n, NP_])
        v1_ = tmp[:, 0, 0:n * NP_].rearrange("p (k j) -> p k j", k=n)
        v2_ = tmp[:, 1, 0:n * NP_].rearrange("p (k j) -> p k j", k=n)
        cmul(rows(0, n + 1, 2 * n + 1), rows(1, n + 1, 2 * n + 1), rows(0, 1, n + 1), rows(1, 1, n + 1), top(0), top(1), v1_, v2_)
        n *= 2
    ca = S.ca
    K9 = SL + 1
    tf = [tmp[:, i, 0:K9 * SP_].rearrange("p (k q) -> p k q", k=K9) for i in range(2)]
    for j in range(NP_):
        sh = [P, K9, SP_]
        cj = lambda r_, j=j: cmat[:, r_, j, :].unsqueeze(1).to_broadcast(sh)
        pj = lambda r_, j=j: pw[:, r_, :, j].unsqueeze(2).to_broadcast(sh)
        x1, x2 = tf
        TT(ca[:, 0, j], cj(0), pj(0), ALU.mult)
        TT(x1, cj(1), pj(1), ALU.mult)
        TT(ca[:, 0, j], ca[:, 0, j], x1, ALU.subtract)
        TT(ca[:, 1, j], cj(0), pj(1), ALU.mult)
        TT(x2, cj(1), pj(0), ALU.mult)
        m.dve(lambda e, j=j, x2=x2: e.scalar_tensor_tensor(out=ca[:, 1, j], in0=ca[:, 1, j], scalar=-1.0, in1=x2,
                                                           op0=ALU.mult, op1=ALU.subtract), m.dve.last)
    ca_done = m.dve.last
    wtmp = m.take(2, NP_, SL, SP_)
    for j in range(NP_):
        sh = [P, SL, SP_]
        bj = lambda r_, j=j: bb[:, r_, j, :].unsqueeze(1).to_broadcast(sh)
        pj = lambda r_, j=j: pw[:, r_, SL - 1::-1, j].unsqueeze(2).to_broadcast(sh)
        x = tf[0][:, 0:SL, :]
        x2 = tf[1][:, 0:SL, :]
        cmul(wtmp[:, 0, j], wtmp[:, 1, j], bj(0), bj(1), pj(0), pj(1), x, x2)
    w_done = m.dve.last
    for r_ in range(2):
        for g in range(4):
            b = m.bank()
            for i in range(4):
                t = m.pe(lambda e, b=b, i=i, g=g, r_=r_: e.transpose(
                    b.view[:, i * P:(i + 1) * P], wtmp[:, r_, g * 4 + i].rearrange("p s q -> p (s q)"), c.ident),
                    w_done, b.readers if i == 0 else None)
            t = m.act(lambda e, b=b, g=g, r_=r_: e.activation(
                S.inject[:, r_, g * 4:(g + 1) * 4, :].rearrange("p j n -> p (j n)"), b.view, ACT.Copy), t)
            b.readers = [t]
    S.inject_done = t
    zero = m.dve(lambda e: e.memset(S.toeplitz, 0.0))
    kern = m.take(8, P)
    kslot = Slot(kern, m.sem("toeplitz_in"))
    kfree = None
    for g8 in range(4):
        for half in range(2):
            b = m.bank()
            for i in range(4):
                j, e0 = g8 * 4 + i, 64 * half
                for r_ in range(2):
                    t = m.pe(lambda e, b=b, i=i, j=j, e0=e0, r_=r_: e.matmul(
                        b.view[0:SP_, i * P:(i + 1) * P], bb[e0:e0 + 64, r_, j, :],
                        ca[e0:e0 + 64, r_, j, 0:SL, :].rearrange("p k q -> p (k q)"), start=(r_ == 0), stop=(r_ == 1)),
                        ca_done, b.readers if i == 0 and r_ == 0 else None)
            t = m.act(lambda e, b=b, half=half: e.activation(
                kern[0:SP_, half:8:2, :], b.view[0:SP_, :].rearrange("p (g n) -> p g n", g=4), ACT.Copy), t, kfree)
            b.readers = [t]
        pieces = [(S.toeplitz[SP_ * s:SP_ * (s + 1), g8 * 8:(g8 + 1) * 8, SP_ * s:P], kern[0:SP_, :, 0:P - SP_ * s])
                  for s in range(SL)]
        kfree = kslot.fill(m.sp, pieces, t, zero)
    S.toeplitz_done = kfree
    TS(u1, cm1, 1.0, None, ALU.add, ALU.bypass)
    cur = (u1, sn)
    for i in range(3):
        nxt = ((zr, zi), (fr, fi))[i % 2]
        cmul(nxt[0], nxt[1], cur[0], cur[1], cur[0], cur[1], u2, u3)
        cur = nxt
    TT(m8, mag, mag, ALU.mult)
    TT(m8, m8, m8, ALU.mult)
    TT(S.decay, m8, m8, ALU.mult)
    rot = S.rotor
    m.dve(lambda e: e.memset(rot[:, 0, :, 0:1], 1.0), m.dve.last)
    m.dve(lambda e: e.memset(rot[:, 1, :, 0:1], 0.0), m.dve.last)
    n = 1
    flip = [(am1, den), (zr, zi)]
    while n < SC_:
        sh = [P, NP_, n]
        zb = [x.unsqueeze(2).to_broadcast(sh) for x in cur]
        y1 = tmp[:, 0, 0:NP_ * n].rearrange("p (j c) -> p j c", j=NP_)
        y2 = tmp[:, 1, 0:NP_ * n].rearrange("p (j c) -> p j c", j=NP_)
        cmul(rot[:, 0, :, n:2 * n], rot[:, 1, :, n:2 * n], rot[:, 0, :, 0:n], rot[:, 1, :, 0:n], zb[0], zb[1], y1, y2)
        n *= 2
        if n < SC_:
            nxt = flip[0]
            flip = flip[::-1]
            if nxt[0] is cur[0]:
                nxt = flip[0]
                flip = flip[::-1]
            cmul(nxt[0], nxt[1], cur[0], cur[1], cur[0], cur[1], u2, u3)
            cur = nxt
    S.ready = m.dve.last


def accurate_exp(m, out, x, work, bits, *ready):
    k, r = work
    D = lambda f, *d: m.dve(f, m.dve.last, *d)
    D(lambda e: e.tensor_scalar(r, x, 88.0, -87.3, ALU.min, ALU.max), *ready)
    D(lambda e: e.tensor_scalar(k, r, 1.0 / float(np.log(2.0)), 12582912.0, ALU.mult, ALU.add))
    D(lambda e: e.tensor_scalar(k, k, 12582912.0, None, ALU.subtract))
    high = 0.693359375
    low = float(np.log(2.0)) - high
    D(lambda e: e.scalar_tensor_tensor(out=r, in0=k, scalar=-high, in1=r, op0=ALU.mult, op1=ALU.add))
    D(lambda e: e.scalar_tensor_tensor(out=r, in0=k, scalar=-low, in1=r, op0=ALU.mult, op1=ALU.add))
    polynomial(m, out, r, [1.0 / float(math.factorial(n)) for n in range(9)])
    D(lambda e: e.tensor_scalar(k, k, 127.0, 8388608.0, ALU.add, ALU.mult))
    D(lambda e: e.tensor_copy(bits, k))
    return D(lambda e: e.tensor_tensor(out, out, bits.bitcast(F32), ALU.mult))


def polynomial(m, out, x, coefficients):
    D = lambda f: m.dve(f, m.dve.last)
    top = coefficients[-1]
    D(lambda e: e.tensor_scalar(out, x, 0.0, top, ALU.mult, ALU.add))
    for a in coefficients[-2::-1]:
        D(lambda e: e.tensor_tensor(out, out, x, ALU.mult))
        D(lambda e, a=a: e.tensor_scalar(out, out, a, None, ALU.add))
    return m.dve.last


class S5State:
    pass


def s5(m, c, io, hT, h_ready, y, fence):
    w_in = io["w_in"]
    S = S5State()
    base = m.top
    S.ca = m.take(2, NP_, SL + 1, SP_)
    S.inject = m.take(2, NP_, P)
    S.toeplitz = m.take(SG, P)
    S.rotor = m.take(2, NP_, SC_)
    S.decay = m.take(NP_)
    mark = m.top
    if fence:
        for q in (m.act, m.dve, m.pool, m.sp):
            m_wait(q, fence)
    s5_parameters(m, c, io, S)
    after_parameters = m.fence()
    m.top = mark
    U = m.take(SG, P)
    state = m.take(2, NP_, SC_)
    tmp = m.take(2, BANK)
    slot, w, landed = load_weights(m, w_in, 0, 512)
    u_done = []

    def evac_u(i, n, ps, step):
        dst = y[:, i, :].rearrange("p (s c) -> p c s", s=SL)[:, n * (SC_ // 2):(n + 1) * (SC_ // 2), :]
        s = m.act(lambda e: e.activation(dst, ps.rearrange("p (c s) -> p c s", s=SL), ACT.Copy), step, fence)
        u_done.append(s)
        return s

    project_channels(m, hT, h_ready, slot, w, landed, TILES4, evac_u)
    by_channel = io["s5_scratch"].rearrange("(i p) t -> p i t", p=P)
    by_chunk = io["s5_scratch"].rearrange("(g q) (s c) -> s q g c", q=SP_, s=SL)
    out_slot = Slot(y, m.sem("u_out"))
    u_out = out_slot.fill(m.sp, [(by_channel, y)], u_done)
    uslot = Slot(U, m.sem("u_in_chunks"))
    moves = [(U[SP_ * s_:SP_ * (s_ + 1), :, :], by_chunk[s_]) for s_ in range(SL)]
    u_in = uslot.fill(m.sp, moves, u_out, after_parameters)
    g_done = []
    tfree = None
    for q in range(4):
        pr = [m.bank() for _ in range(2)]
        for r_ in range(2):
            for i in range(4):
                j = q * 4 + i
                for e_ in range(2):
                    t = m.pe(lambda e, r_=r_, i=i, j=j, e_=e_, b=pr[r_]: e.matmul(
                        b.view[64 * e_:64 * e_ + 64, i * P:(i + 1) * P], S.inject[:, r_, j, 64 * e_:64 * e_ + 64],
                        U[:, 2 * j + e_, :], start=True, stop=True), u_in, S.inject_done,
                        pr[r_].readers if i == 0 and e_ == 0 else None)
        js = slice(q * 4, q * 4 + 4)
        flat = lambda v: v.rearrange("p j c -> p (j c)")
        zre, zim = flat(S.rotor[:, 0, js, :]), flat(S.rotor[:, 1, js, :])
        gre, gim = flat(state[:, 0, js, :]), flat(state[:, 1, js, :])
        D = lambda *a: m.dve(*a)
        s = m.dve(lambda e, b=pr[0], gre=gre, zre=zre: e.tensor_tensor(gre, b.view, zre, ALU.mult), t, after_parameters, S.ready)
        s = m.dve(lambda e, b=pr[1], zim=zim: e.tensor_tensor(tmp[:, 0, :], b.view, zim, ALU.mult), s)
        s = m.dve(lambda e, gre=gre: e.tensor_tensor(gre, gre, tmp[:, 0, :], ALU.add), s)
        s = m.dve(lambda e, b=pr[1], gim=gim, zre=zre: e.tensor_tensor(gim, b.view, zre, ALU.mult), s)
        s = m.dve(lambda e, b=pr[0], zim=zim: e.tensor_tensor(tmp[:, 1, :], b.view, zim, ALU.mult), s)
        pr[0].readers = pr[1].readers = [s]
        s = m.dve(lambda e, gim=gim: e.tensor_tensor(gim, gim, tmp[:, 1, :], ALU.subtract), s)
        for r_ in range(2):
            for i in range(4):
                j = q * 4 + i
                s3 = m.dve(lambda e, r_=r_, j=j: e.tensor_tensor_scan(
                    state[:, r_, j, :], S.decay[:, j:j + 1].to_broadcast([P, SC_]), state[:, r_, j, :], 0.0,
                    ALU.mult, ALU.add), s)
        g_done.append(s3)
    before = S.inject
    full = slice(0, SC_ - 1)
    s = m.dve(lambda e: e.memset(before[:, :, :, 0:1], 0.0), g_done)
    for q in range(4):
        js = slice(q * 4, q * 4 + 4)
        gre, gim = state[:, 0, js, full], state[:, 1, js, full]
        zre, zim = S.rotor[:, 0, js, full], S.rotor[:, 1, js, full]
        bre, bim = before[:, 0, js, 1:SC_], before[:, 1, js, 1:SC_]
        v = [tmp[:, i, :].rearrange("p (j c) -> p j c", j=4)[:, :, full] for i in range(2)]
        s = m.dve(lambda e, a=bre, x=gre, z=zre: e.tensor_tensor(a, x, z, ALU.mult), s, g_done[q])
        s = m.dve(lambda e, a=v[0], x=gim, z=zim: e.tensor_tensor(a, x, z, ALU.mult), s)
        s = m.dve(lambda e, a=bre, x=v[0]: e.tensor_tensor(a, a, x, ALU.subtract), s)
        s = m.dve(lambda e, a=bim, x=gre, z=zim: e.tensor_tensor(a, x, z, ALU.mult), s)
        s = m.dve(lambda e, a=v[1], x=gim, z=zre: e.tensor_tensor(a, x, z, ALU.mult), s)
        s = m.dve(lambda e, a=bim, x=v[1]: e.tensor_tensor(a, a, x, ALU.add), s)
    before_done = s
    outs = []
    for q in range(8):
        b = m.bank()
        for i in range(4):
            g = (q // 2) * 8 + 2 * i + q % 2
            j, e0 = g // 2, 64 * (g % 2)
            o = b.view[:, i * P:(i + 1) * P]
            t = m.pe(lambda e, o=o, g=g: e.matmul(o, S.toeplitz[:, g, :], U[:, g, :], start=True, stop=False),
                     S.toeplitz_done, u_in, b.readers if i == 0 else None)
            for r_ in range(2):
                t = m.pe(lambda e, o=o, r_=r_, j=j, e0=e0: e.matmul(
                    o, S.ca[e0:e0 + 64, r_, j, 1:SL + 1, :].rearrange("p k q -> p (k q)"), before[e0:e0 + 64, r_, j, :],
                    start=False, stop=(r_ == 1)), before_done)
        cp = m.act(lambda e, b=b, q=q: e.activation(U[:, (q // 2) * 8 + q % 2:(q // 2) * 8 + 8:2, :],
                                                    b.view.rearrange("p (g c) -> p g c", g=4), ACT.Copy), t)
        b.readers = [cp]
        outs.append(cp)
    ys = S.rotor.rearrange("p a j c -> p (a j c)").rearrange("p (i t) -> p i t", i=4)
    back = Slot(U, m.sem("s5_out"))
    gone = back.fill(m.sp, [(by_chunk[s_], U[SP_ * s_:SP_ * (s_ + 1), :, :]) for s_ in range(SL)], outs)
    yslot = Slot(ys, m.sem("s5_out_in"))
    y_in = yslot.fill(m.sp, [(ys, by_channel)], gone, before_done)
    gel = []
    for i in range(4):
        s = m.dve(lambda e, i=i: e.scalar_tensor_tensor(out=ys[:, i, :], in0=y[:, i, :], scalar=c.vec("ssm_d", i),
                                                        in1=ys[:, i, :], op0=ALU.mult, op1=ALU.add), y_in)
        gel.append(m.act(lambda e, i=i: e.activation(ys[:, i, :], ys[:, i, :], ACT.Gelu_apprx_tanh), s))
    slot, w, landed = load_weights(m, io["glu_w"], 0, 512, 4)
    y_done = []

    gfree = [None, None]
    turn = [0]

    def evac_glu(i, n, ps, step):
        k = turn[0] % 2
        turn[0] += 1
        a = m.act(lambda e: e.activation(tmp[:, k, :], ps, ACT.Sigmoid, bias=c.vec("glu_b", i)), step, gfree[k], before_done)
        dst = y[:, i, :].rearrange("p (c s) -> p s c", s=SL)[:, n * 4:(n + 1) * 4, :]
        s = m.dve(lambda e: e.tensor_tensor(dst, ys[:, i, n * BANK:(n + 1) * BANK].rearrange("p (s c) -> p s c", s=4),
                                            tmp[:, k, :].rearrange("p (s c) -> p s c", s=4), ALU.mult), a, gel)
        gfree[k] = s
        y_done.append(s)
        return a

    project_channels(m, ys, gel, slot, w, landed, TILES4, evac_glu, kt=4)
    m.top = base
    return gate_with_silu(m, hT, h_ready, w_in, 512, y, y_done)



BH, BD = 8, 64


def stick_breaking(m, c, io, hT, h_ready, y, fence):
    w_in = io["w_in_2"]
    q = m.take(4, T)
    k = m.take(4, T)
    v = m.take(NB, BH, BD)
    z = m.take(2, BANK)
    sp = m.take(2, BANK)
    lg = m.take(2, BANK)
    A = m.take(2, BANK)
    total = m.take(2, BANK)
    done = {}
    for name, dst, c0 in (("k", k, 512), ("q", q, 0)):
        slot, w, landed = load_weights(m, w_in, c0, c0 + 512)

        def evac(i, n, ps, step, name=name, dst=dst):
            s = m.act(lambda e: e.activation(dst[:, i, n * BANK:(n + 1) * BANK], ps, ACT.Copy,
                                             scale=float(BD) ** -0.5 if name == "q" else 1.0), step, fence)
            done[name] = s
            return s

        project_channels(m, hT, h_ready, slot, w, landed, TILES4, evac)
    slot, w, landed = load_weights(m, w_in, 1024, 1536)

    def evac_v(blk, ps, step):
        s = m.act(lambda e: e.activation(v[:, blk].rearrange("p h d -> p (h d)"), ps, ACT.Copy), step, fence)
        done["v"] = s
        return s

    project_tokens(m, hT, h_ready, slot, w, landed, 0, 512, evac_v)
    if fence:
        m_wait(m.dve, fence)
    y_done = []
    free = {n: [None, None] for n in ("z", "sp", "lg", "A")}
    turn = 0
    for b in range(NB):
        for par in range(2):
            out = m.held[par]
            running = None
            e0 = BD * par
            for j in range(b, -1, -1):
                i = turn % 2
                turn += 1
                zb = m.bank()
                for g in range(4):
                    s = m.pe(lambda e, zb=zb, g=g, b=b, j=j, e0=e0: e.matmul(
                        zb.view[:, g * P:(g + 1) * P], k[e0:e0 + BD, g, j * P:(j + 1) * P],
                        q[e0:e0 + BD, g, b * P:(b + 1) * P], start=True, stop=True),
                        done["k"], done["q"], zb.readers if g == 0 else None)
                a = m.act(lambda e, zb=zb, i=i: e.activation(lg[:, i, :], zb.view, ACT.Abs), s, free["lg"][i])
                zc = m.dve(lambda e, zb=zb, i=i: e.tensor_copy(z[:, i, :], zb.view), a, free["z"][i])
                zb.readers = [zc]
                a = m.act(lambda e, i=i: e.activation(lg[:, i, :], lg[:, i, :], ACT.Exp, scale=-1.0), a)
                a = m.act(lambda e, i=i: e.activation(lg[:, i, :], lg[:, i, :], ACT.Ln, bias=1.0), a)
                s = m.dve(lambda e, i=i: e.scalar_tensor_tensor(out=sp[:, i, :], in0=z[:, i, :], scalar=0.0,
                                                                in1=lg[:, i, :], op0=ALU.max, op1=ALU.add),
                          a, zc, free["sp"][i])
                free["lg"][i] = s
                if j == b:
                    s = m.pool(lambda e, i=i: e.affine_select(out=sp[:, i, :], in_=sp[:, i, :], compare_op=ALU.is_gt,
                                                              fill=0.0, base=0, pattern=[[0, 4], [1, P]],
                                                              channel_multiplier=-1), s)
                rb = m.bank()
                r = m.pe(lambda e, rb=rb, i=i, j=j, b=b: e.matmul(rb.view, c.tail_t, sp[:, i, :], start=True, stop=(j == b)),
                         s, rb.readers)
                if j < b:
                    r = m.pe(lambda e, rb=rb, par=par: e.matmul(rb.view, c.ones, total[:, par, :], start=False, stop=True),
                             running)
                if j == b:
                    running = m.pool(lambda e, i=i, par=par: e.tensor_copy(total[:, par, :], sp[:, i, :]), s, out.readers)
                else:
                    running = m.pool(lambda e, i=i, par=par: e.tensor_tensor(total[:, par, :], total[:, par, :], sp[:, i, :],
                                                                             ALU.add), s, running, r)
                free["sp"][i] = [running, r]
                s = m.dve(lambda e, rb=rb, i=i: e.tensor_tensor(A[:, i, :], z[:, i, :], rb.view, ALU.subtract), r, free["A"][i])
                rb.readers = [s]
                free["z"][i] = s
                s = m.act(lambda e, i=i: e.activation(A[:, i, :], A[:, i, :], ACT.Exp), s)
                if j == b:
                    s = m.pool(lambda e, i=i: e.affine_select(out=A[:, i, :], in_=A[:, i, :], compare_op=ALU.is_gt,
                                                              fill=0.0, base=0, pattern=[[0, 4], [1, P]],
                                                              channel_multiplier=-1), s)
                for g in range(4):
                    pv = m.pe(lambda e, out=out, g=g, i=i, j=j, b=b, par=par: e.matmul(
                        out.view[64 * par:64 * par + 64, g * P:(g + 1) * P], v[:, j, 2 * g + par, :],
                        A[:, i, g * P:(g + 1) * P], start=(j == b and g == 0), stop=(j == 0), skip_group_check=True),
                        s, done["v"], out.readers if j == b and g == 0 else None)
                free["A"][i] = pv
            s = m.act(lambda e, out=out, b=b, par=par: e.activation(
                y[64 * par:64 * par + 64, :, b * P:(b + 1) * P],
                out.view[64 * par:64 * par + 64, :].rearrange("p (g t) -> p g t", g=4), ACT.Copy), pv, fence)
            out.readers = [s]
            y_done.append(s)
    return gate_with_silu(m, hT, h_ready, w_in, 1536, y, y_done)



DH, DP, DN, DG = 16, 64, 64, 2
HG = DH // DG


def ssd(m, c, io, hT, h_ready, y, fence):
    w_in = io["w_in_2"]
    Z0 = 2048
    X0 = Z0 + 1024
    DT0 = X0 + 1280
    bT = m.take(T)
    cT = m.take(T)
    xtok = m.take(NB, 1024)
    btok = m.take(NB, P)
    raw = m.take(2, T + 3)
    dtr = m.take(T)
    csr = m.take(T)
    tmpr = m.take(T)
    tokg = m.take(4, NB, DH)
    elast = m.take(NB, DH)
    csb = m.take(2, 4, P)
    E = m.take(2, BANK)
    cb = m.take(DG, P)
    W = m.take(2, BANK)
    xdt = m.take(1024)
    xw = m.take(1024)
    state = m.take(BANK)
    yc = m.take(1024)
    stat = m.take(2, NB)
    if fence:
        for qq in (m.act, m.dve, m.pool):
            m_wait(qq, fence)
    for j in range(2):
        pad = m.pool(lambda e, j=j: e.memset(raw[:, j, 0:3], 0.0))
    raw_free = [None, None]
    done = {}
    xfree = [None, None]
    order = [(0, 4), (4, 8), (8, 10)]
    work = m.take(2, T)
    wfree = [None, None]
    for t0, t1 in order:
        slot, w, landed = load_weights(m, w_in, X0 + t0 * P, X0 + t1 * P)

        def evac(i, n, ps, step, t0=t0):
            t = t0 + i
            j = t % 2
            s = m.act(lambda e: e.activation(raw[:, j, 3 + n * BANK:3 + (n + 1) * BANK], ps, ACT.Copy), step, raw_free[j])
            if n == 1:
                dst = work[:, j, :] if t < 8 else (bT if t == 8 else cT)
                cv = depthwise_conv(m, c, raw[:, j, :], dst, t, 10, "conv_w_2", "conv_b_2", [s, pad], wfree[j] if t < 8 else None)
                raw_free[j] = cv
                a = m.act(lambda e, dst=dst: e.activation(dst, dst, ACT.Silu), cv)
                done[t] = a
                if t <= 8:
                    for g in range(2):
                        b = m.bank()
                        for i4 in range(4):
                            blk = g * 4 + i4
                            p = m.pe(lambda e, b=b, i4=i4, blk=blk, dst=dst: e.transpose(
                                b.view[:, i4 * P:(i4 + 1) * P], dst[:, blk * P:(blk + 1) * P], c.ident), a,
                                b.readers if i4 == 0 else None)
                        o = (xtok[:, g * 4:(g + 1) * 4, t * P:(t + 1) * P] if t < 8 else btok[:, g * 4:(g + 1) * 4, :])
                        p2 = m.dve(lambda e, b=b, o=o: e.tensor_copy(o, b.view.rearrange("p (k n) -> p k n", k=4)), p)
                        b.readers = [p2]
                    wfree[j] = p
                    done["tok", t] = p2
            return s

        project_channels(m, hT, h_ready, slot, w, landed, [(i * P, (i + 1) * P) for i in range(t1 - t0)], evac)
    slot, w, landed = load_weights(m, w_in, DT0, DT0 + DH)
    R = slice(0, DH)
    rd = []

    def evac_dt(i, n, ps, step):
        s = m.dve(lambda e: e.tensor_scalar(dtr[R, n * BANK:(n + 1) * BANK], ps, c.vec("dt_bias_2")[R], None, ALU.add), step)
        rd.append(s)
        return s

    project_channels(m, hT, h_ready, slot, w, landed, [(0, DH)], evac_dt)
    a = m.act(lambda e: e.activation(tmpr[R], dtr[R], ACT.Abs), rd)
    a = m.act(lambda e: e.activation(tmpr[R], tmpr[R], ACT.Exp, scale=-1.0), a)
    a = m.act(lambda e: e.activation(tmpr[R], tmpr[R], ACT.Ln, bias=1.0), a)
    dt_done = m.dve(lambda e: e.scalar_tensor_tensor(out=dtr[R], in0=dtr[R], scalar=0.0, in1=tmpr[R], op0=ALU.max,
                                                     op1=ALU.add), a)
    ah = m.take(1)
    a = m.act(lambda e: e.activation(ah[R], c.vec("a_log_2")[R], ACT.Exp))
    s = m.dve(lambda e: e.tensor_scalar(tmpr[R], dtr[R], ah[R], -1.0, ALU.mult, ALU.mult), a, dt_done)
    for blk in range(NB):
        s2 = m.dve(lambda e, blk=blk: e.tensor_tensor_scan(
            csr[R, blk * P:(blk + 1) * P], c.zero[R].to_broadcast([DH, P]), tmpr[R, blk * P:(blk + 1) * P], 0.0,
            ALU.add, ALU.add), s)
    cs_done = s2
    b = m.bank()
    for r, row in enumerate((dtr, csr)):
        for blk in range(NB):
            o = (r * NB + blk) * DH
            t = m.pe(lambda e, row=row, blk=blk, o=o, b=b: e.transpose(
                b.view[:, o:o + DH], row[R, blk * P:(blk + 1) * P], c.ident[R, 0:DH]), cs_done,
                b.readers if o == 0 else None)
    t0 = m.dve(lambda e, b=b: e.tensor_copy(tokg[:, 0:2].rearrange("p a k h -> p (a k h)"), b.view[:, 0:2 * NB * DH]), t)
    b.readers = [t0]
    b = m.bank()
    lastrow = m.take(P)
    s = m.pool(lambda e: e.memset(lastrow, 0.0))
    s = m.pool(lambda e: e.affine_select(out=lastrow, in_=lastrow, compare_op=ALU.not_equal, fill=1.0, base=-(P - 1),
                                         pattern=[[0, P]], channel_multiplier=1), s)
    flat = lambda i: tokg[:, i].rearrange("p k h -> p (k h)")
    t = m.pe(lambda e, b=b: e.matmul(b.view[:, 0:NB * DH], lastrow, flat(1), start=True, stop=True), s, t0, b.readers)
    s = m.act(lambda e, b=b: e.activation(elast.rearrange("p k h -> p (k h)"), b.view[:, 0:NB * DH], ACT.Exp), t)
    s1 = m.dve(lambda e, b=b: e.tensor_tensor(flat(3), b.view[:, 0:NB * DH], flat(1), ALU.subtract), t, s)
    b.readers = [s1]
    s = m.act(lambda e: e.activation(flat(3), flat(3), ACT.Exp), s1)
    s = m.act(lambda e: e.activation(flat(2), flat(1), ACT.Exp), t0)
    tok_ready = [t0, s]

    zslot = []
    zw = [load_weights(m, w_in, Z0 + g * BANK, Z0 + (g + 1) * BANK) for g in range(2)]
    Efree, Wfree, csfree = [None, None], [None, None], [None, None]
    cbfree = None
    turn = 0
    state_done = m.dve(lambda e: e.memset(state, 0.0))
    state_read = None
    xdt_free = xw_free = yc_free = None
    y_done = []
    heads = lambda v: v.rearrange("p (h d) -> p h d", h=v.shape[1] // DP)
    for ck in range(NB):
        cols = slice(ck * P, (ck + 1) * P)
        cbs = []
        for g in range(DG):
            b = m.bank()
            s = m.pe(lambda e, b=b, g=g, cols=cols: e.matmul(b.view[:, 0:P], bT[g * DN:(g + 1) * DN, cols],
                                                             cT[g * DN:(g + 1) * DN, cols], start=True, stop=True),
                     done[8], done[9], b.readers)
            s = m.dve(lambda e, b=b, g=g: e.tensor_tensor(cb[:, g, :], b.view[:, 0:P], c.upper, ALU.mult), s, cbfree)
            b.readers = [s]
            cbs.append(s)
        wide = lambda i, ck=ck: tokg[:, i, ck, :].unsqueeze(2).to_broadcast([P, DH, DP])
        xd = m.dve(lambda e, ck=ck, wide=wide: e.tensor_tensor(heads(xdt), heads(xtok[:, ck, :]), wide(0), ALU.mult),
                   tok_ready, xdt_free, [done["tok", t] for t in range(9)])
        xs = m.pool(lambda e, wide=wide: e.tensor_tensor(heads(xw), heads(xdt), wide(3), ALU.mult), xd, xw_free, tok_ready)
        yd = [m.held[0], m.held[1]]
        for h4 in range(4):
            k = turn % 2
            turn += 1
            b = m.bank()
            for i in range(4):
                h = h4 * 4 + i
                s = m.pe(lambda e, b=b, i=i, h=h, cols=cols: e.matmul(b.view[:, i * P:(i + 1) * P], c.row_picker(DH, h),
                                                                      csr[R, cols], start=True, stop=True),
                         cs_done, b.readers if i == 0 else None)
            bcs = tokg[:, 1, ck, h4 * 4:h4 * 4 + 4].unsqueeze(2).to_broadcast([P, 4, P])
            s = m.dve(lambda e, b=b, k=k, bcs=bcs: e.tensor_tensor(E[:, k, :].rearrange("p (h l) -> p h l", h=4),
                                                                   b.view.rearrange("p (h l) -> p h l", h=4), bcs,
                                                                   ALU.subtract), s, tok_ready, Efree[k])
            b.readers = [s]
            s = m.dve(lambda e, k=k: e.tensor_scalar(E[:, k, :], E[:, k, :], 0.0, None, ALU.min), s)
            s = m.act(lambda e, k=k: e.activation(E[:, k, :], E[:, k, :], ACT.Exp), s)
            g = h4 // 2
            s = m.pool(lambda e, k=k, g=g: e.tensor_tensor(W[:, k, :].rearrange("p (h l) -> p h l", h=4),
                                                          E[:, k, :].rearrange("p (h l) -> p h l", h=4),
                                                          cb[:, g, :].unsqueeze(1).to_broadcast([P, 4, P]), ALU.mult),
                      s, cbs, Wfree[k])
            Efree[k] = s
            for i in range(4):
                h = h4 * 4 + i
                o = yd[g].view[:, (h % HG) * DP:(h % HG + 1) * DP]
                t = m.pe(lambda e, o=o, k=k, i=i, h=h: e.matmul(o, W[:, k, i * P:(i + 1) * P], xdt[:, h * DP:(h + 1) * DP],
                                                               start=True, stop=True), s, xd,
                         yd[g].readers if h % HG == 0 else None)
            Wfree[k] = t
        cbfree = s
        diag_done = t
        s = state_done
        parts = []
        for g in range(DG):
            gs = slice(g * DN, (g + 1) * DN)
            b = m.bank()
            t = m.pe(lambda e, b=b, gs=gs, cols=cols: e.matmul(b.view, cT[gs, cols], state[gs, :], start=True, stop=True),
                     state_done, b.readers)
            if g == 1:
                state_read = t
            o = yc[:, g * BANK:(g + 1) * BANK]
            wg = tokg[:, 2, ck, g * HG:(g + 1) * HG].unsqueeze(2).to_broadcast([P, HG, DP])
            s = m.dve(lambda e, b=b, o=o, wg=wg: e.tensor_tensor(heads(o), heads(b.view), wg, ALU.mult), t, tok_ready, yc_free)
            b.readers = [s]
            s = m.dve(lambda e, o=o, g=g: e.tensor_tensor(o, o, yd[g].view, ALU.add), s, diag_done)
            yd[g].readers = [s]
            parts.append(s)
        xdt_free = [diag_done, xs]
        dsk = c.vecs("d_skip_2").unsqueeze(2).to_broadcast([P, DH, DP])
        s = m.dve(lambda e, dsk=dsk, ck=ck: e.tensor_tensor(heads(xtok[:, ck, :]), heads(xtok[:, ck, :]), dsk, ALU.mult), xd)
        s = m.dve(lambda e, ck=ck: e.tensor_tensor(yc, yc, xtok[:, ck, :], ALU.add), s, parts)
        for g in range(2):
            zs, zwv, zl = zw[g]
            b = m.bank()
            for k in range(KD):
                t = m.pe(lambda e, b=b, k=k, cols=cols, zwv=zwv: e.matmul(b.view, hT[:, k, cols], zwv[:, k, :],
                                                                          start=(k == 0), stop=(k == KD - 1)),
                         zl, h_ready, b.readers if k == 0 else None)
            zs.readers = [t]
            j = m.silu_turn % 2
            m.silu_turn += 1
            a = m.act(lambda e, b=b, j=j: e.activation(m.silu_tmp[:, j, :], b.view, ACT.Silu), t, m.silu_free[j])
            b.readers = [a]
            s = m.dve(lambda e, g=g, j=j: e.tensor_tensor(yc[:, g * BANK:(g + 1) * BANK], yc[:, g * BANK:(g + 1) * BANK],
                                                          m.silu_tmp[:, j, :], ALU.mult), a, s)
            m.silu_free[j] = s
        q = m.act(lambda e, ck=ck: e.activation(xdt, yc, ACT.Square, accum_out=stat[:, 0, ck:ck + 1]), s, xdt_free)
        xdt_free = [xdt_free, q]
        s = m.dve(lambda e, ck=ck: e.tensor_scalar(stat[:, 0, ck:ck + 1], stat[:, 0, ck:ck + 1], 1.0 / D, EPS, ALU.mult, ALU.add), q)
        s = root_of_inverse(m, stat[:, 0, ck:ck + 1], s)
        s = m.dve(lambda e, ck=ck: e.tensor_scalar(yc, yc, stat[:, 0, ck:ck + 1], None, ALU.mult), s)
        for g in range(2):
            b = m.bank()
            for i in range(4):
                t = m.pe(lambda e, b=b, i=i, g=g: e.transpose(b.view[:, i * P:(i + 1) * P],
                                                             yc[:, (g * 4 + i) * P:(g * 4 + i + 1) * P], c.ident), s,
                         b.readers if i == 0 else None)
            gn = c.vecs("ssd_norm_g_2")[:, g * 4:g * 4 + 4].unsqueeze(2).to_broadcast([P, 4, P])
            s2 = m.dve(lambda e, b=b, g=g, gn=gn, cols=cols: e.tensor_tensor(
                y[:, g * 4:g * 4 + 4, cols], b.view.rearrange("p (i t) -> p i t", i=4), gn, ALU.mult), t)
            b.readers = [s2]
            y_done.append(s2)
        yc_free = t
        if ck < NB - 1:
            for g in range(DG):
                gs = slice(g * DN, (g + 1) * DN)
                b = m.bank()
                t = m.pe(lambda e, b=b, gs=gs, ck=ck, g=g: e.matmul(b.view[gs, :], btok[:, ck, gs],
                                                                    xw[:, g * BANK:(g + 1) * BANK], start=True, stop=True),
                         xs, done["tok", 8], b.readers)
                el = elast[gs, ck, g * HG:(g + 1) * HG].unsqueeze(2).to_broadcast([DN, HG, DP])
                st = state[gs, :]
                s = m.dve(lambda e, st=st, el=el: e.tensor_tensor(heads(st), heads(st), el, ALU.mult), state_read, state_done)
                s = m.dve(lambda e, st=st, b=b, gs=gs: e.tensor_tensor(st, st, b.view[gs, :], ALU.add), s, t)
                b.readers = [s]
            state_done = s
            xw_free = t
    return y_done



RH, RD = 8, 64
RL = 64
RC = T // RL


def rwkv(m, c, io, hT, h_ready, y, fence, h_saved):
    w_in = io["w_in_2"]
    C0 = 2048 + 2320
    base = m.top
    alpha = m.take(4, T)
    beta = m.take(4, T)
    kappa = m.take(4, T)
    rho = m.take(4, T)
    plast = m.take(4, RC)
    mask4 = m.take(4, P)
    maskA = m.take(P)
    level = m.take(6, P)
    levelT0 = m.take(P)
    mark = m.top
    vT = m.take(4, T)
    raw = m.take(2, T + 1)
    lo = m.take(T)
    room = hT.rearrange("p k t -> p (k t)")
    lw, cs, aT, t1, t2 = [room[:, T * i:T * (i + 1)] for i in range(5)]
    wup = m.take(512)
    reset = m.take(T)
    zero_ps = None
    if fence:
        for q_ in (m.act, m.dve, m.pool, m.sp):
            m_wait(q_, fence)
    pool = m.pool

    def tri(view, strict, transposed, size, n):
        s = pool(lambda e: e.memset(view, 1.0))
        s = pool(lambda e: e.affine_select(out=view, in_=view, compare_op=ALU.is_gt if strict else ALU.is_ge, fill=0.0,
                                           base=0, pattern=[[1 if transposed else -1, P]],
                                           channel_multiplier=-1 if transposed else 1), s)
        return same_block(view, size, s)

    def same_block(view, size, s):
        nb = P // size
        v = view.rearrange("p (b i) -> p b i", b=nb)
        s = pool(lambda e: e.affine_select(out=v, in_=v, compare_op=ALU.is_ge, fill=0.0, base=0,
                                           pattern=[[-size, nb], [0, size]], channel_multiplier=1), s)
        return pool(lambda e: e.affine_select(out=v, in_=v, compare_op=ALU.is_ge, fill=0.0, base=size - 1,
                                              pattern=[[size, nb], [0, size]], channel_multiplier=-1), s)

    for i, strict in enumerate((True, False, True, False)):
        tri(mask4[:, i, :], strict, True, RL, P)
    s = tri(maskA, True, False, RL, P)
    for k_ in range(6):
        s = tri(level[:, k_, :], True, False, 2 ** (k_ + 1), P)
    tri(levelT0, True, True, 2, P)
    sub = None
    for k_ in range(5, 0, -1):
        sub = m.dve(lambda e, k_=k_: e.tensor_tensor(level[:, k_, :], level[:, k_, :], level[:, k_ - 1, :], ALU.subtract),
                    pool.last, sub)
    masks = [pool.last, sub]
    s = m.dve(lambda e: e.memset(reset, 1.0))
    reset_ready = m.dve(lambda e: e.memset(reset.rearrange("p (c l) -> p c l", c=RC)[:, :, 0:1], 0.0), s)
    for j in range(2):
        pad = m.dve(lambda e, j=j: e.memset(raw[:, j, 0:1], 0.0))
    wslot = Slot(wup, m.sem("rw_up_in"))
    wl = wslot.fill(m.sp, [(wup[0:64, :], io["rw_w_up_2"]), (wup[64:128, :], io["rw_a_up_2"])])

    raw_free = [None, None]
    turn = [0]

    def mix_tiles(c0, n, dst_of):
        slot, w, landed = load_weights(m, w_in, C0 + c0 * P, C0 + (c0 + n) * P)
        done = {}

        def evac(i, h, ps, step):
            j = (turn[0] // 2) % 2
            turn[0] += 1
            s = m.act(lambda e: e.activation(raw[:, j, 1 + h * BANK:1 + (h + 1) * BANK], ps, ACT.Copy), step, raw_free[j])
            if h == 1:
                dst, free = dst_of(i)
                mu = c.vec("rw_mu_2", c0 + i)
                d = m.dve(lambda e: e.tensor_tensor(dst, raw[:, j, 0:T], raw[:, j, 1:T + 1], ALU.subtract), s, pad, free)
                d = m.dve(lambda e: e.scalar_tensor_tensor(out=dst, in0=dst, scalar=mu, in1=raw[:, j, 1:T + 1],
                                                           op0=ALU.mult, op1=ALU.add), d)
                raw_free[j] = d
                done[i] = d
            return s

        project_channels(m, hT, h_ready, slot, w, landed, [(i * P, (i + 1) * P) for i in range(n)], evac)
        return done

    d = mix_tiles(16, 1, lambda i: (lo, None))
    lo_done = m.act(lambda e: e.activation(lo[0:64, :], lo[0:64, :], ACT.Tanh), d[0])
    r_done = mix_tiles(0, 4, lambda i: (rho[:, i, :], None))
    k_done = mix_tiles(4, 4, lambda i: (kappa[:, i, :], None))
    v_done = mix_tiles(8, 4, lambda i: (vT[:, i, :], None))

    h_free = [m.pe.last, h_saved]
    m_wait(m.act, h_free)
    m_wait(m.dve, h_free)

    def block_sum(src, ready, use):
        for n in range(HALVES):
            b = m.bank()
            s = m.pe(lambda e, b=b, n=n: e.matmul(b.view, c.pair_ones, src[:, n * BANK:(n + 1) * BANK], start=True, stop=True),
                     ready, c.pair_ready, b.readers)
            b.readers = [use(slice(n * BANK, (n + 1) * BANK), b.view, s)]

    g = [None] * 8
    ready = {}
    prev = []
    DV = lambda f, *d: m.dve(f, m.dve.last, *d)
    for i in range(4):
        rr, kk_, vv = rho[:, i, :], kappa[:, i, :], vT[:, i, :]
        al, be = alpha[:, i, :], beta[:, i, :]
        for n in range(HALVES):
            cols = slice(n * BANK, (n + 1) * BANK)
            for base_, dst, bias in ((0, lw, "rw_w0_2"), (64, aT, "rw_a0_2")):
                b = m.bank()
                s = m.pe(lambda e, b=b, base_=base_, i=i, cols=cols: e.matmul(
                    b.view, wup[base_:base_ + 64, i * P:(i + 1) * P], lo[base_:base_ + 64, cols], start=True, stop=True),
                    wl, lo_done, d[0], b.readers)
                s = m.act(lambda e, b=b, dst=dst, bias=bias, i=i, cols=cols: e.activation(
                    dst[:, cols], b.view, ACT.Sigmoid, bias=c.vec(bias, i)), s, prev)
                b.readers = [s]
        DV(lambda e: e.tensor_scalar(lw, lw, -float(np.exp(-0.5)), None, ALU.mult), s)
        DV(lambda e: e.tensor_tensor_scan(cs, reset, lw, 0.0, ALU.mult, ALU.add), reset_ready)
        DV(lambda e, kk_=kk_, i=i: e.tensor_scalar(t1, kk_, c.vec("rw_k_k_2", i), None, ALU.mult), k_done[i])
        s = DV(lambda e: e.tensor_tensor(t2, t1, t1, ALU.mult))

        def norm(cols, ps, step):
            return m.act(lambda e, cols=cols: e.activation(t2[:, cols], ps, ACT.Sqrt), step)

        block_sum(t2, s, norm)
        s = m.act.last
        DV(lambda e: e.tensor_scalar(t2, t2, 1e-12, None, ALU.max), s)
        DV(lambda e: e.reciprocal(t2, t2))
        DV(lambda e: e.tensor_tensor(t1, t1, t2, ALU.mult))
        DV(lambda e, be=be: e.tensor_tensor(be, t1, aT, ALU.mult))
        DV(lambda e, i=i: e.tensor_scalar(aT, aT, -1.0, c.vec("rw_k_a_2", i), ALU.add, ALU.mult))
        DV(lambda e, kk_=kk_: e.scalar_tensor_tensor(out=kk_, in0=aT, scalar=1.0, in1=kk_, op0=ALU.add, op1=ALU.mult))
        DV(lambda e, rr=rr, kk_=kk_: e.tensor_tensor(t2, rr, kk_, ALU.mult), r_done[i])
        s = DV(lambda e, i=i: e.tensor_scalar(t2, t2, c.vec("rw_r_k_2", i), None, ALU.mult))

        def bonus(cols, ps, step, i=i):
            return m.dve(lambda e, cols=cols: e.tensor_tensor(y[:, i, cols], ps, vT[:, i, cols], ALU.mult), step, v_done[i])

        block_sum(t2, s, bonus)
        DV(lambda e: e.tensor_tensor(lw, cs, lw, ALU.subtract))
        s = m.act(lambda e: e.activation(lw, lw, ACT.Exp), m.dve.last)
        DV(lambda e, al=al: e.tensor_tensor(al, t1, lw, ALU.mult), s)
        s = m.act(lambda e: e.activation(aT, cs, ACT.Exp), m.dve.last)
        DV(lambda e, rr=rr: e.tensor_tensor(rr, rr, aT, ALU.mult), s)
        DV(lambda e, i=i: e.tensor_copy(plast[:, i, :], aT.rearrange("p (c l) -> p c l", c=RC)[:, :, RL - 1]))
        s = m.act(lambda e: e.activation(t2, cs, ACT.Exp, scale=-1.0), m.dve.last)
        DV(lambda e, be=be: e.tensor_tensor(be, be, t2, ALU.mult), s)
        DV(lambda e, kk_=kk_: e.tensor_tensor(kk_, kk_, t2, ALU.mult))
        prev = [m.dve.last]
    prepared = [m.dve.last, m.act.last, m.pe.last, h_saved]

    m.top = mark + 4 * T
    tokv = m.take(4, P)
    toka = m.take(4, P)
    tokb = m.take(4, P)
    tokk = m.take(4, P)
    scaled = m.take(2, 4, P)
    gram = room[:, 0:4096].rearrange("p (h g t) -> p h g t", h=RH, g=4)
    A, X, Z, Wm = [room[:, 4096 + 1024 * i:5120 + 1024 * i].rearrange("p (h t) -> p h t", h=RH) for i in range(4)]
    rhs = Wm
    U = X
    E = m.take(4, P)
    Gt = m.take(2, 4, RD)
    S = m.take(4, RD)
    Y = m.take(4, P)
    sq = E
    mean = toka
    s_state = m.dve(lambda e: e.memset(S, 0.0), prepared)
    m_wait(m.act, prepared)
    last_of_block = None
    quads = [range(0, 4), range(4, 8)]
    y_done = []
    for blk in range(NB):
        cols = slice(blk * P, (blk + 1) * P)
        chunk0 = 2 * blk
        pl = plast[:, :, 2 * blk:2 * blk + 2].unsqueeze(3).to_broadcast([P, 4, 2, RL])
        spl = []
        for r_, src in ((0, beta), (1, kappa)):
            for cc in range(2):
                plc = plast[:, :, 2 * blk + cc].unsqueeze(2).to_broadcast([P, 4, RL])
                ccols = slice(blk * P + cc * RL, blk * P + (cc + 1) * RL)
                s = m.dve(lambda e, r_=r_, src=src, plc=plc, cc=cc, ccols=ccols: e.tensor_tensor(
                    scaled[:, r_, :, cc * RL:(cc + 1) * RL], src[:, :, ccols], plc, ALU.mult), last_of_block)
            spl.append(s)
        tk = {}
        for dst, src, dep in ((tokv, vT[:, :, cols], None), (toka, alpha[:, :, cols], None),
                              (tokb, scaled[:, 0], spl[0]), (tokk, scaled[:, 1], spl[1])):
            b = m.bank()
            for i in range(4):
                t = m.pe(lambda e, b=b, i=i, src=src: e.transpose(b.view[:, i * P:(i + 1) * P], src[:, i, :], c.ident),
                         dep, prepared, b.readers if i == 0 else None)
            t = m.act(lambda e, b=b, dst=dst: e.activation(dst.rearrange("p i n -> p (i n)"), b.view, ACT.Copy), t, last_of_block)
            b.readers = [t]
        tok_done = t
        grams = []
        for h in range(RH):
            i, e0 = h // 2, RD * (h % 2)
            es = slice(e0, e0 + RD)
            b = m.bank()
            for r_, lhs in ((0, beta), (1, kappa)):
                for q_, rh in ((0, alpha), (1, rho)):
                    t = m.pe(lambda e, b=b, i=i, es=es, lhs=lhs, rh=rh, r_=r_, q_=q_, cols=cols: e.matmul(
                        b.view[:, (2 * r_ + q_) * P:(2 * r_ + q_ + 1) * P], lhs[es, i, cols], rh[es, i, cols],
                        start=True, stop=True), prepared, b.readers if r_ + q_ == 0 else None)
            s = m.dve(lambda e, b=b, h=h: e.tensor_tensor(gram[:, h], b.view.rearrange("p (g t) -> p g t", g=4), mask4,
                                                          ALU.mult), t, masks, last_of_block)
            b.readers = [s]
            grams.append(s)
        for par in range(2):
            b = m.bank()
            for i in range(4):
                es = slice(RD * par, RD * par + RD)
                t = m.pe(lambda e, b=b, i=i, es=es, cols=cols: e.matmul(b.view[:, i * P:(i + 1) * P], alpha[es, i, cols],
                                                            beta[es, i, cols], start=True, stop=True),
                         prepared, b.readers if i == 0 else None)
            s = m.dve(lambda e, b=b, par=par: e.tensor_tensor(
                A[:, par:RH:2, :], b.view.rearrange("p (h s) -> p h s", h=4),
                maskA.unsqueeze(1).to_broadcast([P, 4, P]), ALU.mult), t, masks, last_of_block)
            b.readers = [s]
        wide = lambda v, n=RH: v.unsqueeze(1).to_broadcast([P, n, P])
        idw = wide(c.ident)
        s = m.dve(lambda e: e.tensor_tensor(X, A, wide(level[:, 0, :]), ALU.mult), s, last_of_block)
        sx = m.dve(lambda e: e.tensor_tensor(X, idw, X, ALU.subtract), s)
        s = m.dve(lambda e: e.tensor_tensor(Z, gram[:, :, 0, :], wide(levelT0), ALU.mult), grams)
        sz = m.dve(lambda e: e.tensor_tensor(Z, idw, Z, ALU.subtract), s)
        xd, zd = [sx, sx], [sz, sz]
        for k_ in range(1, 6):
            for qi, quad in enumerate(quads):
                hs = slice(4 * qi, 4 * qi + 4)
                b = m.bank()
                for i, h in enumerate(quad):
                    t = m.pe(lambda e, b=b, i=i, h=h: e.matmul(b.view[:, i * P:(i + 1) * P], gram[:, h, 0, :], X[:, h, :],
                                                              start=True, stop=True), xd[qi], grams,
                             b.readers if i == 0 else None)
                w_ = m.dve(lambda e, b=b, hs=hs, k_=k_: e.tensor_tensor(
                    Wm[:, hs, :], b.view.rearrange("p (h s) -> p h s", h=4), wide(level[:, k_, :], 4), ALU.mult), t)
                b.readers = [w_]
                if k_ < 5:
                    b = m.bank()
                    for i, h in enumerate(quad):
                        t = m.pe(lambda e, b=b, i=i, h=h: e.matmul(b.view[:, i * P:(i + 1) * P], Z[:, h, :], Wm[:, h, :],
                                                                  start=True, stop=True), w_, zd[qi],
                                 b.readers if i == 0 else None)
                    xd[qi] = m.dve(lambda e, b=b, hs=hs: e.tensor_tensor(
                        X[:, hs, :], X[:, hs, :], b.view.rearrange("p (h s) -> p h s", h=4), ALU.subtract), t)
                    b.readers = [xd[qi]]
                b = m.bank()
                for i, h in enumerate(quad):
                    t = m.pe(lambda e, b=b, i=i, h=h: e.matmul(b.view[:, i * P:(i + 1) * P], Wm[:, h, :], Z[:, h, :],
                                                              start=True, stop=True), w_, zd[qi],
                             b.readers if i == 0 else None)
                zd[qi] = m.dve(lambda e, b=b, hs=hs: e.tensor_tensor(
                    Z[:, hs, :], Z[:, hs, :], b.view.rearrange("p (h s) -> p h s", h=4), ALU.subtract), t)
                b.readers = [zd[qi]]
        b = m.bank()
        for h in range(RH):
            t = m.pe(lambda e, b=b, h=h: e.matmul(b.view[:, h * RD:(h + 1) * RD], gram[:, h, 2, :],
                                                  tokv[:, h // 2, RD * (h % 2):RD * (h % 2) + RD], start=True, stop=True),
                     grams, tok_done, b.readers if h == 0 else None)
        s1 = m.act(lambda e, b=b: e.activation(rhs[:, :, RD:P], b.view.rearrange("p (h d) -> p h d", h=RH), ACT.Copy), t,
                   zd)
        b.readers = [s1]
        s2 = m.act(lambda e: e.activation(rhs[:, :, 0:RD], toka.rearrange("p i (e d) -> p (i e) d", e=2), ACT.Copy), tok_done,
                   zd)
        ud = []
        for qi, quad in enumerate(quads):
            b = m.bank()
            for i, h in enumerate(quad):
                t = m.pe(lambda e, b=b, i=i, h=h: e.matmul(b.view[:, i * P:(i + 1) * P], Z[:, h, :], rhs[:, h, :],
                                                          start=True, stop=True), zd[qi], s1, s2,
                         b.readers if i == 0 else None)
            s = m.act(lambda e, b=b, qi=qi: e.activation(U[:, 4 * qi:4 * qi + 4, :].rearrange("p h n -> p (h n)"), b.view,
                                                         ACT.Copy, scale=-1.0), t, last_of_block)
            b.readers = [s]
            ud.append(s)
        b = m.bank()
        for h in range(RH):
            i, e0 = h // 2, RD * (h % 2)
            t = m.pe(lambda e, b=b, h=h, i=i, e0=e0: e.matmul(b.view[e0:e0 + RD, i * P:(i + 1) * P], U[:, h, 0:RD],
                                                              gram[:, h, 1, :], start=True, stop=True), ud, grams,
                     b.readers if h == 0 else None)
        e_done = m.dve(lambda e, b=b, cols=cols: e.tensor_tensor(E, b.view.rearrange("p (i t) -> p i t", i=4), rho[:, :, cols],
                                                      ALU.add), t, last_of_block)
        b.readers = [e_done]
        gd = []
        for cc in range(2):
            rs = slice(cc * RL, (cc + 1) * RL)
            b = m.bank()
            for h in range(RH):
                i, e0 = h // 2, RD * (h % 2)
                t = m.pe(lambda e, b=b, h=h, i=i, e0=e0, rs=rs: e.matmul(
                    b.view[e0:e0 + RD, i * RD:(i + 1) * RD], U[rs, h, 0:RD], tokb[rs, i, e0:e0 + RD], start=True, stop=True),
                    ud, tok_done, b.readers if h == 0 else None)
            for i in range(4):
                s = m.dve(lambda e, b=b, i=i, cc=cc, chunk0=chunk0: e.scalar_tensor_tensor(
                    out=Gt[:, cc, i, :], in0=c.stacked_ident, scalar=plast[:, i, chunk0 + cc:chunk0 + cc + 1],
                    in1=b.view[:, i * RD:(i + 1) * RD], op0=ALU.mult, op1=ALU.add), t, last_of_block, c.stacked_ready)
            b.readers = [s]
            gd.append(s)
        yb = m.bank()
        for h in range(RH):
            i, e0 = h // 2, RD * (h % 2)
            o = yb.view[e0:e0 + RD, i * P:(i + 1) * P]
            m.pe(lambda e, o=o, h=h: e.matmul(o, U[:, h, RD:P], gram[:, h, 1, :], start=True, stop=False,
                                              skip_group_check=True), ud, grams, yb.readers if h == 0 else None)
            t = m.pe(lambda e, o=o, h=h, i=i, e0=e0: e.matmul(o, tokv[:, i, e0:e0 + RD], gram[:, h, 3, :], start=False,
                                                              stop=True, skip_group_check=True), tok_done)
        y1 = m.act(lambda e, yb=yb: e.activation(Y.rearrange("p i t -> p (i t)"), yb.view, ACT.Copy), t, last_of_block)
        yb.readers = [y1]
        for cc in range(2):
            rs = slice(cc * RL, (cc + 1) * RL)
            for par in range(2):
                es = slice(RD * par, RD * par + RD)
                b2 = m.bank()
                for i in range(4):
                    t = m.pe(lambda e, b2=b2, es=es, i=i, cc=cc: e.matmul(
                        b2.view[es, i * RL:(i + 1) * RL], S[es, i, :], E[es, i, cc * RL:(cc + 1) * RL],
                        start=True, stop=True), s_state, e_done, b2.readers if i == 0 else None)
                s = m.dve(lambda e, b2=b2, es=es, cc=cc: e.tensor_tensor(
                    Y[es, :, cc * RL:(cc + 1) * RL], Y[es, :, cc * RL:(cc + 1) * RL],
                    b2.view[es, 0:4 * RL].rearrange("p (i t) -> p i t", i=4), ALU.add), t, y1)
                b2.readers = [s]
            read_state = t
            hb = m.bank()
            for h in range(RH):
                i, e0 = h // 2, RD * (h % 2)
                o = hb.view[e0:e0 + RD, i * RD:(i + 1) * RD]
                m.pe(lambda e, o=o, h=h, i=i, e0=e0, rs=rs: e.matmul(o, tokb[rs, i, e0:e0 + RD], U[rs, h, RD:P], start=True,
                                                                    stop=False, skip_group_check=True),
                     hb.readers if h == 0 else None)
                t = m.pe(lambda e, o=o, h=h, i=i, e0=e0, rs=rs: e.matmul(o, tokk[rs, i, e0:e0 + RD], tokv[rs, i, e0:e0 + RD],
                                                                        start=False, stop=True, skip_group_check=True))
            hs_done = t
            gb = [m.bank(), m.bank()]
            for par in range(2):
                es = slice(RD * par, RD * par + RD)
                for i in range(4):
                    t = m.pe(lambda e, b=gb[par], es=es, i=i, cc=cc: e.matmul(
                        b.view[es, i * RD:(i + 1) * RD], Gt[es, cc, i, :], S[es, i, :], start=True, stop=True),
                        s_state, gd[cc], gb[par].readers if i == 0 else None)
            s = m.dve(lambda e, hb=hb: e.tensor_copy(S, hb.view[:, 0:4 * RD].rearrange("p (i d) -> p i d", i=4)), t, hs_done)
            hb.readers = [s]
            for par in range(2):
                es = slice(RD * par, RD * par + RD)
                s2 = m.dve(lambda e, b=gb[par], es=es: e.tensor_tensor(
                    S[es], S[es], b.view[es, 0:4 * RD].rearrange("p (i d) -> p i d", i=4), ALU.add), s)
                gb[par].readers = [s2]
            s_state = s2
        flatY = Y.rearrange("p i t -> p (i t)")
        flat = lambda v: v.rearrange("p i t -> p (i t)")
        yd = m.dve.last
        b = m.bank()
        t = m.pe(lambda e, b=b: e.matmul(b.view, c.pair_ones, flat(Y), start=True, stop=True), yd, b.readers)
        s = m.dve(lambda e, b=b: e.scalar_tensor_tensor(out=flat(Y), in0=b.view, scalar=-1.0 / RD, in1=flat(Y), op0=ALU.mult,
                                                        op1=ALU.add), t)
        b.readers = [s]
        s = m.act(lambda e: e.activation(flat(sq), flat(Y), ACT.Square), s)
        b = m.bank()
        t = m.pe(lambda e, b=b: e.matmul(b.view, c.pair_ones, flat(sq), start=True, stop=True), s, b.readers)
        s = m.dve(lambda e, b=b: e.tensor_scalar(flat(mean), b.view, 1.0 / RD, 64e-5, ALU.mult, ALU.add), t)
        b.readers = [s]
        s = root_of_inverse(m, flat(mean), s)
        s = m.dve(lambda e: e.tensor_tensor(Y, Y, mean, ALU.mult), s)
        for i in range(4):
            s = m.dve(lambda e, i=i: e.tensor_scalar(Y[:, i, :], Y[:, i, :], c.vec("rw_ln_g_2", i), c.vec("rw_ln_b_2", i),
                                                     ALU.mult, ALU.add), m.dve.last)
        s = m.dve(lambda e, cols=cols: e.tensor_tensor(y[:, :, cols], y[:, :, cols], Y, ALU.add), s)
        y_done.append(s)
        last_of_block = [m.pe.last, m.dve.last, m.act.last]
    m.top = base
    raw = m.take(2, T + 1)
    gt = m.take(2, T)
    after = m.fence()
    m_wait(m.act, after)
    m_wait(m.dve, after)
    m.h_slot.readers = after
    h_ready = m.h_back = m.h_slot.fill(m.sp, [(hT, io["h_second"].rearrange("(k p) t -> p k t", p=P))])
    for j in range(2):
        pad = m.dve(lambda e, j=j: e.memset(raw[:, j, 0:1], 0.0))
    slot, w, landed = load_weights(m, w_in, C0 + 12 * P, C0 + 16 * P)
    raw_free = [None, None]
    out = []

    def evac(i, h, ps, step):
        j = i % 2
        s = m.act(lambda e: e.activation(raw[:, j, 1 + h * BANK:1 + (h + 1) * BANK], ps, ACT.Copy), step, raw_free[j])
        if h == 1:
            mu = c.vec("rw_mu_2", 12 + i)
            d = m.dve(lambda e: e.tensor_tensor(gt[:, j, :], raw[:, j, 0:T], raw[:, j, 1:T + 1], ALU.subtract), s, pad)
            d = m.dve(lambda e: e.scalar_tensor_tensor(out=gt[:, j, :], in0=gt[:, j, :], scalar=mu, in1=raw[:, j, 1:T + 1],
                                                       op0=ALU.mult, op1=ALU.add), d)
            a = m.act(lambda e: e.activation(gt[:, j, :], gt[:, j, :], ACT.Silu), d)
            d = m.dve(lambda e: e.tensor_tensor(y[:, i, :], y[:, i, :], gt[:, j, :], ALU.mult), a)
            raw_free[j] = d
            out.append(d)
        return s

    project_channels(m, hT, h_ready, slot, w, landed, TILES4, evac)
    m.top = base
    return out



def channels(dram):
    return dram.rearrange("(k p) t -> p k t", p=P)


def normalize(m, c, x, ready, gains, out):
    base = m.top
    squares = m.take(2, T)
    rows = m.take(T)
    fence = m.fence()
    m_wait(m.act, fence)
    m_wait(m.dve, fence)
    r = rms_rows(m, c, x, ready, squares, rows)
    done = []
    for k in range(KD):
        done.append(m.dve(lambda e, k=k: e.scalar_tensor_tensor(
            out=out[:, k, :], in0=x[:, k, :], scalar=c.vec(gains, k), in1=rows, op0=ALU.mult, op1=ALU.mult), r, ready(k)))
    m.top = base
    return done


def merge(m, c, io, hT, h_ready, w_in, gate0, branches, w_out, residual, out_space):
    base = m.top
    fence = m.fence()
    mg = Merge(m, c)
    m_wait(m.dve, fence)
    m_wait(m.act, fence)
    for i, (y_dram, stored, kt, w_b) in enumerate(branches):
        y = m.take(kt, T)
        slot = Slot(y, m.sem(f"y_back{gate0}_{i}"))
        y_in = slot.fill(m.sp, [(y, channels(y_dram))], stored, fence)
        mg.add(m, hT, h_ready, w_in, gate0 + i * D, w_b, y, y_in, kt)
    merged_ready = [mg.written[d, n] for d in range(KD) for n in range(HALVES)]
    res = m.take(2, T)
    rslot = [Slot(res[:, i, :], m.sem(f"residual{gate0}_{i}")) for i in range(2)]
    hfree = mg.last
    done = {}
    for half in range(2):
        slot, w, landed = load_weights(m, w_out, half * BANK, (half + 1) * BANK)
        arrived = {}

        def evac(i, n, ps, step, half=half, arrived=arrived):
            d = half * 4 + i
            j = d % 2
            if n == 0:
                arrived[i] = rslot[j].fill(m.sp, [(rslot[j].view, channels(residual)[:, d, :])], fence)
            cols = slice(n * BANK, (n + 1) * BANK)
            s = m.dve(lambda e: e.tensor_tensor(out_space[:, d, cols], ps, rslot[j].view[:, cols], ALU.add), step,
                      arrived[i], hfree)
            if n == 1:
                rslot[j].readers = [s]
                done[d] = s
            return s

        project_channels(m, mg.merged, merged_ready, slot, w, landed, TILES4, evac)
    m.top = base
    return done


def both_blocks(nc, ctx, io):
    m, c = setup(nc, ctx, io)
    h = m.take(KD, T)
    m.h_slot = Slot(h, m.sem("h_in"))
    x_in = m.h_slot.fill(m.sp, [(h, channels(io["xT"]))])
    h_ready = normalize(m, c, h, lambda k: x_in, "norm_g", h)
    mixers = m.top

    def run_mixer(mixer, kt, dram, *more):
        m.top = mixers
        fence = m.fence()
        y = m.take(kt, T)
        slot = Slot(y, m.sem("out_" + mixer.__name__))
        for q in (m.act, m.dve, m.pool):
            m_wait(q, [fence, run_mixer.stored])
        last = mixer(m, c, io, h, h_ready, y, [fence, run_mixer.stored], *more)
        run_mixer.stored = slot.fill(m.sp, [(channels(dram), y)], last, m.fence())
        m.top = mixers
        return run_mixer.stored

    run_mixer.stored = None
    ys = [run_mixer(f, 4, io[f"y_first{i}"]) for i, f in enumerate((s5, mlstm, dsa))]
    x1 = merge(m, c, io, h, h_ready, io["w_in"], 4176, [(io[f"y_first{i}"], ys[i], 4, io[f"w_branch{i}"]) for i in range(3)],
               io["w_out"], io["xT"], h)
    x1 = normalize(m, c, h, lambda k: x1[k], "final_norm_g", h)
    m.h_slot.readers = []
    kept = m.h_slot.fill(m.sp, [(channels(io["x_middle"]), h)], x1)
    m_wait(m.dve, [kept])
    h_ready = normalize(m, c, h, lambda k: x1[k], "norm_g_2", h)
    h_kept = m.h_slot.fill(m.sp, [(channels(io["h_second"]), h)], h_ready)
    zs = [run_mixer(stick_breaking, 4, io["y_second0"]), run_mixer(ssd, 8, io["y_second1"])]
    zs.append(run_mixer(rwkv, 4, io["y_second2"], h_kept))
    out = merge(m, c, io, h, h_ready + [m.h_back], io["w_in_2"], 9616 - 3072,
                [(io["y_second0"], zs[0], 4, io["w_out_sb_2"]), (io["y_second1"], zs[1], 8, io["w_out_ssd_2"]),
                 (io["y_second2"], zs[2], 4, io["w_out_rw_2"])], io["w_o_2"], io["x_middle"], h)
    out = normalize(m, c, h, lambda k: out[k], "final_g_2", h)
    slot = Slot(h, m.sem("result_out"))
    m_wait(m.sp, [slot.fill(m.sp, [(channels(io["result"]), h)], out)])
    m.play()
    return m



def channel_columns(a):
    return np.ascontiguousarray(a.reshape(-1, P).T)


def pack_vectors(x):
    v = np.zeros((P, VEC_N), np.float32)

    def put(name, a):
        c0, n = VEC_AT[name]
        assert a.shape[1] == n, name
        v[0:a.shape[0], c0:c0 + n] = a

    for name in ("norm_g", "ssm_d", "glu_b", "qk_conv_b", "mh_norm_g", "q_norm_g", "norm_g_2", "conv_b_2",
                 "ssd_norm_g_2", "rw_mu_2", "rw_w0_2", "rw_a0_2", "rw_k_k_2", "rw_k_a_2", "rw_r_k_2", "rw_ln_g_2",
                 "rw_ln_b_2", "final_norm_g", "final_g_2"):
        put(name, channel_columns(x[name].reshape(-1)))
    for name in ("qk_conv_w", "conv_w_2"):
        taps = x[name][0]
        put(name, np.concatenate([channel_columns(taps[k]) for k in range(4)], axis=1))
    for name in ("kidx_norm_g", "kidx_norm_b"):
        put(name, np.concatenate([x[name].reshape(-1, 1)] * 2, axis=0))
    for name in ("igate_b", "fgate_b", "dt_bias_2", "a_log_2"):
        put(name, x[name].reshape(-1, 1))
    put("d_skip_2", np.repeat(x["d_skip_2"].reshape(1, 16), P, axis=0))
    put("ssm_a_re", channel_columns(x["ssm_a_re"].reshape(-1)))
    put("ssm_a_im", channel_columns(x["ssm_a_im"].reshape(-1)))
    put("ssm_log_dt", channel_columns(np.repeat(x["ssm_log_dt"].reshape(-1), 64)))
    return v


def lay_out(x):
    arrays = {"xT": np.ascontiguousarray(x["x"][0].T), "vectors": pack_vectors(x)}
    arrays["ssm_b"] = np.ascontiguousarray(np.stack(
        [x[n][0].reshape(16, P, 16).transpose(1, 0, 2) for n in ("ssm_b_re", "ssm_b_im")], axis=1).reshape(P, -1))
    arrays["ssm_c"] = np.ascontiguousarray(np.stack(
        [x[n][0].transpose(0, 2, 1).reshape(16, P, 16).transpose(1, 0, 2) for n in ("ssm_c_re", "ssm_c_im")],
        axis=1).reshape(P, -1))
    for name in ("w_in", "w_out", "glu_w", "w_uq", "w_qidx", "w_in_2", "w_out_sb_2", "w_out_ssd_2", "w_out_rw_2",
                 "w_o_2", "rw_w_up_2", "rw_a_up_2"):
        arrays[name] = np.ascontiguousarray(x[name][0])
    for i in range(3):
        arrays[f"w_branch{i}"] = np.ascontiguousarray(x["w_branch"][0, i])
    return arrays


def kernel(**inputs):
    import concourse.bacc as bacc
    from concourse.bass_utils import run_bass_kernel_spmd

    nc = bacc.Bacc("TRN2", target_bir_lowering=False, num_devices=1)
    arrays = lay_out({name: np.asarray(a) for name, a in inputs.items()})
    io = {name: nc.dram_tensor(f"in_{name}", a.shape, F32, kind="ExternalInput").ap() for name, a in arrays.items()}
    for name, shape in SCRATCH:
        io[name] = nc.dram_tensor(name, shape, F32, kind="Internal").ap()
    io["result"] = nc.dram_tensor("result", (D, T), F32, kind="ExternalOutput").ap()
    with ExitStack() as ctx:
        both_blocks(nc, ctx, io)
    done = run_bass_kernel_spmd(nc, [{f"in_{name}": a for name, a in arrays.items()}], core_ids=[0])
    return np.ascontiguousarray(done.results[0]["result"].T).reshape(1, T, D)
```

```python
import math
from contextlib import ExitStack

import numpy as np

import concourse.bass as bass
from concourse import mybir

F32 = mybir.dt.float32
BF16 = mybir.dt.bfloat16
I32 = mybir.dt.int32
ALU = mybir.AluOpType
ACT = mybir.ActivationFunctionType
AX = mybir.AxisListType

P = 128
BANK = 512
D = 1024
T = 1024
KD = D // P
NB = T // P
HALVES = T // BANK
EPS = 1e-6
TAKEN = -3.0e38
FUTURE = -1.0e38
DROP = -1.0e30


class Step:
    __slots__ = ("queue", "needed", "count")

    def __init__(self, queue):
        self.queue, self.needed, self.count = queue, False, None


class Landed:
    __slots__ = ("sem", "value")

    def __init__(self, sem, value):
        self.sem, self.value = sem, value


def flatten(producers):
    flat = []
    for x in producers:
        if isinstance(x, (list, tuple)):
            flat.extend(flatten(x))
        elif x is not None:
            flat.append(x)
    return flat


class Queue:

    def __init__(self, engine, sem):
        self.engine, self.sem, self.items, self.last = engine, sem, [], None

    def __call__(self, emit, *producers):
        flat = flatten(producers)
        for x in flat:
            if isinstance(x, Step):
                x.needed = True
        step = Step(self)
        self.items.append((emit, flat, step))
        self.last = step
        return step

    def number(self):
        n = 0
        for _, _, step in self.items:
            if step.needed:
                n += 1
                step.count = n

    def play(self):
        reached = {}
        for emit, producers, step in self.items:
            wanted = {}
            for x in producers:
                sem, value = (x.queue.sem, x.count) if isinstance(x, Step) else (x.sem, x.value)
                wanted[sem.name] = (sem, max(value, wanted.get(sem.name, (sem, 0))[1]))
            for name, (sem, value) in wanted.items():
                if value > reached.get(name, 0):
                    self.engine.wait_ge(sem, value)
                    reached[name] = value
            if emit is None:
                continue
            done = emit(self.engine)
            if step.needed:
                done.then_inc(self.sem, 1)


class Slot:

    def __init__(self, view, sem):
        self.view, self.sem, self.filled, self.readers = view, sem, 0, []

    def fill(self, queue, pieces, *producers):
        waits = [self.readers, list(producers)]
        for out, src in pieces:
            self.filled += 16
            last = queue.last
            queue(lambda e, out=out, src=src: e.dma_start(out, src).then_inc(self.sem, 16), *waits)
            queue.last = last
            waits = []
        self.readers = []
        self.landed = Landed(self.sem, self.filled)
        return self.landed


class Bank:

    def __init__(self, view):
        self.view, self.readers = view, []


class Machine:

    def __init__(self, nc, ctx):
        self.nc, self.ctx = nc, ctx
        self.pe = Queue(nc.tensor, self.sem("pe_done"))
        self.act = Queue(nc.scalar, self.sem("act_done"))
        self.dve = Queue(nc.vector, self.sem("dve_done"))
        self.pool = Queue(nc.gpsimd, self.sem("pool_done"))
        self.sp = Queue(nc.sync, self.sem("sp_done"))
        self.banks = [Bank(ctx.enter_context(nc.psum_tensor(f"bank{i}", [P, BANK], F32))[:, :]) for i in range(8)]
        self.next_bank = 0
        self.ring = list(range(5))
        self.held = self.banks[6:8]
        self.arena = ctx.enter_context(nc.sbuf_tensor("arena", [P, 53200], F32))
        self.top = 0
        self.peak = 0

    def sem(self, name):
        return self.ctx.enter_context(self.nc.semaphore(name))

    def take(self, *shape):
        n = int(np.prod(shape))
        view = self.arena[:, self.top:self.top + n]
        self.top += n
        self.peak = max(self.peak, self.top)
        assert self.top <= 53200, self.top
        if len(shape) == 2:
            view = view.rearrange("p (a b) -> p a b", a=shape[0])
        elif len(shape) == 3:
            view = view.rearrange("p (a b c) -> p a b c", a=shape[0], b=shape[1])
        elif len(shape) == 4:
            view = view.rearrange("p (a b c d) -> p a b c d", a=shape[0], b=shape[1], c=shape[2])
        return view

    def take_pair(self, *shape):
        n = int(np.prod(shape))
        assert n % 2 == 0
        view = self.take(n).bitcast(BF16)
        if len(shape) == 1:
            return view.rearrange("p (s a) -> p s a", s=2)
        return view.rearrange("p (s a b) -> p s a b", s=2, a=shape[0])

    def slot(self, name, *shape):
        return Slot(self.take(*shape), self.sem(name))

    def bank(self):
        b = self.banks[self.ring[self.next_bank % len(self.ring)]]
        self.next_bank += 1
        return b

    def fence(self):
        return [q.last for q in (self.pe, self.act, self.dve, self.pool) if q.last is not None]

    def play(self):
        for q in (self.pe, self.act, self.dve, self.pool, self.sp):
            q.number()
        for q in (self.pe, self.act, self.dve, self.pool, self.sp):
            q.play()





def make_constants(m, c):
    c.ident = m.take(P)
    c.ones = m.take(P)
    c.zero = m.take(1)
    c.upper = m.take(P)
    c.tail_t = m.take(P)
    c.pair_ones = m.take(P)
    pool = m.pool

    def fill(view, value):
        return pool(lambda e: e.memset(view, value))

    def keep(view, cmp, pattern, base, channel, value, after):
        return pool(lambda e: e.affine_select(out=view, in_=view, compare_op=cmp, fill=value, base=base,
                                              pattern=pattern, channel_multiplier=channel), after)

    s = fill(c.ident, 0.0)
    c.ident_ready = keep(c.ident, ALU.not_equal, [[-1, P]], 0, 1, 1.0, s)
    fill(c.zero, 0.0)
    s = fill(c.upper, 1.0)
    keep(c.upper, ALU.is_ge, [[1, P]], 0, -1, 0.0, s)
    s = fill(c.tail_t, 1.0)
    keep(c.tail_t, ALU.is_ge, [[-1, P]], 0, 1, 0.0, s)
    s = m.dve(lambda e: e.memset(c.pair_ones, 0.0))
    m.dve(lambda e: e.memset(c.pair_ones[0:64, 0:64], 1.0), s)
    c.pair_ready = m.dve(lambda e: e.memset(c.pair_ones[64:128, 64:128], 1.0), s)
    c.stacked_ident = m.take(64)
    s = fill(c.stacked_ident, 0.0)
    s = keep(c.stacked_ident, ALU.not_equal, [[-1, 64]], 0, 1, 1.0, s)
    c.stacked_ready = keep(c.stacked_ident, ALU.not_equal, [[-1, 64]], -64, 1, 1.0, s)
    c.ready = fill(c.ones, 1.0)


def root_of_inverse(m, view, *ready):
    s = m.dve(lambda e: e.reciprocal(view, view), *ready)
    return m.act(lambda e: e.activation(view, view, ACT.Sqrt), s)


def rms_rows(m, c, src, ready, square_tmp, out):
    banks = [m.bank() for _ in range(HALVES)]
    free = [None, None]
    step = None
    for k in range(KD):
        sq = m.act(lambda e, k=k: e.activation(square_tmp[:, k % 2, :], src[:, k, :], ACT.Square),
                   ready(k), free[k % 2])
        for n in range(HALVES):
            cols = slice(n * BANK, (n + 1) * BANK)
            step = m.pe(lambda e, k=k, n=n, cols=cols: e.matmul(banks[n].view, c.ones, square_tmp[:, k % 2, cols],
                                                                start=(k == 0), stop=(k == KD - 1)),
                        sq, c.ready, banks[n].readers if k == 0 else None)
        free[k % 2] = step
    for n in range(HALVES):
        cols = slice(n * BANK, (n + 1) * BANK)
        s = m.dve(lambda e, n=n, cols=cols: e.tensor_scalar(out[:, cols], banks[n].view, 1.0 / D, EPS,
                                                            ALU.mult, ALU.add), step)
        banks[n].readers = [s]
    return root_of_inverse(m, out, s)


def split(m, src, pair, ready, free=None, low=None):
    hi = m.act(lambda e: e.activation(pair[0], src, ACT.Copy), ready, free)
    return [hi, (low or m.pool)(lambda e: e.tensor_tensor(pair[1], src, pair[0], ALU.subtract), hi)]


PRODUCTS = ((0, 0), (0, 1), (1, 0))
GROUP = 256
AHEAD = 2


class Weights:

    def __init__(self, m, name, group, slots, stages, ahead):
        self.m, self.group, self.ahead = m, group, ahead
        start = m.top
        self.pairs = [m.take_pair(KD * group) for _ in range(slots)]
        self.readers = [None] * slots
        self.stages = [Slot(m.take(KD * group // 2), m.sem(f"{name}_stage{i}")) for i in range(stages)]
        self.room = m.arena[:, start:m.top]
        self.plan, self.loaded, self.used = [], {}, 0
        self.pieces, self.sent, self.turned = [], 0, 0

    def extend(self, dram, c0, c1, kt=KD):
        for c in range(c0, c1, self.group):
            n = min(c + self.group, c1) - c
            self.plan.append((dram, c, c + n, kt))
            half = max(1, kt // 2)
            source = dram.rearrange("(k p) n -> p k n", p=P)
            self.pieces += [(source[:, k0:k0 + half, c:c + n], k0, half, n) for k0 in range(0, kt, half)]

    def give_back(self, steps):
        self.readers = [steps] * len(self.readers)
        for st in self.stages:
            st.readers = steps

    def stage(self, i):
        src, k0, half, n = self.pieces[i]
        st = self.stages[i % len(self.stages)]
        return st, st.view[:, 0:half * n].rearrange("p (k n) -> p k n", k=half)

    def send(self):
        while self.sent < min(self.turned + len(self.stages), len(self.pieces)):
            st, room = self.stage(self.sent)
            st.fill(self.m.sp, [(room, self.pieces[self.sent][0])])
            self.sent += 1

    def load(self, i):
        dram, c0, c1, kt = self.plan[i]
        j = i % len(self.pairs)
        view = self.pairs[j][:, :, 0:kt * (c1 - c0)].rearrange("p s (k n) -> p s k n", k=kt)
        ready = []
        while len(ready) < 2 * kt // max(1, kt // 2):
            self.send()
            st, room = self.stage(self.turned)
            _, k0, half, n = self.pieces[self.turned]
            done = split(self.m, room, [view[:, s, k0:k0 + half, :] for s in range(2)], st.landed, self.readers[j])
            st.readers = done
            ready += done
            self.turned += 1
            self.send()
        self.loaded[i] = (view, ready)

    def prepare(self):
        for k in range(self.used, min(self.used + self.ahead, len(self.plan))):
            if k not in self.loaded:
                self.load(k)

    def take(self, dram, c0, c1):
        i = self.used
        assert self.plan[i][0] is dram and self.plan[i][1:3] == (c0, c1), (self.plan[i][1:3], c0, c1)
        for k in range(i, min(i + 1 + self.ahead, len(self.plan))):
            if k not in self.loaded:
                self.load(k)
        self.used += 1
        view, ready = self.loaded[i]
        j = i % len(self.pairs)

        def read_by(step):
            self.readers[j] = step
        return view, ready, read_by


def product(m, out, left, right, kt, ready, readers):
    step = None
    n = 0
    ready = flatten([ready])
    whole = [x for x in ready if not callable(x)]
    tiles = [x for x in ready if callable(x)]
    for k in range(kt):
        waits = [x(k) for x in tiles]
        for a, b in PRODUCTS:
            step = m.pe(lambda e, l=left(a, k), r=right(b, k), n=n: e.matmul(out, l, r, start=(n == 0),
                                                                             stop=(n == 3 * kt - 1)),
                        [whole, waits, readers] if n == 0 else waits)
            waits = []
            n += 1
    return step


def project_channels(m, src, ready, dram, c0, c1, evacuate, kt=KD):
    for g0 in range(c0, c1, GROUP):
        g1 = min(g0 + GROUP, c1)
        w, landed, read_by = m.weights.take(dram, g0, g1)
        for t0 in range(g0, g1, P):
            t1 = min(t0 + P, g1)
            for n in range(HALVES):
                b = m.bank()
                cols = slice(n * BANK, (n + 1) * BANK)
                step = product(m, b.view[0:t1 - t0, :], lambda a, k, t0=t0, t1=t1: w[:, a, k, t0 - g0:t1 - g0],
                               lambda s, k, cols=cols: src[:, s, k, cols], kt, [landed, ready], b.readers)
                read_by(step)
                b.readers = [evacuate((t0 - c0) // P, n, b.view[0:t1 - t0, :], step)]


def project_tokens(m, src, ready, dram, c0, c1, evacuate, kt=KD):
    for g0 in range(c0, c1, GROUP):
        g1 = min(g0 + GROUP, c1)
        w, landed, read_by = m.weights.take(dram, g0, g1)
        for blk in range(NB):
            b = m.bank()
            step = product(m, b.view[:, 0:g1 - g0], lambda a, k, blk=blk: src[:, a, k, blk * P:(blk + 1) * P],
                           lambda s, k: w[:, s, k, :], kt, [landed, ready], b.readers)
            read_by(step)
            b.readers = [evacuate(blk, g0 - c0, b.view[:, 0:g1 - g0], step)]


class Background:

    def __init__(self, m):
        self.m = m
        self.weights = Weights(m, "background", P, 2, 2, 1)
        self.out = [Slot(m.take(BANK), m.sem(f"background_out{i}")) for i in range(2)]
        self.bank = m.banks[5]
        self.units, self.turn, self.pending, self.current = [], 0, None, None
        self.stored = {}

    def add(self, h, h_ready, dram, c0, c1, to, row0):
        self.weights.extend(dram, c0, c1)
        for c in range(c0, c1, P):
            for n in range(HALVES):
                self.units.append((h, h_ready, dram, c, n, to, row0 + c - c0))

    def flush(self):
        if self.pending:
            slot, out, step, key = self.pending
            self.stored[key] = slot.fill(self.m.act, [(out, slot.view)], step)
            self.pending = None

    def step(self):
        m = self.m
        if self.current is None:
            if not self.units:
                return
            self.current, self.k = self.units.pop(0), 0
            if self.current[4] == 0:
                self.w = self.weights.take(*self.current[2:4], self.current[3] + P)
        h, h_ready, dram, c, half, to, row = self.current
        w, landed, read_by = self.w
        cols = slice(half * BANK, (half + 1) * BANK)
        for k in range(self.k, self.k + KD // 4):
            for n, (a, b) in enumerate(PRODUCTS):
                step = m.pe(lambda e, l=w[:, a, k, :], r=h[:, b, k, cols], first=(k + n == 0), last=(k == KD - 1 and n == 2):
                            e.matmul(self.bank.view, l, r, start=first, stop=last),
                            h_ready(k), [landed, self.bank.readers] if k + n == 0 else None)
        read_by(step)
        self.k += KD // 4
        if self.k < KD:
            return
        self.flush()
        slot = self.out[self.turn % 2]
        self.turn += 1
        step = m.act(lambda e: e.activation(slot.view, self.bank.view, ACT.Copy), step,
                     slot.landed if slot.filled else None)
        self.bank.readers = [step]
        self.pending = (slot, to[row:row + P, cols], step, (id(to), row, half))
        self.current = None

    def run(self, n=1):
        for _ in range(4 * n):
            self.step()

    def run_until(self, to, row):
        while any(u[5] is to and GATE_ROWS <= u[6] < row for u in self.units + [self.current] if u):
            self.step()
        self.flush()

    def arrived(self, to, row):
        return [self.stored[id(to), row, half] for half in range(HALVES)]

    def finish(self):
        self.run(len(self.units) + 1)
        self.flush()


def rounds(jobs, depth):
    jobs = iter(jobs)
    active = []
    while True:
        if len(active) < depth:
            job = next(jobs, None)
            if job is not None:
                active = active + [job]
        if not active:
            return
        active = [j for j in active if next(j, "done") != "done"]
        yield


def interleave(m, jobs, depth, background=0, every=1):
    for n, _ in enumerate(rounds(jobs, depth)):
        for _ in range(background if n % every == 0 else 0):
            m.background.step()



TOPK = 256
AH, AD = 4, 128
IH, ID = 8, 64
QR = 256


def dsa(m, c, io, hT, h_ready, y, fence):
    w_in = io["w_in"]
    C0 = 2 * 512 + 3 * 512 + 8 + 512
    K0 = C0 + QR
    V0 = K0 + AD
    NTOK = QR + AD + ID + IH
    tok = m.take(NB, NTOK)
    kT = m.take(T)
    kiT = m.take(T)
    cqT = m.take(2, T)
    qT = m.take(4, T)
    qiT = m.take(4, T)
    score = [m.take((b + 1) * P) for b in range(NB)]
    ki2 = m.take(NB, 2, ID)
    sq = m.take(NB, ID)
    stat = m.take(6, NB)
    wi = m.take(NB, IH)
    best = m.take(8)
    relu = m.take(3, BANK)
    prob, probT = qiT[:, 0:2, :], qiT[:, 2:4, :]
    small = m.take(2, 8)
    att = cqT.rearrange("p a t -> p (a t)")[:, 0:2 * BANK].rearrange("p (a t) -> p a t", a=2)

    tok_done = [None] * NB

    def evac_tok(first):
        def evac(blk, c0, ps, step):
            o = tok[:, blk, first + c0:first + c0 + ps.shape[1]]
            s = m.act(lambda e: e.activation(o, ps, ACT.Copy), step)
            tok_done[blk] = s
            return s
        return evac

    project_tokens(m, hT, h_ready, w_in, C0, C0 + QR, evac_tok(0))
    project_tokens(m, hT, h_ready, w_in, V0, V0 + NTOK - QR, evac_tok(QR))
    k_done = []

    def evac_k(i, n, ps, step):
        s = m.act(lambda e: e.activation(kT[:, n * BANK:(n + 1) * BANK], ps, ACT.Copy), step)
        k_done.append(s)
        return s

    project_channels(m, hT, h_ready, w_in, K0, K0 + AD, evac_k)

    junk = relu[:, 0, 0:QR]
    s = None
    for blk in range(NB):
        s = m.act(lambda e, blk=blk: e.activation(junk, tok[:, blk, 0:QR], ACT.Square, accum_out=stat[:, 0, blk:blk + 1]),
                  tok_done[blk], s)
    s = m.dve(lambda e: e.tensor_scalar(stat[:, 1, :], stat[:, 0, :], 1.0 / QR, EPS, ALU.mult, ALU.add), s, fence)
    s = root_of_inverse(m, stat[:, 1, :], s)
    s = m.dve(lambda e: e.tensor_tensor(tok[:, :, 0:QR], tok[:, :, 0:QR],
                                        stat[:, 1, :].unsqueeze(2).to_broadcast([P, NB, QR]), ALU.mult), s)
    cq_done = []
    for j in range(2):
        for g in range(2):
            b = m.bank()
            for i in range(4):
                blk = g * 4 + i
                t = m.pe(lambda e, b=b, i=i, blk=blk, j=j: e.transpose(
                    b.view[:, i * P:(i + 1) * P], tok[:, blk, j * P:(j + 1) * P], c.ident), s, c.ready,
                    b.readers if i == 0 else None)
            t = m.act(lambda e, b=b, j=j, g=g: e.activation(cqT[:, j, g * BANK:(g + 1) * BANK], b.view, ACT.Copy,
                                                            scale=c.vec("q_norm_g", j)), t)
            b.readers = [t]
            cq_done.append(t)

    KI = slice(QR + AD, QR + AD + ID)
    s = m.dve(lambda e: e.tensor_reduce(stat[:, 2, :], tok[:, :, KI], AX.X, ALU.add), tok_done)
    s = m.dve(lambda e: e.tensor_scalar(stat[:, 2, :], stat[:, 2, :], 1.0 / ID, None, ALU.mult), s)
    s = m.dve(lambda e: e.tensor_tensor(tok[:, :, KI], tok[:, :, KI],
                                        stat[:, 2, :].unsqueeze(2).to_broadcast([P, NB, ID]), ALU.subtract), s)
    s = m.dve(lambda e: e.tensor_tensor(sq, tok[:, :, KI], tok[:, :, KI], ALU.mult), s)
    s = m.dve(lambda e: e.tensor_reduce(stat[:, 3, :], sq, AX.X, ALU.add), s)
    s = m.dve(lambda e: e.tensor_scalar(stat[:, 3, :], stat[:, 3, :], 1.0 / ID, EPS, ALU.mult, ALU.add), s)
    s = root_of_inverse(m, stat[:, 3, :], s)
    for r in range(2):
        s2 = m.dve(lambda e, r=r: e.tensor_tensor(ki2[:, :, r, :], tok[:, :, KI],
                                                  stat[:, 3, :].unsqueeze(2).to_broadcast([P, NB, ID]), ALU.mult), s)
    ki_done = []
    for g in range(2):
        b = m.bank()
        for i in range(4):
            t = m.pe(lambda e, b=b, i=i, g=g: e.transpose(
                b.view[:, i * P:(i + 1) * P], ki2[:, g * 4 + i, :, :].rearrange("p r d -> p (r d)"), c.ident), s2,
                b.readers if i == 0 else None)
        t = m.dve(lambda e, b=b, g=g: e.tensor_scalar(kiT[:, g * BANK:(g + 1) * BANK], b.view,
                                                      c.vec("kidx_norm_g"), c.vec("kidx_norm_b"), ALU.mult, ALU.add), t)
        b.readers = [t]
        ki_done.append(t)
    wi_done = m.dve(lambda e: e.tensor_scalar(wi, tok[:, :, NTOK - IH:NTOK], float(IH) ** -0.5, float(ID) ** -0.5,
                                              ALU.mult, ALU.mult), tok_done)

    q_done = {}
    cq_split = m.take_pair(2, T)
    pieces = []
    for j in range(2):
        pieces += split(m, cqT[:, j, :], [cq_split[:, r, j, :] for r in range(2)], cq_done)
    for name, dst in (("w_qidx", qiT), ("w_uq", qT)):
        def evac_q(i, n, ps, step, name=name, dst=dst):
            s = m.act(lambda e: e.activation(dst[:, i, n * BANK:(n + 1) * BANK], ps, ACT.Copy), step)
            q_done[name] = s
            return s

        project_channels(m, cq_split, pieces, io[name], 0, 512, evac_q, kt=2)

    relu_free = [None] * 3
    turn = [0]
    score_done = [None] * NB

    def index_score(b):
        for c0 in range(0, (b + 1) * P, BANK):
            c1 = min(c0 + BANK, (b + 1) * P)
            prev = None
            for h in range(IH):
                r0 = ID * (h % 2)
                pb = m.bank()
                s = m.pe(lambda e, h=h, r0=r0, pb=pb, c0=c0, c1=c1: e.matmul(
                    pb.view[:, 0:c1 - c0], qiT[r0:r0 + ID, h // 2, b * P:(b + 1) * P], kiT[r0:r0 + ID, c0:c1],
                    start=True, stop=True), q_done["w_qidx"], ki_done, pb.readers)
                j = turn[0] % 3
                turn[0] += 1
                s = m.act(lambda e, pb=pb, j=j, n=c1 - c0: e.activation(relu[:, j, 0:n], pb.view[:, 0:n], ACT.Relu),
                          s, relu_free[j])
                pb.readers = [s]
                dst = score[b][:, c0:c1]
                if h == 0:
                    prev = m.dve(lambda e, j=j, h=h, dst=dst, n=c1 - c0: e.tensor_scalar(
                        dst, relu[:, j, 0:n], wi[:, b, h:h + 1], None, ALU.mult), s, wi_done)
                else:
                    prev = m.dve(lambda e, j=j, h=h, dst=dst, n=c1 - c0: e.scalar_tensor_tensor(
                        out=dst, in0=relu[:, j, 0:n], scalar=wi[:, b, h:h + 1], in1=dst, op0=ALU.mult, op1=ALU.add),
                        s, prev)
                relu_free[j] = prev
                yield
        diag = score[b][:, b * P:(b + 1) * P]
        score_done[b] = m.pool(lambda e: e.affine_select(
            out=diag, in_=diag, compare_op=ALU.is_ge, fill=FUTURE, base=0, pattern=[[-1, P]], channel_multiplier=1), prev)

    interleave(m, (index_score(b) for b in range(NB)), 1)
    scores_over = m.act.last

    SC = float(AD) ** -0.5
    y_done = []
    pfree, tfree, afree = [None, None], [None, None], [None, None]

    def attend(b, h, turn):
        N = (b + 1) * P
        out_bank = m.held[b % 2]
        j = turn % 2
        top = stat[:, 4, 2 * j:2 * j + 1]
        parts, logits = [], []
        for c0 in range(0, N, BANK):
            c1 = min(c0 + BANK, N)
            pb = m.bank()
            s = m.pe(lambda e, pb=pb, c0=c0, c1=c1: e.matmul(
                pb.view[:, 0:c1 - c0], qT[:, h, b * P:(b + 1) * P], kT[:, c0:c1], start=True, stop=True),
                q_done["w_uq"], k_done, pb.readers)
            logits.append((pb, s, c0, c1))
        yield
        for pb, s, c0, c1 in logits:
            i = len(parts)
            s = m.dve(lambda e, pb=pb, c0=c0, c1=c1, i=i: e.tensor_tensor_reduce(
                out=prob[:, j, c0:c1], in0=pb.view[:, 0:c1 - c0], in1=score[b][:, c0:c1], scale=1.0, scalar=-3e38,
                op0=ALU.add, op1=ALU.max, accum_out=stat[:, 4, 2 * j + i:2 * j + i + 1]),
                s, score_done[b], pfree[j], scores_over)
            pb.readers = [s]
            parts.append(s)
        if len(parts) == 2:
            s = m.dve(lambda e: e.tensor_tensor(top, top, stat[:, 4, 2 * j + 1:2 * j + 2], ALU.max), parts)
        s = m.dve(lambda e: e.tensor_scalar(stat[:, 5, j:j + 1], top, -SC, None, ALU.mult), s)
        s = m.act(lambda e: e.activation(prob[:, j, 0:N], prob[:, j, 0:N], ACT.Exp, bias=stat[:, 5, j:j + 1], scale=SC,
                                         accum_out=small[:, b % 2, h:h + 1]), s)
        last_exp = s
        yield
        for g in range(0, b + 1, 4):
            tb = m.bank()
            n = min(4, b + 1 - g)
            for i in range(n):
                s2 = m.pe(lambda e, tb=tb, i=i, g=g: e.transpose(
                    tb.view[:, i * P:(i + 1) * P], prob[:, j, (g + i) * P:(g + i + 1) * P], c.ident), s,
                    tb.readers if i == 0 else None)
            pfree[j] = s2
            cp = m.act(lambda e, tb=tb, g=g, n=n: e.activation(
                probT[:, j, g * P:(g + n) * P], tb.view[:, 0:n * P], ACT.Copy), s2, tfree[j])
            tb.readers = [cp]
        yield
        for i in range(b + 1):
            pv = m.pe(lambda e, i=i: e.matmul(
                out_bank.view[:, h * P:(h + 1) * P], probT[:, j, i * P:(i + 1) * P], tok[:, i, QR:QR + AD],
                start=(i == 0), stop=(i == b)), cp, out_bank.readers if h == 0 and i == 0 else None)
        tfree[j] = pv
        if h < AH - 1:
            return
        a = b % 2
        s = m.dve(lambda e: e.reciprocal(small[:, a, 4:8], small[:, a, 0:4]), last_exp)
        s = m.dve(lambda e: e.tensor_tensor(
            att[:, a, :].rearrange("p (h d) -> p h d", h=AH), out_bank.view.rearrange("p (h d) -> p h d", h=AH),
            small[:, a, 4:8].unsqueeze(2).to_broadcast([P, AH, AD]), ALU.mult), s, pv, afree[a])
        out_bank.readers = [s]
        yield
        tb = m.bank()
        for i in range(AH):
            s2 = m.pe(lambda e, i=i: e.transpose(tb.view[:, i * P:(i + 1) * P], att[:, a, i * P:(i + 1) * P], c.ident), s,
                      tb.readers if i == 0 else None)
        afree[a] = s2
        s = m.act(lambda e: e.activation(y[:, :, b * P:(b + 1) * P], tb.view.rearrange("p (h t) -> p h t", h=AH),
                                         ACT.Copy), s2)
        tb.readers = [s]
        y_done.append(s)

    def choose(b):
        s = score_done[b]
        if (b + 1) * P > TOPK:
            for n in range(TOPK // 8):
                s = m.dve(lambda e: e.max(best, score[b]), s)
                s = m.dve(lambda e: e.match_replace(score[b], best, score[b], TAKEN), s)
                if n % 4 == 3:
                    yield
            s = m.dve(lambda e: e.tensor_scalar(score[b], score[b], TAKEN, DROP, ALU.not_equal, ALU.mult), s)
        else:
            s = m.dve(lambda e: e.tensor_scalar(score[b], score[b], 0.5 * FUTURE, DROP, ALU.is_lt, ALU.mult), s)
        score_done[b] = s

    attention = rounds([], 2)
    for b in range(NB):
        for n, _ in enumerate(choose(b)):
            next(attention, None)
            for _ in range((n + 1) * 5 * (b + 1) // 8 - n * 5 * (b + 1) // 8):
                m.background.step()
        for _ in attention:
            pass
        attention = rounds([attend(b, h, b * AH + h) for h in range(AH)], 2)
    for _ in attention:
        pass
    return y_done



def vector_columns(names):
    at, n = {}, 0
    for name, width in names:
        at[name] = (n, width)
        n += width
    return at, n


VECS = [("norm_g", 8), ("ssm_d", 4), ("glu_b", 4), ("qk_conv_w", 32), ("qk_conv_b", 8), ("mh_norm_g", 4),
        ("q_norm_g", 2), ("kidx_norm_g", 1), ("kidx_norm_b", 1), ("final_norm_g", 8), ("igate_b", 1), ("fgate_b", 1),
        ("norm_g_2", 8), ("conv_w_2", 40), ("conv_b_2", 10), ("dt_bias_2", 1), ("a_log_2", 1), ("ssd_norm_g_2", 8),
        ("rw_mu_2", 17), ("rw_w0_2", 4), ("rw_a0_2", 4), ("rw_k_k_2", 4), ("rw_k_a_2", 4), ("rw_r_k_2", 4),
        ("rw_ln_g_2", 4), ("rw_ln_b_2", 4), ("final_g_2", 8), ("ssm_a_re", 16), ("ssm_a_im", 16), ("ssm_log_dt", 16),
        ("d_skip_2", 16)]
VEC_AT, VEC_N = vector_columns(VECS)


class Constants:

    def row_picker(self, heads, h):
        return self.ident[0:heads, h:h + 1].to_broadcast([heads, P])

    def vec(self, name, i=0):
        c0, n = VEC_AT[name]
        return self.vectors[:, c0 + i:c0 + i + 1]

    def vecs(self, name):
        c0, n = VEC_AT[name]
        return self.vectors[:, c0:c0 + n]


def setup(nc, ctx, io):
    m = Machine(nc, ctx)
    c = Constants()
    c.vectors = m.take(VEC_N)
    vs = Slot(c.vectors, m.sem("vectors_in"))
    c.landed = vs.fill(m.sp, [(c.vectors, io["vectors"])])
    make_constants(m, c)
    m.weights = Weights(m, "weights", GROUP, 3, 3, AHEAD)
    m.background = Background(m)
    for q in (m.act, m.dve, m.pe, m.pool):
        m_wait(q, [c.landed, c.ready] if q is not m.pool else [c.landed])
    return m, c


def m_wait(queue, producers):
    flat = flatten(producers)
    for x in flat:
        if isinstance(x, Step):
            x.needed = True
    queue.items.append((None, flat, Step(queue)))


GATE_ROWS = 3 * D
FIRST_Z_ROWS = [GATE_ROWS, GATE_ROWS + 512, GATE_ROWS + 1024]
SB_Z_ROW, SSD_Z_ROW, RW_Z_ROW = GATE_ROWS, GATE_ROWS + 512, GATE_ROWS + 1536

SCRATCH = [("s5_scratch", (512, T)), ("y_first0", (512, T)), ("y_first1", (512, T)), ("y_first2", (512, T)),
           ("y_second0", (512, T)), ("y_second1", (1024, T)), ("y_second2", (512, T)), ("x_middle", (D, T)),
           ("gates_first", (GATE_ROWS + 1536, T)), ("gates_second", (GATE_ROWS + 2048, T))]



MH, MD = 4, 128


def depthwise_conv(m, c, src, dst, i, tiles, wname, bname, ready, free):
    def tap(k):
        return c.vec(wname, k * tiles + i)

    s = m.dve(lambda e: e.tensor_scalar(dst, src[:, 3:3 + T], tap(3), c.vec(bname, i), ALU.mult, ALU.add), ready, free)
    for k in range(3):
        s = m.dve(lambda e, k=k: e.scalar_tensor_tensor(out=dst, in0=src[:, k:k + T], scalar=tap(k), in1=dst,
                                                        op0=ALU.mult, op1=ALU.add), s)
    return s


def log_sigmoid_rows(m, x, tmp, s):
    a = m.act(lambda e: e.activation(tmp, x, ACT.Abs), s)
    a = m.act(lambda e: e.activation(tmp, tmp, ACT.Exp, scale=-1.0), a)
    a = m.act(lambda e: e.activation(tmp, tmp, ACT.Ln, bias=1.0), a)
    s = m.dve(lambda e: e.tensor_scalar(x, x, 0.0, None, ALU.min), a)
    return m.dve(lambda e: e.tensor_tensor(x, x, tmp, ALU.subtract), s)


def mlstm(m, c, io, hT, h_ready, y, fence):
    w_in = io["w_in"]
    Q0 = 2 * 512
    V0 = Q0 + 2 * 512
    I0 = V0 + 512
    qk = m.take(8, T)
    v1 = m.take(NB, MH, MD + 1)
    weight = m.take(NB * (NB + 1) // 2 * P)
    negM = m.take(T)
    raw = m.take(2, T + 3)
    ig = m.take(T)
    F = m.take(T)
    M = m.take(T)
    hnum = m.take(NB, MD + 1)
    tokg = m.take(2, NB, MH)
    small = m.take(3, NB)
    E = m.take(2, BANK)
    SC = float(MD) ** -0.5

    for j in range(2):
        pad = m.pool(lambda e, j=j: e.memset(raw[:, j, 0:3], 0.0), fence)
    raw_free = [None, None]
    qk_done = {}
    for g in range(2):
        halves = {}

        def evac(i, n, ps, step, g=g, halves=halves):
            t = g * 4 + i
            j = t % 2
            s = m.act(lambda e: e.activation(raw[:, j, 3 + n * BANK:3 + (n + 1) * BANK], ps, ACT.Copy),
                      step, raw_free[j], fence)
            if n == 1:
                cv = depthwise_conv(m, c, raw[:, j, :], qk[:, t, :], t, 8, "qk_conv_w", "qk_conv_b", [s, pad], fence)
                raw_free[j] = cv
                qk_done[t] = m.act(lambda e, t=t: e.activation(qk[:, t, :], qk[:, t, :], ACT.Silu), cv)
            return s

        project_channels(m, hT, h_ready, w_in, Q0 + g * BANK, Q0 + (g + 1) * BANK, evac)

    one = m.pool(lambda e: e.memset(v1[:, :, :, MD:MD + 1], 1.0), fence)
    v_done = [one]

    def evac_v(blk, c0, ps, step):
        h0, nh = c0 // MD, ps.shape[1] // MD
        s = m.act(lambda e: e.activation(v1[:, blk, h0:h0 + nh, 0:MD], ps.rearrange("p (h d) -> p h d", h=nh), ACT.Copy), step)
        v_done.append(s)
        return s

    project_tokens(m, hT, h_ready, w_in, V0, V0 + 512, evac_v)

    rows = {}
    w, landed, read_by = m.weights.take(w_in, I0, I0 + 8)
    for i, (dst, bias) in enumerate(((ig, "igate_b"), (F, "fgate_b"))):
        for n in range(HALVES):
            cols = slice(n * BANK, (n + 1) * BANK)
            b = m.bank()
            step = product(m, b.view[0:MH, :], lambda a, k, i=i: w[:, a, k, MH * i:MH * (i + 1)],
                           lambda s, k, cols=cols: hT[:, s, k, cols], KD, [landed, h_ready], b.readers)
            read_by(step)
            rows[i] = m.dve(lambda e, b=b, dst=dst, cols=cols, bias=bias: e.tensor_scalar(
                dst[0:MH, cols], b.view[0:MH, :], c.vec(bias)[0:MH], None, ALU.add), step)
            b.readers = [rows[i]]
    R = slice(0, MH)
    m.background.run(2)
    s = log_sigmoid_rows(m, F[R], M[R], rows[1])
    s = m.dve(lambda e: e.tensor_tensor_scan(F[R], c.zero[R].to_broadcast([MH, T]), F[R], 0.0, ALU.add, ALU.add), s)
    a = m.dve(lambda e: e.tensor_tensor(ig[R], ig[R], F[R], ALU.subtract), s, rows[0])
    s = m.dve(lambda e: e.tensor_tensor_scan(M[R], ig[R], ig[R], 0.0, ALU.max, ALU.max), a)
    mr = m.dve(lambda e: e.tensor_tensor(F[R], F[R], M[R], ALU.add), s)
    nm = m.dve(lambda e: e.tensor_scalar(M[R], M[R], -1.0, None, ALU.mult), mr)
    b = m.bank()
    first = True
    for r, (row, dep) in enumerate(((ig, a), (F, mr))):
        for blk in range(NB):
            o = (r * NB + blk) * MH
            t = m.pe(lambda e, row=row, blk=blk, o=o, b=b: e.transpose(
                b.view[:, o:o + MH], row[R, blk * P:(blk + 1) * P], c.ident[R, 0:MH]), dep, b.readers if first else None)
            first = False
    s = m.dve(lambda e, b=b: e.tensor_copy(tokg[:, 0].rearrange("p b h -> p (b h)"), b.view[:, 0:NB * MH]), t)
    s2 = m.act(lambda e, b=b: e.activation(tokg[:, 1].rearrange("p b h -> p (b h)"), b.view[:, NB * MH:2 * NB * MH],
                                           ACT.Exp, scale=-1.0), t, s)
    b.readers = [s2]
    tok_ready = [s, s2]

    def at(j):
        return sum((NB - i) * P for i in range(j))

    E_free = [None, None]
    turn = 0
    nm_free, w_free, hn_free = None, None, None
    y_done = []
    for h in range(MH):
        for n in range(HALVES):
            b = m.bank()
            s = m.pe(lambda e, b=b, h=h, n=n: e.matmul(b.view, c.row_picker(MH, h), M[R, n * BANK:(n + 1) * BANK],
                                                       start=True, stop=True), nm, b.readers)
            s = m.dve(lambda e, b=b, n=n: e.tensor_copy(negM[:, n * BANK:(n + 1) * BANK], b.view), s, nm_free)
            b.readers = [s]
        neg_ready = s
        wdone = {}
        for j in range(NB):
            for t0 in range(j * P, T, BANK):
                t1 = min(t0 + BANK, T)
                n = t1 - t0
                b = m.bank()
                s = m.pe(lambda e, b=b, h=h, j=j, t0=t0, t1=t1, n=n: e.matmul(
                    b.view[:, 0:n], qk[:, 4 + h, j * P:(j + 1) * P], qk[:, h, t0:t1], start=True, stop=True),
                    qk_done[h], qk_done[4 + h], b.readers)
                k = turn % 2
                turn += 1
                bias = tokg[:, 0, j, h:h + 1]
                diag = t0 == j * P
                deps = [neg_ready, tok_ready]
                if diag:
                    d = m.dve(lambda e, k=k, bias=bias, t0=t0: e.tensor_scalar(
                        E[:, k, 0:P], negM[:, t0:t0 + P], bias, 0.0, ALU.add, ALU.min), deps, E_free[k])
                    x = m.act(lambda e, k=k: e.activation(E[:, k, 0:P], E[:, k, 0:P], ACT.Exp), d)
                    mask = m.pool(lambda e, k=k: e.affine_select(out=E[:, k, 0:P], in_=E[:, k, 0:P], compare_op=ALU.is_ge,
                                                                 fill=0.0, base=0, pattern=[[1, P]],
                                                                 channel_multiplier=-1), x)
                    if n > P:
                        x = m.act(lambda e, k=k, bias=bias, t0=t0, n=n, t1=t1: e.activation(
                            E[:, k, P:n], negM[:, t0 + P:t1], ACT.Exp, bias=bias))
                    x = [x, mask]
                else:
                    x = m.act(lambda e, k=k, bias=bias, t0=t0, n=n, t1=t1: e.activation(
                        E[:, k, 0:n], negM[:, t0:t1], ACT.Exp, bias=bias), deps, E_free[k])
                o = at(j) + t0 - j * P
                s = m.dve(lambda e, b=b, k=k, n=n, o=o: e.scalar_tensor_tensor(
                    out=weight[:, o:o + n], in0=b.view[:, 0:n], scalar=SC, in1=E[:, k, 0:n], op0=ALU.mult, op1=ALU.mult),
                    s, x, w_free)
                b.readers = [s]
                E_free[k] = s
        nm_free = x
        for g in range(0, NB, 3):
            b = m.bank()
            nblk = min(3, NB - g)
            for i in range(nblk):
                for j in range(g + i + 1):
                    o = at(j) + (g + i - j) * P
                    t = m.pe(lambda e, b=b, i=i, j=j, o=o, h=h, g=g: e.matmul(
                        b.view[:, i * (MD + 1):(i + 1) * (MD + 1)], weight[:, o:o + P], v1[:, j, h, :],
                        start=(j == 0), stop=(j == g + i)), s, v_done, b.readers if i == 0 and j == 0 else None)
            cp = m.act(lambda e, b=b, g=g, nblk=nblk: e.activation(
                hnum[:, g:g + nblk, :].rearrange("p b d -> p (b d)"), b.view[:, 0:nblk * (MD + 1)], ACT.Copy), t, hn_free)
            b.readers = [cp]
        w_free = t
        m.background.run(1)
        den = hnum[:, :, MD]
        s = m.act(lambda e, den=den: e.activation(small[:, 0, :], den, ACT.Abs), cp)
        s = m.dve(lambda e, h=h: e.tensor_tensor(small[:, 0, :], small[:, 0, :], tokg[:, 1, :, h], ALU.max), s, tok_ready)
        s = m.dve(lambda e: e.reciprocal(small[:, 0, :], small[:, 0, :]), s)
        num = hnum[:, :, 0:MD]
        s = m.dve(lambda e, num=num: e.tensor_tensor(num, num, small[:, 0, :].unsqueeze(2).to_broadcast([P, NB, MD]), ALU.mult), s)
        junk = E[:, 0, 0:P]
        q = [s, E_free]
        for blk in range(NB):
            q = m.act(lambda e, blk=blk, junk=junk: e.activation(junk, hnum[:, blk, 0:MD], ACT.Square,
                                                                accum_out=small[:, 1, blk:blk + 1]), q)
        s = m.dve(lambda e: e.tensor_scalar(small[:, 1, :], small[:, 1, :], 1.0 / MD, EPS, ALU.mult, ALU.add), q)
        m.background.run(1)
        s = root_of_inverse(m, small[:, 1, :], s)
        s = m.dve(lambda e, num=num: e.tensor_tensor(num, num, small[:, 1, :].unsqueeze(2).to_broadcast([P, NB, MD]), ALU.mult), s)
        E_free = [s, s]
        for g in range(2):
            b = m.bank()
            for i in range(4):
                t = m.pe(lambda e, b=b, i=i, g=g: e.transpose(b.view[:, i * P:(i + 1) * P], hnum[:, g * 4 + i, 0:MD], c.ident),
                         s, b.readers if i == 0 else None)
            cp = m.act(lambda e, b=b, g=g, h=h: e.activation(y[:, h, g * BANK:(g + 1) * BANK], b.view, ACT.Copy,
                                                             scale=c.vec("mh_norm_g", h)), t, fence)
            b.readers = [cp]
            y_done.append(cp)
        hn_free = t
    return y_done



SG, SN, SP_ = 32, 64, 16
SL = 8
SC_ = T // SL
NP_ = SG // 2


def s5_parameters(m, c, io, S):
    par = m.take(24, NP_)
    bmat = m.take(2, NP_, SP_)
    cmat = m.take(2, NP_, SP_)
    bb = m.take(2, NP_, SP_)
    pw = m.take(2, SL + 1, NP_)
    tmp = m.take(2, NP_ * SC_ // 2)
    slot = Slot(bmat, m.sem("ssm_params_in"))
    landed = slot.fill(m.sp, [(bmat, io["ssm_b"].rearrange("p (r j q) -> p r j q", r=2, j=NP_)),
                              (cmat, io["ssm_c"].rearrange("p (r j q) -> p r j q", r=2, j=NP_))])
    dt, mag, ang, k, r, sn, hs, cm1, are, aim, den, fr, fi, am1, zr, zi, m8, u1, u2, u3 = [par[:, i, :] for i in range(20)]
    ar, ai, ldt = c.vecs("ssm_a_re"), c.vecs("ssm_a_im"), c.vecs("ssm_log_dt")
    TT = lambda o, a, b, op, *d: m.dve(lambda e: e.tensor_tensor(o, a, b, op), m.dve.last, *d)
    TS = lambda o, a, s1, s2, o1, o2, *d: m.dve(lambda e: e.tensor_scalar(o, a, s1, s2, o1, o2), m.dve.last, *d)

    def cmul(o_re, o_im, a_re, a_im, b_re, b_im, t1, t2):
        TT(o_re, a_re, b_re, ALU.mult)
        TT(t1, a_im, b_im, ALU.mult)
        TT(o_re, o_re, t1, ALU.subtract)
        TT(o_im, a_re, b_im, ALU.mult)
        TT(t2, a_im, b_re, ALU.mult)
        return TT(o_im, o_im, t2, ALU.add)

    bits = m.take(NP_).bitcast(I32)
    accurate_exp(m, dt, ldt, (u2, u3), bits)
    TT(u1, ar, dt, ALU.mult)
    accurate_exp(m, mag, u1, (u2, u3), bits)
    TT(ang, ai, dt, ALU.mult)
    TS(k, ang, 1.0 / (2 * np.pi), 12582912.0, ALU.mult, ALU.add)
    TS(k, k, 12582912.0, None, ALU.subtract, ALU.bypass)
    two_pi = 2 * np.pi
    p1 = float(np.float32(6.28125))
    p2 = float(np.float32(np.round((two_pi - p1) * 2.0 ** 21) / 2.0 ** 21))
    p3 = float(np.float32(two_pi - p1 - p2))
    src = ang
    for part in (p1, p2, p3):
        m.dve(lambda e, part=part, src=src: e.scalar_tensor_tensor(out=r, in0=k, scalar=-part, in1=src, op0=ALU.mult,
                                                                   op1=ALU.add), m.dve.last)
        src = r
    TS(r, r, 0.5, None, ALU.mult, ALU.bypass)
    TT(k, r, r, ALU.mult)
    polynomial(m, hs, k, [(-1.0) ** n / math.factorial(2 * n + 1) for n in range(8)])
    TT(hs, hs, r, ALU.mult)
    polynomial(m, cm1, k, [(-1.0) ** n / math.factorial(2 * n) for n in range(9)])
    TT(sn, hs, cm1, ALU.mult)
    TS(sn, sn, 2.0, None, ALU.mult, ALU.bypass)
    TT(cm1, hs, hs, ALU.mult)
    TS(cm1, cm1, -2.0, None, ALU.mult, ALU.bypass)
    TT(u1, mag, cm1, ALU.mult)
    TT(are, mag, u1, ALU.add)
    TT(aim, mag, sn, ALU.mult)
    TS(am1, mag, -1.0, None, ALU.add, ALU.bypass)
    TT(am1, am1, u1, ALU.add)
    TT(den, ar, ar, ALU.mult)
    TT(u1, ai, ai, ALU.mult)
    TT(den, den, u1, ALU.add)
    m.dve(lambda e: e.reciprocal(den, den), m.dve.last)
    TT(fr, am1, ar, ALU.mult)
    TT(u1, aim, ai, ALU.mult)
    TT(fr, fr, u1, ALU.add)
    TT(fr, fr, den, ALU.mult)
    TT(fi, aim, ar, ALU.mult)
    TT(u1, am1, ai, ALU.mult)
    TT(fi, fi, u1, ALU.subtract)
    TT(fi, fi, den, ALU.mult)
    wide = lambda v: v.unsqueeze(2).to_broadcast([P, NP_, SP_])
    t1 = tmp[:, 0, 0:NP_ * SP_].rearrange("p (j q) -> p j q", j=NP_)
    t2 = tmp[:, 1, 0:NP_ * SP_].rearrange("p (j q) -> p j q", j=NP_)
    m_wait(m.dve, [landed])
    cmul(bb[:, 0], bb[:, 1], bmat[:, 0], bmat[:, 1], wide(fr), wide(fi), t1, t2)
    m.dve(lambda e: e.memset(pw[:, 0, 0, :], 1.0))
    m.dve(lambda e: e.memset(pw[:, 1, 0, :], 0.0))
    TS(pw[:, 0, 1, :], are, 0.0, None, ALU.add, ALU.bypass)
    TS(pw[:, 1, 1, :], aim, 0.0, None, ALU.add, ALU.bypass)
    n = 1
    while n < SL:
        rows = lambda r_, a, b: pw[:, r_, a:b, :]
        top = lambda r_, n=n: pw[:, r_, n:n + 1, :].to_broadcast([P, n, NP_])
        v1_ = tmp[:, 0, 0:n * NP_].rearrange("p (k j) -> p k j", k=n)
        v2_ = tmp[:, 1, 0:n * NP_].rearrange("p (k j) -> p k j", k=n)
        cmul(rows(0, n + 1, 2 * n + 1), rows(1, n + 1, 2 * n + 1), rows(0, 1, n + 1), rows(1, 1, n + 1), top(0), top(1), v1_, v2_)
        n *= 2
    ca = S.ca
    K9 = SL + 1
    tf = [tmp[:, i, 0:K9 * SP_].rearrange("p (k q) -> p k q", k=K9) for i in range(2)]
    for j in range(NP_):
        sh = [P, K9, SP_]
        cj = lambda r_, j=j: cmat[:, r_, j, :].unsqueeze(1).to_broadcast(sh)
        pj = lambda r_, j=j: pw[:, r_, :, j].unsqueeze(2).to_broadcast(sh)
        x1, x2 = tf
        TT(ca[:, 0, j], cj(0), pj(0), ALU.mult)
        TT(x1, cj(1), pj(1), ALU.mult)
        TT(ca[:, 0, j], ca[:, 0, j], x1, ALU.subtract)
        TT(ca[:, 1, j], cj(0), pj(1), ALU.mult)
        TT(x2, cj(1), pj(0), ALU.mult)
        m.dve(lambda e, j=j, x2=x2: e.scalar_tensor_tensor(out=ca[:, 1, j], in0=ca[:, 1, j], scalar=-1.0, in1=x2,
                                                           op0=ALU.mult, op1=ALU.subtract), m.dve.last)
    ca_done = m.dve.last
    m.background.run(12)
    wtmp = m.take(2, NP_, SL, SP_)
    for j in range(NP_):
        sh = [P, SL, SP_]
        bj = lambda r_, j=j: bb[:, r_, j, :].unsqueeze(1).to_broadcast(sh)
        pj = lambda r_, j=j: pw[:, r_, SL - 1::-1, j].unsqueeze(2).to_broadcast(sh)
        x = tf[0][:, 0:SL, :]
        x2 = tf[1][:, 0:SL, :]
        cmul(wtmp[:, 0, j], wtmp[:, 1, j], bj(0), bj(1), pj(0), pj(1), x, x2)
    w_done = m.dve.last
    for r_ in range(2):
        for g in range(4):
            b = m.bank()
            for i in range(4):
                t = m.pe(lambda e, b=b, i=i, g=g, r_=r_: e.transpose(
                    b.view[:, i * P:(i + 1) * P], wtmp[:, r_, g * 4 + i].rearrange("p s q -> p (s q)"), c.ident),
                    w_done, b.readers if i == 0 else None)
            t = m.act(lambda e, b=b, g=g, r_=r_: e.activation(
                S.inject[:, r_, g * 4:(g + 1) * 4, :].rearrange("p j n -> p (j n)"), b.view, ACT.Copy), t)
            b.readers = [t]
    S.inject_done = t
    zero = m.dve(lambda e: e.memset(S.toeplitz, 0.0))
    kern = m.take(8, P)
    kslot = Slot(kern, m.sem("toeplitz_in"))
    kfree = None
    for g8 in range(4):
        for half in range(2):
            b = m.bank()
            for i in range(4):
                j, e0 = g8 * 4 + i, 64 * half
                for r_ in range(2):
                    t = m.pe(lambda e, b=b, i=i, j=j, e0=e0, r_=r_: e.matmul(
                        b.view[0:SP_, i * P:(i + 1) * P], bb[e0:e0 + 64, r_, j, :],
                        ca[e0:e0 + 64, r_, j, 0:SL, :].rearrange("p k q -> p (k q)"), start=(r_ == 0), stop=(r_ == 1)),
                        ca_done, b.readers if i == 0 and r_ == 0 else None)
            t = m.act(lambda e, b=b, half=half: e.activation(
                kern[0:SP_, half:8:2, :], b.view[0:SP_, :].rearrange("p (g n) -> p g n", g=4), ACT.Copy), t, kfree)
            b.readers = [t]
        pieces = [(S.toeplitz[SP_ * s:SP_ * (s + 1), g8 * 8:(g8 + 1) * 8, SP_ * s:P], kern[0:SP_, :, 0:P - SP_ * s])
                  for s in range(SL)]
        kfree = kslot.fill(m.sp, pieces, t, zero)
    S.toeplitz_done = kfree
    TS(u1, cm1, 1.0, None, ALU.add, ALU.bypass)
    cur = (u1, sn)
    for i in range(3):
        nxt = ((zr, zi), (fr, fi))[i % 2]
        cmul(nxt[0], nxt[1], cur[0], cur[1], cur[0], cur[1], u2, u3)
        cur = nxt
    TT(m8, mag, mag, ALU.mult)
    TT(m8, m8, m8, ALU.mult)
    TT(S.decay, m8, m8, ALU.mult)
    rot = S.rotor
    m.dve(lambda e: e.memset(rot[:, 0, :, 0:1], 1.0), m.dve.last)
    m.dve(lambda e: e.memset(rot[:, 1, :, 0:1], 0.0), m.dve.last)
    n = 1
    flip = [(am1, den), (zr, zi)]
    while n < SC_:
        sh = [P, NP_, n]
        zb = [x.unsqueeze(2).to_broadcast(sh) for x in cur]
        y1 = tmp[:, 0, 0:NP_ * n].rearrange("p (j c) -> p j c", j=NP_)
        y2 = tmp[:, 1, 0:NP_ * n].rearrange("p (j c) -> p j c", j=NP_)
        cmul(rot[:, 0, :, n:2 * n], rot[:, 1, :, n:2 * n], rot[:, 0, :, 0:n], rot[:, 1, :, 0:n], zb[0], zb[1], y1, y2)
        n *= 2
        if n < SC_:
            nxt = flip[0]
            flip = flip[::-1]
            if nxt[0] is cur[0]:
                nxt = flip[0]
                flip = flip[::-1]
            cmul(nxt[0], nxt[1], cur[0], cur[1], cur[0], cur[1], u2, u3)
            cur = nxt
    S.ready = m.dve.last


def accurate_exp(m, out, x, work, bits, *ready):
    k, r = work
    D = lambda f, *d: m.dve(f, m.dve.last, *d)
    D(lambda e: e.tensor_scalar(r, x, 88.0, -87.3, ALU.min, ALU.max), *ready)
    D(lambda e: e.tensor_scalar(k, r, 1.0 / float(np.log(2.0)), 12582912.0, ALU.mult, ALU.add))
    D(lambda e: e.tensor_scalar(k, k, 12582912.0, None, ALU.subtract))
    high = 0.693359375
    low = float(np.log(2.0)) - high
    D(lambda e: e.scalar_tensor_tensor(out=r, in0=k, scalar=-high, in1=r, op0=ALU.mult, op1=ALU.add))
    D(lambda e: e.scalar_tensor_tensor(out=r, in0=k, scalar=-low, in1=r, op0=ALU.mult, op1=ALU.add))
    polynomial(m, out, r, [1.0 / float(math.factorial(n)) for n in range(9)])
    D(lambda e: e.tensor_scalar(k, k, 127.0, 8388608.0, ALU.add, ALU.mult))
    D(lambda e: e.tensor_copy(bits, k))
    return D(lambda e: e.tensor_tensor(out, out, bits.bitcast(F32), ALU.mult))


def polynomial(m, out, x, coefficients):
    D = lambda f: m.dve(f, m.dve.last)
    top = coefficients[-1]
    D(lambda e: e.tensor_scalar(out, x, 0.0, top, ALU.mult, ALU.add))
    for a in coefficients[-2::-1]:
        D(lambda e: e.tensor_tensor(out, out, x, ALU.mult))
        D(lambda e, a=a: e.tensor_scalar(out, out, a, None, ALU.add))
    return m.dve.last


class S5State:
    pass


def s5(m, c, io, hT, h_ready, y, fence):
    w_in = io["w_in"]
    S = S5State()
    base = m.top
    S.ca = m.take(2, NP_, SL + 1, SP_)
    S.inject = m.take(2, NP_, P)
    S.toeplitz = m.take(SG, P)
    S.rotor = m.take(2, NP_, SC_)
    S.decay = m.take(NP_)
    mark = m.top
    if fence:
        for q in (m.act, m.dve, m.pool, m.sp):
            m_wait(q, fence)
    u_done = []

    def evac_u(i, n, ps, step):
        dst = y[:, i, :].rearrange("p (s c) -> p c s", s=SL)[:, n * (SC_ // 2):(n + 1) * (SC_ // 2), :]
        s = m.act(lambda e: e.activation(dst, ps.rearrange("p (c s) -> p c s", s=SL), ACT.Copy), step)
        u_done.append(s)
        return s

    project_channels(m, hT, h_ready, w_in, 0, 512, evac_u)
    by_channel = io["s5_scratch"].rearrange("(i p) t -> p i t", p=P)
    by_chunk = io["s5_scratch"].rearrange("(g q) (s c) -> s q g c", q=SP_, s=SL)
    out_slot = Slot(y, m.sem("u_out"))
    u_out = out_slot.fill(m.sp, [(by_channel, y)], u_done)
    s5_parameters(m, c, io, S)
    after_parameters = m.fence()
    m.top = mark
    U = m.take(SG, P)
    state = m.take(2, NP_, SC_)
    tmp = m.take(2, BANK)
    uslot = Slot(U, m.sem("u_in_chunks"))
    moves = [(U[SP_ * s_:SP_ * (s_ + 1), :, :], by_chunk[s_]) for s_ in range(SL)]
    u_in = uslot.fill(m.sp, moves, u_out, after_parameters)
    g_done = []
    tfree = None
    for q in range(4):
        pr = [m.bank() for _ in range(2)]
        for r_ in range(2):
            for i in range(4):
                j = q * 4 + i
                for e_ in range(2):
                    t = m.pe(lambda e, r_=r_, i=i, j=j, e_=e_, b=pr[r_]: e.matmul(
                        b.view[64 * e_:64 * e_ + 64, i * P:(i + 1) * P], S.inject[:, r_, j, 64 * e_:64 * e_ + 64],
                        U[:, 2 * j + e_, :], start=True, stop=True), u_in, S.inject_done,
                        pr[r_].readers if i == 0 and e_ == 0 else None)
        js = slice(q * 4, q * 4 + 4)
        flat = lambda v: v.rearrange("p j c -> p (j c)")
        zre, zim = flat(S.rotor[:, 0, js, :]), flat(S.rotor[:, 1, js, :])
        gre, gim = flat(state[:, 0, js, :]), flat(state[:, 1, js, :])
        D = lambda *a: m.dve(*a)
        s = m.dve(lambda e, b=pr[0], gre=gre, zre=zre: e.tensor_tensor(gre, b.view, zre, ALU.mult), t, after_parameters, S.ready)
        s = m.dve(lambda e, b=pr[1], zim=zim: e.tensor_tensor(tmp[:, 0, :], b.view, zim, ALU.mult), s)
        s = m.dve(lambda e, gre=gre: e.tensor_tensor(gre, gre, tmp[:, 0, :], ALU.add), s)
        s = m.dve(lambda e, b=pr[1], gim=gim, zre=zre: e.tensor_tensor(gim, b.view, zre, ALU.mult), s)
        s = m.dve(lambda e, b=pr[0], zim=zim: e.tensor_tensor(tmp[:, 1, :], b.view, zim, ALU.mult), s)
        pr[0].readers = pr[1].readers = [s]
        s = m.dve(lambda e, gim=gim: e.tensor_tensor(gim, gim, tmp[:, 1, :], ALU.subtract), s)
        for r_ in range(2):
            for i in range(4):
                j = q * 4 + i
                s3 = m.dve(lambda e, r_=r_, j=j: e.tensor_tensor_scan(
                    state[:, r_, j, :], S.decay[:, j:j + 1].to_broadcast([P, SC_]), state[:, r_, j, :], 0.0,
                    ALU.mult, ALU.add), s)
        g_done.append(s3)
    m.background.run(4)
    before = S.inject
    full = slice(0, SC_ - 1)
    s = m.dve(lambda e: e.memset(before[:, :, :, 0:1], 0.0), g_done)
    for q in range(4):
        js = slice(q * 4, q * 4 + 4)
        gre, gim = state[:, 0, js, full], state[:, 1, js, full]
        zre, zim = S.rotor[:, 0, js, full], S.rotor[:, 1, js, full]
        bre, bim = before[:, 0, js, 1:SC_], before[:, 1, js, 1:SC_]
        v = [tmp[:, i, :].rearrange("p (j c) -> p j c", j=4)[:, :, full] for i in range(2)]
        s = m.dve(lambda e, a=bre, x=gre, z=zre: e.tensor_tensor(a, x, z, ALU.mult), s, g_done[q])
        s = m.dve(lambda e, a=v[0], x=gim, z=zim: e.tensor_tensor(a, x, z, ALU.mult), s)
        s = m.dve(lambda e, a=bre, x=v[0]: e.tensor_tensor(a, a, x, ALU.subtract), s)
        s = m.dve(lambda e, a=bim, x=gre, z=zim: e.tensor_tensor(a, x, z, ALU.mult), s)
        s = m.dve(lambda e, a=v[1], x=gim, z=zre: e.tensor_tensor(a, x, z, ALU.mult), s)
        s = m.dve(lambda e, a=bim, x=v[1]: e.tensor_tensor(a, a, x, ALU.add), s)
    before_done = s
    outs = []
    for q in range(8):
        b = m.bank()
        for i in range(4):
            g = (q // 2) * 8 + 2 * i + q % 2
            j, e0 = g // 2, 64 * (g % 2)
            o = b.view[:, i * P:(i + 1) * P]
            t = m.pe(lambda e, o=o, g=g: e.matmul(o, S.toeplitz[:, g, :], U[:, g, :], start=True, stop=False),
                     S.toeplitz_done, u_in, b.readers if i == 0 else None)
            for r_ in range(2):
                t = m.pe(lambda e, o=o, r_=r_, j=j, e0=e0: e.matmul(
                    o, S.ca[e0:e0 + 64, r_, j, 1:SL + 1, :].rearrange("p k q -> p (k q)"), before[e0:e0 + 64, r_, j, :],
                    start=False, stop=(r_ == 1)), before_done)
        cp = m.act(lambda e, b=b, q=q: e.activation(U[:, (q // 2) * 8 + q % 2:(q // 2) * 8 + 8:2, :],
                                                    b.view.rearrange("p (g c) -> p g c", g=4), ACT.Copy), t)
        b.readers = [cp]
        outs.append(cp)
    ys = S.rotor.rearrange("p a j c -> p (a j c)").rearrange("p (i t) -> p i t", i=4)
    back = Slot(U, m.sem("s5_out"))
    gone = back.fill(m.sp, [(by_chunk[s_], U[SP_ * s_:SP_ * (s_ + 1), :, :]) for s_ in range(SL)], outs)
    yslot = Slot(ys, m.sem("s5_out_in"))
    y_in = yslot.fill(m.sp, [(ys, by_channel)], gone, before_done)
    gel = []
    for i in range(4):
        s = m.dve(lambda e, i=i: e.scalar_tensor_tensor(out=ys[:, i, :], in0=y[:, i, :], scalar=c.vec("ssm_d", i),
                                                        in1=ys[:, i, :], op0=ALU.mult, op1=ALU.add), y_in)
        gel.append(m.act(lambda e, i=i: e.activation(ys[:, i, :], ys[:, i, :], ACT.Gelu_apprx_tanh), s))
    g_split = state.rearrange("p a j c -> p (a j c)").bitcast(BF16).rearrange("p (s i t) -> p s i t", s=2, i=4)
    pieces = []
    for i in range(4):
        pieces += split(m, ys[:, i, :], [g_split[:, r_, i, :] for r_ in range(2)], gel[i], before_done)
    m.background.run(4)
    y_done = []

    gfree = [None, None]
    turn = [0]

    def evac_glu(i, n, ps, step):
        k = turn[0] % 2
        turn[0] += 1
        a = m.act(lambda e: e.activation(tmp[:, k, :], ps, ACT.Sigmoid, bias=c.vec("glu_b", i)), step, gfree[k], before_done)
        dst = y[:, i, :].rearrange("p (c s) -> p s c", s=SL)[:, n * 4:(n + 1) * 4, :]
        s = m.dve(lambda e: e.tensor_tensor(dst, ys[:, i, n * BANK:(n + 1) * BANK].rearrange("p (s c) -> p s c", s=4),
                                            tmp[:, k, :].rearrange("p (s c) -> p s c", s=4), ALU.mult), a, gel)
        gfree[k] = s
        y_done.append(s)
        return a

    project_channels(m, g_split, pieces, io["glu_w"], 0, 512, evac_glu, kt=4)
    m.top = base
    return y_done



BH, BD = 8, 64


def stick_breaking(m, c, io, hT, h_ready, y, fence):
    w_in = io["w_in_2"]
    q = m.take(4, T)
    k = m.take(4, T)
    v = m.take(NB, BH, BD)
    DEEP = 5
    z, sp, lg, A = [m.take(DEEP, BANK) for _ in range(4)]
    total = m.take(2, BANK)
    done = {}
    for name, dst, c0 in (("k", k, 512), ("q", q, 0)):

        def evac(i, n, ps, step, name=name, dst=dst):
            s = m.act(lambda e: e.activation(dst[:, i, n * BANK:(n + 1) * BANK], ps, ACT.Copy,
                                             scale=float(BD) ** -0.5 if name == "q" else 1.0), step)
            done[name] = s
            return s

        project_channels(m, hT, h_ready, w_in, c0, c0 + 512, evac)

    def evac_v(blk, c0, ps, step):
        o = v[:, blk].rearrange("p h d -> p (h d)")[:, c0:c0 + ps.shape[1]]
        s = m.act(lambda e: e.activation(o, ps, ACT.Copy), step)
        done["v"] = s
        return s

    project_tokens(m, hT, h_ready, w_in, 1024, 1536, evac_v)
    if fence:
        m_wait(m.dve, fence)
    m.act(lambda e: e.preload_act_table_set("natural_log_exp_and_others"))
    y_done = []
    free = {n: [None] * DEEP for n in ("z", "sp", "lg", "A")}
    running = [None, None]

    def step_down(b, par, j, i):
        out = m.held[par]
        e0 = BD * par
        zb = m.bank()
        for g in range(4):
            s = m.pe(lambda e, g=g: e.matmul(
                zb.view[:, g * P:(g + 1) * P], k[e0:e0 + BD, g, j * P:(j + 1) * P],
                q[e0:e0 + BD, g, b * P:(b + 1) * P], start=True, stop=True),
                done["k"], done["q"], zb.readers if g == 0 else None)
        yield
        zc = m.dve(lambda e: e.tensor_copy(z[:, i, :], zb.view), s, free["z"][i])
        zb.readers = [zc]
        a = m.dve(lambda e: e.scalar_tensor_tensor(out=lg[:, i, :], in0=z[:, i, :], scalar=-1.0, in1=z[:, i, :],
                                                   op0=ALU.mult, op1=ALU.min), zc, free["lg"][i])
        a = m.act(lambda e: e.activation(lg[:, i, :], lg[:, i, :], ACT.Exp), a)
        a = m.act(lambda e: e.activation(lg[:, i, :], lg[:, i, :], ACT.Ln, bias=1.0), a)
        yield
        s = m.dve(lambda e: e.scalar_tensor_tensor(out=sp[:, i, :], in0=z[:, i, :], scalar=0.0,
                                                   in1=lg[:, i, :], op0=ALU.max, op1=ALU.add), a, free["sp"][i])
        free["lg"][i] = s
        if j == b:
            s = m.pool(lambda e: e.affine_select(out=sp[:, i, :], in_=sp[:, i, :], compare_op=ALU.is_gt, fill=0.0, base=0,
                                                 pattern=[[0, 4], [1, P]], channel_multiplier=-1), s)
        rb = m.bank()
        r = m.pe(lambda e: e.matmul(rb.view, c.tail_t, sp[:, i, :], start=True, stop=(j == b)), s, rb.readers)
        if j < b:
            r = m.pe(lambda e: e.matmul(rb.view, c.ones, total[:, par, :], start=False, stop=True), running[par])
        if j == b:
            running[par] = m.pool(lambda e: e.tensor_copy(total[:, par, :], sp[:, i, :]), s, running[par], r)
        elif j > 0:
            running[par] = m.pool(lambda e: e.tensor_tensor(total[:, par, :], total[:, par, :], sp[:, i, :], ALU.add),
                                  s, running[par], r)
        else:
            running[par] = r
        free["sp"][i] = [running[par], r]
        yield
        s = m.dve(lambda e: e.tensor_tensor(A[:, i, :], z[:, i, :], rb.view, ALU.subtract), r, free["A"][i])
        rb.readers = [s]
        free["z"][i] = s
        s = m.act(lambda e: e.activation(A[:, i, :], A[:, i, :], ACT.Exp), s)
        if j == b:
            s = m.pool(lambda e: e.affine_select(out=A[:, i, :], in_=A[:, i, :], compare_op=ALU.is_gt, fill=0.0, base=0,
                                                 pattern=[[0, 4], [1, P]], channel_multiplier=-1), s)
        yield
        for g in range(4):
            pv = m.pe(lambda e, g=g: e.matmul(
                out.view[64 * par:64 * par + 64, g * P:(g + 1) * P], v[:, j, 2 * g + par, :],
                A[:, i, g * P:(g + 1) * P], start=(j == b and g == 0), stop=(j == 0), skip_group_check=True),
                s, done["v"], out.readers if j == b and g == 0 else None)
        free["A"][i] = pv
        if j == 0:
            s = m.act(lambda e: e.activation(
                y[64 * par:64 * par + 64, :, b * P:(b + 1) * P],
                out.view[64 * par:64 * par + 64, :].rearrange("p (g t) -> p g t", g=4), ACT.Copy), pv)
            out.readers = [s]
            y_done.append(s)

    order = [(b, par, j) for b in range(NB) for j in range(b, -1, -1) for par in range(2)]
    interleave(m, (step_down(*x, n % DEEP) for n, x in enumerate(order)), DEEP, 1, 2)
    return y_done



DH, DP, DN, DG = 16, 64, 64, 2
HG = DH // DG


def ssd(m, c, io, hT, h_ready, y, fence):
    w_in = io["w_in_2"]
    X0 = 2048 + 1024
    DT0 = X0 + 1280
    base = m.top
    bT = m.take(T)
    cT = m.take(T)
    xtok = m.take(NB, 1024)
    btok = m.take(NB, P)
    rooms = m.take(4 * (T + 3))
    raw = rooms[:, 0:2 * (T + 3)].rearrange("p (j t) -> p j t", j=2)
    work = rooms[:, 2 * (T + 3):2 * (T + 3) + 2 * T].rearrange("p (j t) -> p j t", j=2)
    dtr = m.take(T)
    csr = m.take(T)
    tmpr = m.take(T)
    tokg = m.take(4, NB, DH)
    elast = m.take(NB, DH)
    cb = m.take(2, DG, P)
    E, W = [rooms[:, 1536 * i:1536 * (i + 1)].rearrange("p (j t) -> p j t", j=3) for i in range(2)]
    xdt, xw = (rooms[:, 3072:4096], tmpr), dtr
    state = m.take(BANK)
    yc = m.take(1024)
    stat = m.take(2, NB)
    if fence:
        for qq in (m.act, m.dve, m.pool):
            m_wait(qq, fence)
    for j in range(2):
        pad = m.pool(lambda e, j=j: e.memset(raw[:, j, 0:3], 0.0))
    raw_free = [None, None]
    done = {}
    xfree = [None, None]
    order = [(0, 4), (4, 8), (8, 10)]
    wfree = [None, None]
    late = []
    for t0, t1 in order:

        def evac(i, n, ps, step, t0=t0):
            t = t0 + i
            j = t % 2
            s = m.act(lambda e: e.activation(raw[:, j, 3 + n * BANK:3 + (n + 1) * BANK], ps, ACT.Copy), step, raw_free[j])
            if n == 1:
                dst = work[:, j, :] if t < 8 else (bT if t == 8 else cT)
                cv = depthwise_conv(m, c, raw[:, j, :], dst, t, 10, "conv_w_2", "conv_b_2", [s, pad], wfree[j] if t < 8 else None)
                raw_free[j] = cv
                a = m.act(lambda e, dst=dst: e.activation(dst, dst, ACT.Silu), cv)
                done[t] = a
                if late:
                    late.pop()()

                def to_tokens(t=t, dst=dst, a=a, j=j):
                    for g in range(2):
                        b = m.bank()
                        for i4 in range(4):
                            blk = g * 4 + i4
                            p = m.pe(lambda e, b=b, i4=i4, blk=blk, dst=dst: e.transpose(
                                b.view[:, i4 * P:(i4 + 1) * P], dst[:, blk * P:(blk + 1) * P], c.ident), a,
                                b.readers if i4 == 0 else None)
                        o = (xtok[:, g * 4:(g + 1) * 4, t * P:(t + 1) * P] if t < 8 else btok[:, g * 4:(g + 1) * 4, :])
                        p2 = m.dve(lambda e, b=b, o=o: e.tensor_copy(o, b.view.rearrange("p (k n) -> p k n", k=4)), p)
                        b.readers = [p2]
                    wfree[j] = p
                    done["tok", t] = p2

                if t <= 8:
                    late.append(to_tokens)
            return s

        project_channels(m, hT, h_ready, w_in, X0 + t0 * P, X0 + t1 * P, evac)
    R = slice(0, DH)
    rd = []

    def evac_dt(i, n, ps, step):
        s = m.dve(lambda e: e.tensor_scalar(dtr[R, n * BANK:(n + 1) * BANK], ps, c.vec("dt_bias_2")[R], None, ALU.add), step)
        rd.append(s)
        return s

    project_channels(m, hT, h_ready, w_in, DT0, DT0 + DH, evac_dt)
    if late:
        late.pop()()
    a = m.act(lambda e: e.activation(tmpr[R], dtr[R], ACT.Abs), rd)
    a = m.act(lambda e: e.activation(tmpr[R], tmpr[R], ACT.Exp, scale=-1.0), a)
    a = m.act(lambda e: e.activation(tmpr[R], tmpr[R], ACT.Ln, bias=1.0), a)
    dt_done = m.dve(lambda e: e.scalar_tensor_tensor(out=dtr[R], in0=dtr[R], scalar=0.0, in1=tmpr[R], op0=ALU.max,
                                                     op1=ALU.add), a)
    ah = m.take(1)
    a = m.act(lambda e: e.activation(ah[R], c.vec("a_log_2")[R], ACT.Exp))
    s = m.dve(lambda e: e.tensor_scalar(tmpr[R], dtr[R], ah[R], -1.0, ALU.mult, ALU.mult), a, dt_done)
    for blk in range(NB):
        s2 = m.dve(lambda e, blk=blk: e.tensor_tensor_scan(
            csr[R, blk * P:(blk + 1) * P], c.zero[R].to_broadcast([DH, P]), tmpr[R, blk * P:(blk + 1) * P], 0.0,
            ALU.add, ALU.add), s)
    cs_done = s2
    b = m.bank()
    for r, row in enumerate((dtr, csr)):
        for blk in range(NB):
            o = (r * NB + blk) * DH
            t = m.pe(lambda e, row=row, blk=blk, o=o, b=b: e.transpose(
                b.view[:, o:o + DH], row[R, blk * P:(blk + 1) * P], c.ident[R, 0:DH]), cs_done,
                b.readers if o == 0 else None)
    t0 = m.dve(lambda e, b=b: e.tensor_copy(tokg[:, 0:2].rearrange("p a k h -> p (a k h)"), b.view[:, 0:2 * NB * DH]), t)
    b.readers = [t0]
    b = m.bank()
    lastrow = m.take(P)
    s = m.pool(lambda e: e.memset(lastrow, 0.0))
    s = m.pool(lambda e: e.affine_select(out=lastrow, in_=lastrow, compare_op=ALU.not_equal, fill=1.0, base=-(P - 1),
                                         pattern=[[0, P]], channel_multiplier=1), s)
    flat = lambda i: tokg[:, i].rearrange("p k h -> p (k h)")
    t = m.pe(lambda e, b=b: e.matmul(b.view[:, 0:NB * DH], lastrow, flat(1), start=True, stop=True), s, t0, b.readers)
    s = m.act(lambda e, b=b: e.activation(elast.rearrange("p k h -> p (k h)"), b.view[:, 0:NB * DH], ACT.Exp), t)
    s1 = m.dve(lambda e, b=b: e.tensor_tensor(flat(3), b.view[:, 0:NB * DH], flat(1), ALU.subtract), t, s)
    b.readers = [s1]
    s = m.act(lambda e: e.activation(flat(3), flat(3), ACT.Exp), s1)
    s = m.act(lambda e: e.activation(flat(2), flat(1), ACT.Exp), t0)
    tok_ready = [t0, s]

    after = m.fence()
    for q_ in (m.act, m.dve, m.pool):
        m_wait(q_, after)
    DEEP = 3
    state_done = m.dve(lambda e: e.memset(state, 0.0))
    Efree, Wfree = [None] * DEEP, [None] * DEEP
    cb_free, xdt_free = [None, None], [None, None]
    xw_free = yc_free = None
    y_done = []
    heads = lambda v: v.rearrange("p (h d) -> p h d", h=v.shape[1] // DP)
    chunk = {}

    def four_heads(ck, h4, k):
        nonlocal state_done, xw_free, yc_free
        cols = slice(ck * P, (ck + 1) * P)
        half = ck % 2
        tok = lambda i: tokg[:, i, ck, :].unsqueeze(2).to_broadcast([P, DH, DP])
        if h4 == 0:
            cbs = []
            for g in range(DG):
                b = m.bank()
                s = m.pe(lambda e, b=b, g=g: e.matmul(b.view[:, 0:P], bT[g * DN:(g + 1) * DN, cols],
                                                      cT[g * DN:(g + 1) * DN, cols], start=True, stop=True),
                         done[8], done[9], b.readers)
                s = m.dve(lambda e, b=b, g=g: e.tensor_tensor(cb[:, half, g, :], b.view[:, 0:P], c.upper, ALU.mult), s,
                          cb_free[half])
                b.readers = [s]
                cbs.append(s)
            xd = m.dve(lambda e: e.tensor_tensor(heads(xdt[half]), heads(xtok[:, ck, :]), tok(0), ALU.mult),
                       tok_ready, xdt_free[half], [done["tok", t] for t in range(9)])
            chunk[ck] = [cbs, xd, None]
        cbs, xd, _ = chunk[ck]
        if h4 == 1:
            chunk[ck][2] = m.pool(lambda e: e.tensor_tensor(heads(xw), heads(xdt[half]), tok(3), ALU.mult), xd, xw_free,
                                  tok_ready)
        later = m.bank()
        for i in range(4):
            h = h4 * 4 + i
            s = m.pe(lambda e, i=i, h=h: e.matmul(later.view[:, i * P:(i + 1) * P], c.row_picker(DH, h), csr[R, cols],
                                                  start=True, stop=True), cs_done, later.readers if i == 0 else None)
        yield
        bcs = tokg[:, 1, ck, h4 * 4:h4 * 4 + 4].unsqueeze(2).to_broadcast([P, 4, P])
        four = lambda v: v.rearrange("p (h l) -> p h l", h=4)
        s = m.dve(lambda e: e.tensor_tensor(four(E[:, k, :]), four(later.view), bcs, ALU.subtract), s, tok_ready, Efree[k])
        later.readers = [s]
        s = m.dve(lambda e: e.tensor_scalar(E[:, k, :], E[:, k, :], 0.0, None, ALU.min), s)
        s = m.act(lambda e: e.activation(E[:, k, :], E[:, k, :], ACT.Exp), s)
        group = h4 // 2
        s = m.pool(lambda e: e.tensor_tensor(four(W[:, k, :]), four(E[:, k, :]),
                                             cb[:, half, group, :].unsqueeze(1).to_broadcast([P, 4, P]), ALU.mult),
                   s, cbs, Wfree[k])
        Efree[k] = s
        if h4 == 3:
            cb_free[half] = s
        yield
        yd = m.held
        for i in range(4):
            h = h4 * 4 + i
            o = yd[group].view[:, (h % HG) * DP:(h % HG + 1) * DP]
            t = m.pe(lambda e, o=o, i=i, h=h: e.matmul(o, W[:, k, i * P:(i + 1) * P], xdt[half][:, h * DP:(h + 1) * DP],
                                                       start=True, stop=True), s, xd,
                     yd[group].readers if h % HG == 0 else None)
        Wfree[k] = t
        if h4 < 3:
            return
        diag_done, xs = t, chunk[ck][2]
        xdt_free[half] = [diag_done, xs]
        reads = []
        for g in range(DG):
            b = m.bank()
            t = m.pe(lambda e, b=b, g=g: e.matmul(b.view, cT[g * DN:(g + 1) * DN, cols], state[g * DN:(g + 1) * DN, :],
                                                  start=True, stop=True), state_done, b.readers)
            reads.append((b, t))
        grown = []
        for g in range(DG if ck < NB - 1 else 0):
            gs = slice(g * DN, (g + 1) * DN)
            b = m.bank()
            t = m.pe(lambda e, b=b, gs=gs, g=g: e.matmul(b.view[gs, :], btok[:, ck, gs], xw[:, g * BANK:(g + 1) * BANK],
                                                         start=True, stop=True), xs, done["tok", 8], b.readers)
            grown.append((b, t))
            xw_free = t
        parts = []
        for g, (b, t) in enumerate(reads):
            o = yc[:, g * BANK:(g + 1) * BANK]
            wg = tokg[:, 2, ck, g * HG:(g + 1) * HG].unsqueeze(2).to_broadcast([P, HG, DP])
            s = m.dve(lambda e, b=b, o=o, wg=wg: e.tensor_tensor(heads(o), heads(b.view), wg, ALU.mult), t, tok_ready, yc_free)
            b.readers = [s]
            s = m.dve(lambda e, o=o, g=g: e.tensor_tensor(o, o, yd[g].view, ALU.add), s, diag_done)
            yd[g].readers = [s]
            parts.append(s)
        for g, (b, t) in enumerate(grown):
            gs = slice(g * DN, (g + 1) * DN)
            el = elast[gs, ck, g * HG:(g + 1) * HG].unsqueeze(2).to_broadcast([DN, HG, DP])
            st = state[gs, :]
            s = m.dve(lambda e, st=st, el=el: e.tensor_tensor(heads(st), heads(st), el, ALU.mult), reads[1][1], state_done)
            s = m.dve(lambda e, st=st, b=b, gs=gs: e.tensor_tensor(st, st, b.view[gs, :], ALU.add), s, t)
            b.readers = [s]
            state_done = [s]
        dsk = c.vecs("d_skip_2").unsqueeze(2).to_broadcast([P, DH, DP])
        s = m.pool(lambda e: e.tensor_tensor(heads(xtok[:, ck, :]), heads(xtok[:, ck, :]), dsk, ALU.mult), xd)
        s = m.pool(lambda e: e.tensor_tensor(yc, yc, xtok[:, ck, :], ALU.add), s, parts)
        yield
        for g in range(2):
            b = m.bank()
            for i in range(4):
                t = m.pe(lambda e, b=b, i=i, g=g: e.transpose(b.view[:, i * P:(i + 1) * P],
                                                             yc[:, (g * 4 + i) * P:(g * 4 + i + 1) * P], c.ident), s,
                         b.readers if i == 0 else None)
            s2 = m.act(lambda e, b=b, g=g: e.activation(
                y[:, g * 4:g * 4 + 4, cols], b.view.rearrange("p (i t) -> p i t", i=4), ACT.Copy), t)
            b.readers = [s2]
            y_done.append(s2)
        yc_free = t

    jobs = [four_heads(ck, h4, (4 * ck + h4) % DEEP) for ck in range(NB) for h4 in range(4)]
    interleave(m, jobs, DEEP, 2)
    z = [Slot(raw[:, j, 0:T], m.sem(f"ssd_z{j}")) for j in range(2)]
    m.background.run_until(io["gates_second"], SSD_Z_ROW + D)
    after = m.fence()
    done = []
    for t in range(8):
        zs = z[t % 2]
        row = SSD_Z_ROW + t * P
        arrived = zs.fill(m.sp, [(zs.view, io["gates_second"][row:row + P, :])],
                          m.background.arrived(io["gates_second"], row), after if t < 2 else None)
        s = m.act(lambda e, zs=zs: e.activation(zs.view, zs.view, ACT.Silu), arrived)
        s = m.dve(lambda e, t=t, zs=zs: e.tensor_tensor(y[:, t, :], y[:, t, :], zs.view, ALU.mult), s, y_done)
        zs.readers = [s]
        done.append(s)
    m.top = base
    return normalize(m, c, y, lambda k: done[k], "ssd_norm_g_2", y)



RH, RD = 8, 64
RL = 64
RC = T // RL


def rwkv(m, c, io, hT, h_ready, y, fence):
    w_in = io["w_in_2"]
    C0 = 2048 + 2320
    base = m.top
    alpha = m.take(4, T)
    beta = m.take(4, T)
    kappa = m.take(4, T)
    rho = m.take(4, T)
    plast = m.take(4, RC)
    mask4 = m.take(4, P)
    maskA = m.take(P)
    level = m.take(6, P)
    levelT0 = m.take(P)
    mark = m.top
    vT = m.take(4, T)
    raw = m.take(2, T + 1)
    lo = m.take(T)
    lo2 = m.take(T)
    room = m.weights.room
    lw, cs, aT, t1, t2 = [room[:, T * i:T * (i + 1)] for i in range(5)]
    wup, reset = raw[:, 0, 0:512], raw[:, 1, 0:T]
    if fence:
        for q_ in (m.act, m.dve, m.pool, m.sp):
            m_wait(q_, fence)
    pool = m.pool

    def tri(view, strict, transposed, size, n):
        s = pool(lambda e: e.memset(view, 1.0))
        s = pool(lambda e: e.affine_select(out=view, in_=view, compare_op=ALU.is_gt if strict else ALU.is_ge, fill=0.0,
                                           base=0, pattern=[[1 if transposed else -1, P]],
                                           channel_multiplier=-1 if transposed else 1), s)
        return same_block(view, size, s)

    def same_block(view, size, s):
        nb = P // size
        v = view.rearrange("p (b i) -> p b i", b=nb)
        s = pool(lambda e: e.affine_select(out=v, in_=v, compare_op=ALU.is_ge, fill=0.0, base=0,
                                           pattern=[[-size, nb], [0, size]], channel_multiplier=1), s)
        return pool(lambda e: e.affine_select(out=v, in_=v, compare_op=ALU.is_ge, fill=0.0, base=size - 1,
                                              pattern=[[size, nb], [0, size]], channel_multiplier=-1), s)

    for i, strict in enumerate((True, False, True, False)):
        tri(mask4[:, i, :], strict, True, RL, P)
    s = tri(maskA, True, False, RL, P)
    for k_ in range(6):
        s = tri(level[:, k_, :], True, False, 2 ** (k_ + 1), P)
    tri(levelT0, True, True, 2, P)
    sub = None
    for k_ in range(5, 0, -1):
        sub = m.dve(lambda e, k_=k_: e.tensor_tensor(level[:, k_, :], level[:, k_, :], level[:, k_ - 1, :], ALU.subtract),
                    pool.last, sub)
    masks = [pool.last, sub]
    for j in range(2):
        pad = m.dve(lambda e, j=j: e.memset(raw[:, j, 0:1], 0.0))

    raw_free = [None, None]
    turn = [0]

    def mix_tiles(c0, n, dst_of, then=None):
        done = {}

        def evac(i, h, ps, step):
            j = (turn[0] // 2) % 2
            turn[0] += 1
            s = m.act(lambda e: e.activation(raw[:, j, 1 + h * BANK:1 + (h + 1) * BANK], ps, ACT.Copy), step, raw_free[j])
            if h == 1:
                dst, free = dst_of(i)
                mu = c.vec("rw_mu_2", c0 + i)
                d = m.dve(lambda e: e.tensor_tensor(dst, raw[:, j, 0:T], raw[:, j, 1:T + 1], ALU.subtract), s, pad, free)
                d = m.dve(lambda e: e.scalar_tensor_tensor(out=dst, in0=dst, scalar=mu, in1=raw[:, j, 1:T + 1],
                                                           op0=ALU.mult, op1=ALU.add), d)
                raw_free[j] = d
                done[i] = d
                if then:
                    then(i, d)
            return s

        project_channels(m, hT, h_ready, w_in, C0 + c0 * P, C0 + (c0 + n) * P, evac)
        return done

    d = mix_tiles(16, 1, lambda i: (lo, None))
    lo_done = m.act(lambda e: e.activation(lo[0:64, :], lo[0:64, :], ACT.Tanh), d[0])
    r_done = mix_tiles(0, 4, lambda i: (rho[:, i, :], None))
    k_done = mix_tiles(4, 4, lambda i: (kappa[:, i, :], None))
    v_done = mix_tiles(8, 4, lambda i: (vT[:, i, :], None))
    gate = Slot(lo2, m.sem("rw_gate_out"))
    gate_rows = io["gates_second"][RW_Z_ROW:RW_Z_ROW + 512, :]

    def gate_tile(i):
        return lo2, gate.landed if gate.filled else None

    def gate_out(i, d):
        gate.fill(m.sp, [(gate_rows[i * P:(i + 1) * P, :], lo2)], d)

    mix_tiles(12, 4, gate_tile, gate_out)
    m.rw_gate = gate.landed

    h_free = m.fence()
    m_wait(m.act, h_free)
    m_wait(m.dve, h_free)
    s = m.dve(lambda e: e.memset(reset, 1.0))
    reset_ready = m.dve(lambda e: e.memset(reset.rearrange("p (c l) -> p c l", c=RC)[:, :, 0:1], 0.0), s)
    wslot = Slot(wup, m.sem("rw_up_in"))
    wl = wslot.fill(m.sp, [(wup[0:64, :], io["rw_w_up_2"]), (wup[64:128, :], io["rw_a_up_2"])], h_free)

    def block_sum(src, ready, use):
        for n in range(HALVES):
            b = m.bank()
            s = m.pe(lambda e, b=b, n=n: e.matmul(b.view, c.pair_ones, src[:, n * BANK:(n + 1) * BANK], start=True, stop=True),
                     ready, c.pair_ready, b.readers)
            b.readers = [use(slice(n * BANK, (n + 1) * BANK), b.view, s)]

    g = [None] * 8
    ready = {}
    prev = []
    DV = lambda f, *d: m.dve(f, m.dve.last, *d)
    for i in range(4):
        rr, kk_, vv = rho[:, i, :], kappa[:, i, :], vT[:, i, :]
        al, be = alpha[:, i, :], beta[:, i, :]
        for n in range(HALVES):
            cols = slice(n * BANK, (n + 1) * BANK)
            for base_, dst, bias in ((0, lw, "rw_w0_2"), (64, aT, "rw_a0_2")):
                b = m.bank()
                s = m.pe(lambda e, b=b, base_=base_, i=i, cols=cols: e.matmul(
                    b.view, wup[base_:base_ + 64, i * P:(i + 1) * P], lo[base_:base_ + 64, cols], start=True, stop=True),
                    wl, lo_done, d[0], b.readers)
                s = m.act(lambda e, b=b, dst=dst, bias=bias, i=i, cols=cols: e.activation(
                    dst[:, cols], b.view, ACT.Sigmoid, bias=c.vec(bias, i)), s, prev)
                b.readers = [s]
        DV(lambda e: e.tensor_scalar(lw, lw, -float(np.exp(-0.5)), None, ALU.mult), s)
        DV(lambda e: e.tensor_tensor_scan(cs, reset, lw, 0.0, ALU.mult, ALU.add), reset_ready)
        m.background.run(1)
        DV(lambda e, kk_=kk_, i=i: e.tensor_scalar(t1, kk_, c.vec("rw_k_k_2", i), None, ALU.mult), k_done[i])
        s = DV(lambda e: e.tensor_tensor(t2, t1, t1, ALU.mult))

        def norm(cols, ps, step):
            return m.act(lambda e, cols=cols: e.activation(t2[:, cols], ps, ACT.Sqrt), step)

        block_sum(t2, s, norm)
        s = m.act.last
        DV(lambda e: e.tensor_scalar(t2, t2, 1e-12, None, ALU.max), s)
        DV(lambda e: e.reciprocal(t2, t2))
        DV(lambda e: e.tensor_tensor(t1, t1, t2, ALU.mult))
        DV(lambda e, be=be: e.tensor_tensor(be, t1, aT, ALU.mult))
        m.background.run(2)
        DV(lambda e, i=i: e.tensor_scalar(aT, aT, -1.0, c.vec("rw_k_a_2", i), ALU.add, ALU.mult))
        DV(lambda e, kk_=kk_: e.scalar_tensor_tensor(out=kk_, in0=aT, scalar=1.0, in1=kk_, op0=ALU.add, op1=ALU.mult))
        DV(lambda e, rr=rr, kk_=kk_: e.tensor_tensor(t2, rr, kk_, ALU.mult), r_done[i])
        s = DV(lambda e, i=i: e.tensor_scalar(t2, t2, c.vec("rw_r_k_2", i), None, ALU.mult))

        def bonus(cols, ps, step, i=i):
            return m.dve(lambda e, cols=cols: e.tensor_tensor(y[:, i, cols], ps, vT[:, i, cols], ALU.mult), step, v_done[i])

        block_sum(t2, s, bonus)
        m.background.run(2)
        DV(lambda e: e.tensor_tensor(lw, cs, lw, ALU.subtract))
        s = m.act(lambda e: e.activation(lw, lw, ACT.Exp), m.dve.last)
        DV(lambda e, al=al: e.tensor_tensor(al, t1, lw, ALU.mult), s)
        s = m.act(lambda e: e.activation(aT, cs, ACT.Exp), m.dve.last)
        DV(lambda e, rr=rr: e.tensor_tensor(rr, rr, aT, ALU.mult), s)
        DV(lambda e, i=i: e.tensor_copy(plast[:, i, :], aT.rearrange("p (c l) -> p c l", c=RC)[:, :, RL - 1]))
        s = m.act(lambda e: e.activation(t2, cs, ACT.Exp, scale=-1.0), m.dve.last)
        DV(lambda e, be=be: e.tensor_tensor(be, be, t2, ALU.mult), s)
        DV(lambda e, kk_=kk_: e.tensor_tensor(kk_, kk_, t2, ALU.mult))
        prev = [m.dve.last]
    prepared = [m.dve.last, m.act.last, m.pe.last]

    m.top = mark + 4 * T
    tokv = m.take(4, P)
    toka = m.take(4, P)
    tokb = m.take(4, P)
    tokk = m.take(4, P)
    scaled = room[:, 8192:9216].rearrange("p (r i t) -> p r i t", r=2, i=4)
    gram = room[:, 0:4096].rearrange("p (h g t) -> p h g t", h=RH, g=4)
    A, X, Z, Wm = [room[:, 4096 + 1024 * i:5120 + 1024 * i].rearrange("p (h t) -> p h t", h=RH) for i in range(4)]
    rhs = Wm
    U = X
    E = m.take(4, P)
    Gt = m.take(2, 4, RD)
    S = m.take(4, RD)
    outputs = [m.take(4, P) for _ in range(2)]
    sq, mean = scaled[:, 0], scaled[:, 1]
    flat = lambda v: v.rearrange("p i t -> p (i t)")
    y_done = []

    def group_norm(Y, cols, ready):
        b = m.bank()
        t = m.pe(lambda e, b=b: e.matmul(b.view, c.pair_ones, flat(Y), start=True, stop=True), ready, b.readers)
        s = m.dve(lambda e, b=b: e.scalar_tensor_tensor(out=flat(Y), in0=b.view, scalar=-1.0 / RD, in1=flat(Y), op0=ALU.mult,
                                                        op1=ALU.add), t)
        b.readers = [s]
        s = m.act(lambda e: e.activation(flat(sq), flat(Y), ACT.Square), s, y_done)
        yield
        b = m.bank()
        t = m.pe(lambda e, b=b: e.matmul(b.view, c.pair_ones, flat(sq), start=True, stop=True), s, b.readers)
        s = m.dve(lambda e, b=b: e.tensor_scalar(flat(mean), b.view, 1.0 / RD, 64e-5, ALU.mult, ALU.add), t)
        b.readers = [s]
        s = root_of_inverse(m, flat(mean), s)
        yield
        s = m.dve(lambda e: e.tensor_tensor(Y, Y, mean, ALU.mult), s)
        for i in range(4):
            s = m.dve(lambda e, i=i: e.tensor_scalar(Y[:, i, :], Y[:, i, :], c.vec("rw_ln_g_2", i), c.vec("rw_ln_b_2", i),
                                                     ALU.mult, ALU.add), m.dve.last)
        y_done.append(m.dve(lambda e: e.tensor_tensor(y[:, :, cols], y[:, :, cols], Y, ALU.add), s))

    norm_before = iter(())
    s_state = m.dve(lambda e: e.memset(S, 0.0), prepared)
    m_wait(m.act, prepared)
    last_of_block = None
    quads = [range(0, 4), range(4, 8)]
    for blk in range(NB):
        cols = slice(blk * P, (blk + 1) * P)
        Y = outputs[blk % 2]
        chunk0 = 2 * blk
        pl = plast[:, :, 2 * blk:2 * blk + 2].unsqueeze(3).to_broadcast([P, 4, 2, RL])
        spl = []
        for r_, src in ((0, beta), (1, kappa)):
            for cc in range(2):
                plc = plast[:, :, 2 * blk + cc].unsqueeze(2).to_broadcast([P, 4, RL])
                ccols = slice(blk * P + cc * RL, blk * P + (cc + 1) * RL)
                s = m.dve(lambda e, r_=r_, src=src, plc=plc, cc=cc, ccols=ccols: e.tensor_tensor(
                    scaled[:, r_, :, cc * RL:(cc + 1) * RL], src[:, :, ccols], plc, ALU.mult), last_of_block)
            spl.append(s)
        grams = []
        for h in range(RH):
            i, e0 = h // 2, RD * (h % 2)
            es = slice(e0, e0 + RD)
            b = m.bank()
            for r_, lhs in ((0, beta), (1, kappa)):
                for q_, rh in ((0, alpha), (1, rho)):
                    t = m.pe(lambda e, b=b, i=i, es=es, lhs=lhs, rh=rh, r_=r_, q_=q_, cols=cols: e.matmul(
                        b.view[:, (2 * r_ + q_) * P:(2 * r_ + q_ + 1) * P], lhs[es, i, cols], rh[es, i, cols],
                        start=True, stop=True), prepared, b.readers if r_ + q_ == 0 else None)
            s = m.dve(lambda e, b=b, h=h: e.tensor_tensor(gram[:, h], b.view.rearrange("p (g t) -> p g t", g=4), mask4,
                                                          ALU.mult), t, masks, last_of_block)
            b.readers = [s]
            grams.append(s)
        for par in range(2):
            b = m.bank()
            for i in range(4):
                es = slice(RD * par, RD * par + RD)
                t = m.pe(lambda e, b=b, i=i, es=es, cols=cols: e.matmul(b.view[:, i * P:(i + 1) * P], alpha[es, i, cols],
                                                            beta[es, i, cols], start=True, stop=True),
                         prepared, b.readers if i == 0 else None)
            s = m.dve(lambda e, b=b, par=par: e.tensor_tensor(
                A[:, par:RH:2, :], b.view.rearrange("p (h s) -> p h s", h=4),
                maskA.unsqueeze(1).to_broadcast([P, 4, P]), ALU.mult), t, masks, last_of_block)
            b.readers = [s]
        a_done = s
        for dst, src, dep in ((tokv, vT[:, :, cols], None), (toka, alpha[:, :, cols], None),
                              (tokb, scaled[:, 0], spl[0]), (tokk, scaled[:, 1], spl[1])):
            b = m.bank()
            for i in range(4):
                t = m.pe(lambda e, b=b, i=i, src=src: e.transpose(b.view[:, i * P:(i + 1) * P], src[:, i, :], c.ident),
                         dep, prepared, b.readers if i == 0 else None)
            t = m.act(lambda e, b=b, dst=dst: e.activation(dst.rearrange("p i n -> p (i n)"), b.view, ACT.Copy), t, last_of_block)
            b.readers = [t]
        tok_done = t
        next(norm_before, None)
        wide = lambda v, n=RH: v.unsqueeze(1).to_broadcast([P, n, P])
        idw = wide(c.ident)
        s = m.dve(lambda e: e.tensor_tensor(X, A, wide(level[:, 0, :]), ALU.mult), a_done, last_of_block)
        sx = m.dve(lambda e: e.tensor_tensor(X, idw, X, ALU.subtract), s)
        s = m.pool(lambda e: e.tensor_tensor(Z, gram[:, :, 0, :], wide(levelT0), ALU.mult), grams, last_of_block)
        sz = m.pool(lambda e: e.tensor_tensor(Z, idw, Z, ALU.subtract), s)
        m.background.run(1)
        xd, zd = [sx, sx], [sz, sz]
        for k_ in range(1, 6):
            w_ = [None, None]
            for qi, quad in enumerate(quads):
                hs = slice(4 * qi, 4 * qi + 4)
                b = m.bank()
                for i, h in enumerate(quad):
                    t = m.pe(lambda e, b=b, i=i, h=h: e.matmul(b.view[:, i * P:(i + 1) * P], gram[:, h, 0, :], X[:, h, :],
                                                              start=True, stop=True), xd[qi], grams,
                             b.readers if i == 0 else None)
                w_[qi] = m.dve(lambda e, b=b, hs=hs, k_=k_: e.tensor_tensor(
                    Wm[:, hs, :], b.view.rearrange("p (h s) -> p h s", h=4), wide(level[:, k_, :], 4), ALU.mult), t,
                    zd[qi], last_of_block)
                b.readers = [w_[qi]]
            for qi, quad in enumerate(quads):
                hs = slice(4 * qi, 4 * qi + 4)
                if k_ < 5:
                    b = m.bank()
                    for i, h in enumerate(quad):
                        t = m.pe(lambda e, b=b, i=i, h=h: e.matmul(b.view[:, i * P:(i + 1) * P], Z[:, h, :], Wm[:, h, :],
                                                                  start=True, stop=True), w_[qi], zd[qi],
                                 b.readers if i == 0 else None)
                    xd[qi] = m.dve(lambda e, b=b, hs=hs: e.tensor_tensor(
                        X[:, hs, :], X[:, hs, :], b.view.rearrange("p (h s) -> p h s", h=4), ALU.subtract), t)
                    b.readers = [xd[qi]]
                b = m.bank()
                for i, h in enumerate(quad):
                    t = m.pe(lambda e, b=b, i=i, h=h: e.matmul(b.view[:, i * P:(i + 1) * P], Wm[:, h, :], Z[:, h, :],
                                                              start=True, stop=True), w_[qi], zd[qi],
                             b.readers if i == 0 else None)
                zd[qi] = m.dve(lambda e, b=b, hs=hs: e.tensor_tensor(
                    Z[:, hs, :], Z[:, hs, :], b.view.rearrange("p (h s) -> p h s", h=4), ALU.subtract), t)
                b.readers = [zd[qi]]
            if k_ in (1, 3):
                next(norm_before, None)
            if k_ == 1:
                for _ in range(3):
                    m.background.step()
        m.background.step()
        b = m.bank()
        for h in range(RH):
            t = m.pe(lambda e, b=b, h=h: e.matmul(b.view[:, h * RD:(h + 1) * RD], gram[:, h, 2, :],
                                                  tokv[:, h // 2, RD * (h % 2):RD * (h % 2) + RD], start=True, stop=True),
                     grams, tok_done, b.readers if h == 0 else None)
        s1 = m.act(lambda e, b=b: e.activation(rhs[:, :, RD:P], b.view.rearrange("p (h d) -> p h d", h=RH), ACT.Copy), t,
                   zd)
        b.readers = [s1]
        s2 = m.act(lambda e: e.activation(rhs[:, :, 0:RD], toka.rearrange("p i (e d) -> p (i e) d", e=2), ACT.Copy), tok_done,
                   zd)
        ud = []
        for qi, quad in enumerate(quads):
            b = m.bank()
            for i, h in enumerate(quad):
                t = m.pe(lambda e, b=b, i=i, h=h: e.matmul(b.view[:, i * P:(i + 1) * P], Z[:, h, :], rhs[:, h, :],
                                                          start=True, stop=True), zd[qi], s1, s2,
                         b.readers if i == 0 else None)
            s = m.act(lambda e, b=b, qi=qi: e.activation(U[:, 4 * qi:4 * qi + 4, :].rearrange("p h n -> p (h n)"), b.view,
                                                         ACT.Copy, scale=-1.0), t, last_of_block)
            b.readers = [s]
            ud.append(s)
        m.background.step()
        b = m.bank()
        for h in range(RH):
            i, e0 = h // 2, RD * (h % 2)
            t = m.pe(lambda e, b=b, h=h, i=i, e0=e0: e.matmul(b.view[e0:e0 + RD, i * P:(i + 1) * P], U[:, h, 0:RD],
                                                              gram[:, h, 1, :], start=True, stop=True), ud, grams,
                     b.readers if h == 0 else None)
        e_done = m.dve(lambda e, b=b, cols=cols: e.tensor_tensor(E, b.view.rearrange("p (i t) -> p i t", i=4), rho[:, :, cols],
                                                      ALU.add), t, last_of_block)
        b.readers = [e_done]
        gd = []
        for cc in range(2):
            rs = slice(cc * RL, (cc + 1) * RL)
            b = m.bank()
            for h in range(RH):
                i, e0 = h // 2, RD * (h % 2)
                t = m.pe(lambda e, b=b, h=h, i=i, e0=e0, rs=rs: e.matmul(
                    b.view[e0:e0 + RD, i * RD:(i + 1) * RD], U[rs, h, 0:RD], tokb[rs, i, e0:e0 + RD], start=True, stop=True),
                    ud, tok_done, b.readers if h == 0 else None)
            for i in range(4):
                s = m.dve(lambda e, b=b, i=i, cc=cc, chunk0=chunk0: e.scalar_tensor_tensor(
                    out=Gt[:, cc, i, :], in0=c.stacked_ident, scalar=plast[:, i, chunk0 + cc:chunk0 + cc + 1],
                    in1=b.view[:, i * RD:(i + 1) * RD], op0=ALU.mult, op1=ALU.add), t, last_of_block, c.stacked_ready)
            b.readers = [s]
            gd.append(s)
        yb = m.bank()
        for h in range(RH):
            i, e0 = h // 2, RD * (h % 2)
            o = yb.view[e0:e0 + RD, i * P:(i + 1) * P]
            m.pe(lambda e, o=o, h=h: e.matmul(o, U[:, h, RD:P], gram[:, h, 1, :], start=True, stop=False,
                                              skip_group_check=True), ud, grams, yb.readers if h == 0 else None)
            t = m.pe(lambda e, o=o, h=h, i=i, e0=e0: e.matmul(o, tokv[:, i, e0:e0 + RD], gram[:, h, 3, :], start=False,
                                                              stop=True, skip_group_check=True), tok_done)
        y1 = m.act(lambda e, yb=yb, Y=Y: e.activation(Y.rearrange("p i t -> p (i t)"), yb.view, ACT.Copy), t, last_of_block)
        yb.readers = [y1]
        for cc in range(2):
            rs = slice(cc * RL, (cc + 1) * RL)
            for par in range(2):
                es = slice(RD * par, RD * par + RD)
                b2 = m.bank()
                for i in range(4):
                    t = m.pe(lambda e, b2=b2, es=es, i=i, cc=cc: e.matmul(
                        b2.view[es, i * RL:(i + 1) * RL], S[es, i, :], E[es, i, cc * RL:(cc + 1) * RL],
                        start=True, stop=True), s_state, e_done, b2.readers if i == 0 else None)
                s = m.dve(lambda e, b2=b2, es=es, cc=cc, Y=Y: e.tensor_tensor(
                    Y[es, :, cc * RL:(cc + 1) * RL], Y[es, :, cc * RL:(cc + 1) * RL],
                    b2.view[es, 0:4 * RL].rearrange("p (i t) -> p i t", i=4), ALU.add), t, y1)
                b2.readers = [s]
            read_state = t
            hb = m.bank()
            for h in range(RH):
                i, e0 = h // 2, RD * (h % 2)
                o = hb.view[e0:e0 + RD, i * RD:(i + 1) * RD]
                m.pe(lambda e, o=o, h=h, i=i, e0=e0, rs=rs: e.matmul(o, tokb[rs, i, e0:e0 + RD], U[rs, h, RD:P], start=True,
                                                                    stop=False, skip_group_check=True),
                     hb.readers if h == 0 else None)
                t = m.pe(lambda e, o=o, h=h, i=i, e0=e0, rs=rs: e.matmul(o, tokk[rs, i, e0:e0 + RD], tokv[rs, i, e0:e0 + RD],
                                                                        start=False, stop=True, skip_group_check=True))
            hs_done = t
            gb = [m.bank(), m.bank()]
            for par in range(2):
                es = slice(RD * par, RD * par + RD)
                for i in range(4):
                    t = m.pe(lambda e, b=gb[par], es=es, i=i, cc=cc: e.matmul(
                        b.view[es, i * RD:(i + 1) * RD], Gt[es, cc, i, :], S[es, i, :], start=True, stop=True),
                        s_state, gd[cc], gb[par].readers if i == 0 else None)
            s = m.dve(lambda e, hb=hb: e.tensor_copy(S, hb.view[:, 0:4 * RD].rearrange("p (i d) -> p i d", i=4)), t, hs_done)
            hb.readers = [s]
            for par in range(2):
                es = slice(RD * par, RD * par + RD)
                s2 = m.dve(lambda e, b=gb[par], es=es: e.tensor_tensor(
                    S[es], S[es], b.view[es, 0:4 * RD].rearrange("p (i d) -> p i d", i=4), ALU.add), s)
                gb[par].readers = [s2]
            s_state = s2
            m.background.step()
        m.background.step()
        norm_before = group_norm(Y, cols, m.dve.last)
        last_of_block = [m.pe.last, m.dve.last, m.act.last]
    m.background.run(1)
    for _ in norm_before:
        pass
    m.top = base
    m.weights.give_back(m.fence())
    return y_done



def channels(dram):
    return dram.rearrange("(k p) t -> p k t", p=P)


def normalize(m, c, x, ready, gain, out=None, pair=None):
    base = m.top
    squares = m.take(2, T)
    rows = m.take(T)
    scaled = m.take(2, T) if pair is not None else None
    fence = m.fence()
    for q in (m.act, m.dve, m.pool):
        m_wait(q, fence)
    r = rms_rows(m, c, x, ready, squares, rows)
    done, free = [], [None, None]
    for k in range(KD):
        dst = out[:, k, :] if pair is None else scaled[:, k % 2, :]
        s = m.dve(lambda e, k=k, dst=dst: e.scalar_tensor_tensor(
            out=dst, in0=x[:, k, :], scalar=c.vec(gain, k), in1=rows, op0=ALU.mult, op1=ALU.mult), r, ready(k), free[k % 2])
        if pair is not None:
            s = split(m, dst, [pair[:, i, k, :] for i in range(2)], s, low=(m.pool, m.dve)[k % 2])
            free[k % 2] = s
        done.append(s)
    m.top = base
    return done


def merge(m, c, io, name, h, gates, branches, w_out, residual):
    base = m.top
    fence = m.fence()
    for q in (m.act, m.dve, m.pool):
        m_wait(q, fence)
    operands = [m.take_pair(kt, T) for _, _, kt, _, _, _ in branches]
    mark = m.top
    y_in = [m.slot(f"{name}_y{i}", T) for i in range(3)]
    z_in = [m.slot(f"{name}_z{i}", T) for i in range(3)]
    pieces = [{} for _ in branches]
    tiles = [(i, k) for i, branch in enumerate(branches) for k in range(branch[2])]
    landed_tiles = []

    def fetch():
        n = len(landed_tiles)
        if n == len(tiles):
            return
        i, k = tiles[n]
        y, arrived, _, _, z_row, z_arrived = branches[i]
        ys, zs = y_in[n % len(y_in)], z_in[n % len(z_in)]
        y_l, z_l = ys.fill(m.sp, [(ys.view, channels(y)[:, k, :])], arrived, fence), None
        if z_row is not None:
            row = z_row + k * P
            z_l = zs.fill(m.sp, [(zs.view, gates[row:row + P, :])], z_arrived(row), fence)
        landed_tiles.append((ys, zs, y_l, z_l))

    def prepare(i):
        for n, (owner, k) in enumerate(tiles):
            if owner != i:
                continue
            pair = operands[i]
            ys, zs, y_l, z_l = landed_tiles[n]
            ready = y_l
            if z_l is not None:
                z_l = m.act(lambda e, zs=zs: e.activation(zs.view, zs.view, ACT.Silu), z_l)
                ready = m.dve(lambda e, ys=ys, zs=zs: e.tensor_tensor(ys.view, ys.view, zs.view, ALU.mult), y_l, z_l)
                zs.readers = [ready]
            done = split(m, ys.view, [pair[:, part, k, :] for part in range(2)], ready, low=(m.pool, m.dve)[n % 2])
            ys.readers = done
            pieces[i][k] = done
            fetch()

    gate = [m.slot(f"{name}_gate{i}", T) for i in range(3)]
    gate_rows = [i * D + g0 + t * P for g0 in range(0, D, GROUP) for i in range(len(branches)) for t in range(GROUP // P)]
    gate_landed = []

    def fetch_gate():
        n = len(gate_landed)
        if n < len(gate_rows):
            gs, row = gate[n % len(gate)], gate_rows[n]
            gate_landed.append(gs.fill(m.act, [(gs.view, gates[row:row + P, :])], m.background.arrived(gates, row), fence))

    total = m.take(8, BANK)
    gated = m.take(2, BANK)
    merged = h
    turn = 0
    added = {}
    gated_free = [None, None]
    total_free = [None] * 8
    merged_ready = {k: [] for k in range(KD)}
    for _ in y_in:
        fetch()
    m.weights.prepare()
    fetch_gate()
    fetch_gate()
    m.background.finish()
    h_read = m.pe.last
    prepare(0)
    for g0 in range(0, D, GROUP):
        for i, (_, _, kt, w_b, _, _) in enumerate(branches):
            if g0 == 0 and i + 1 < len(branches):
                prepare(i + 1)
            w, landed, read_by = m.weights.take(w_b, g0, g0 + GROUP)
            for t in range(GROUP // P):
                fetch_gate()
                gs = gate[turn % len(gate)]
                g_l = m.act(lambda e, gs=gs: e.activation(gs.view, gs.view, ACT.Sigmoid), gate_landed[turn])
                turn += 1
                for half in range(HALVES):
                    cols = slice(half * BANK, (half + 1) * BANK)
                    b = m.bank()
                    s = product(m, b.view, lambda a, k, w=w, t=t: w[:, a, k, t * P:(t + 1) * P],
                                lambda a, k, i=i, cols=cols: operands[i][:, a, k, cols], kt, [landed, lambda k, i=i: pieces[i][k]], b.readers)
                    read_by(s)
                    q = 4 * (g0 // GROUP % 2) + 2 * t + half
                    o = total[:, q, :]
                    if i == 0:
                        s = m.dve(lambda e, b=b, o=o, gs=gs, cols=cols: e.tensor_tensor(
                            o, b.view, gs.view[:, cols], ALU.mult), s, g_l, total_free[q])
                        added[q] = s
                    else:
                        x = gated[:, half, :]
                        s = m.dve(lambda e, b=b, x=x, gs=gs, cols=cols: e.tensor_tensor(
                            x, b.view, gs.view[:, cols], ALU.mult), s, g_l, gated_free[half])
                        added[q] = m.pool(lambda e, o=o, x=x: e.tensor_tensor(o, o, x, ALU.add), s, added[q])
                        gated_free[half] = added[q]
                    b.readers = [s]
                    gs.readers = [s]
                    if i == len(branches) - 1:
                        total_free[q] = split(m, o, [merged[:, a, g0 // P + t, cols] for a in range(2)], added[q], h_read)
                        merged_ready[g0 // P + t] += total_free[q]
    x_out = m.arena[:, base:base + KD * T].rearrange("p (k t) -> p k t", k=KD)
    m.top = mark
    over = m.fence()
    res = [m.slot(f"{name}_residual{i}", T) for i in range(2)]
    arrived, done = {}, {}

    def evac(d, n, ps, step):
        j = d % 2
        if n == 0:
            arrived[d] = res[j].fill(m.sp, [(res[j].view, channels(residual)[:, d, :])], over)
        cols = slice(n * BANK, (n + 1) * BANK)
        s = m.dve(lambda e: e.tensor_tensor(x_out[:, d, cols], ps, res[j].view[:, cols], ALU.add), step, arrived[d], over)
        res[j].readers = [s]
        done[d] = s
        return s

    project_channels(m, merged, lambda k: merged_ready[k], w_out, 0, D, evac)
    m.top = base
    return x_out, done


def both_blocks(nc, ctx, io):
    m, c = setup(nc, ctx, io)
    h = m.take_pair(KD, T)
    base = m.top
    w1, w2 = io["w_in"], io["w_in_2"]

    G0 = 2 * 512 + 3 * 512 + 8 + 512
    wide = QR + 2 * AD + ID + IH
    for dram, c0, c1, kt in ((w1, 0, 512, KD), (io["glu_w"], 0, 512, 4), (w1, 1024, 1536, KD), (w1, 1536, 2048, KD),
                             (w1, 2048, 2560, KD), (w1, 2560, 2568, KD), (w1, G0, G0 + QR, KD),
                             (w1, G0 + QR + AD, G0 + wide, KD), (w1, G0 + QR, G0 + QR + AD, KD),
                             (io["w_qidx"], 0, 512, 2), (io["w_uq"], 0, 512, 2)):
        m.weights.extend(dram, c0, c1, kt)
    for g0 in range(0, D, GROUP):
        for i in range(3):
            m.weights.extend(io[f"w_branch{i}"], g0, g0 + GROUP, 4)
    m.weights.extend(io["w_out"], 0, D)
    X0 = 4 * 512 + D
    R0 = X0 + 1280 + DH
    for c0, n in ((512, 512), (0, 512), (1024, 512), (X0, 512), (X0 + 512, 512), (X0 + 1024, 256), (X0 + 1280, DH),
                  (R0 + 2048, P), (R0, 512), (R0 + 512, 512), (R0 + 1024, 512), (R0 + 1536, 512)):
        m.weights.extend(w2, c0, c0 + n)

    x = m.take(KD, T)
    x_slots = [Slot(x[:, k, :], m.sem(f"x_in{k}")) for k in range(KD)]
    x_in = [s.fill(m.sp, [(s.view, channels(io["xT"])[:, k, :])]) for k, s in enumerate(x_slots)]
    h_tiles = normalize(m, c, x, lambda k: x_in[k], "norm_g", pair=h)
    h_ready = lambda k: h_tiles[k]

    def run_mixer(mixer, kt, dram):
        m.top = base
        fence = m.fence()
        y = m.take(kt, T)
        slot = Slot(y, m.sem("out_" + mixer.__name__))
        for q in (m.act, m.dve, m.pool):
            m_wait(q, [fence, run_mixer.stored])
        last = mixer(m, c, io, h, h_ready, y, [fence, run_mixer.stored])
        run_mixer.stored = slot.fill(m.sp, [(channels(dram), y)], last)
        m.top = base
        return run_mixer.stored

    run_mixer.stored = None
    gates = io["gates_first"]
    z_columns = (512, 2568, G0 + wide)
    for c0, row in zip(z_columns, FIRST_Z_ROWS):
        m.background.add(h, h_ready, w1, c0, c0 + 512, gates, row)
    m.background.add(h, h_ready, w1, G0 + wide + 512, G0 + wide + 512 + 3 * D, gates, 0)
    ys = [run_mixer(f, 4, io[f"y_first{i}"]) for i, f in enumerate((s5, mlstm, dsa))]
    z_arrived = lambda row: m.background.arrived(gates, row)
    x, x_done = merge(m, c, io, "merge_first", h, gates,
                      [(io[f"y_first{i}"], ys[i], 4, io[f"w_branch{i}"], FIRST_Z_ROWS[i], z_arrived) for i in range(3)],
                      io["w_out"], io["xT"])
    m.top = base + KD * T
    x_done = normalize(m, c, x, lambda k: x_done[k], "final_norm_g", out=x)
    kept = Slot(x, m.sem("x_middle_out")).fill(m.sp, [(channels(io["x_middle"]), x)], x_done)
    h_tiles_2 = normalize(m, c, x, lambda k: x_done[k], "norm_g_2", pair=h)
    h_ready = lambda k: h_tiles_2[k]
    run_mixer.stored = kept

    gates_2 = io["gates_second"]
    m.background.add(h, h_ready, w2, 1536, 2048, gates_2, SB_Z_ROW)
    m.background.add(h, h_ready, w2, 2048, 3072, gates_2, SSD_Z_ROW)
    m.background.add(h, h_ready, w2, R0 + 2176, R0 + 2176 + 3 * D, gates_2, 0)
    ys = [run_mixer(f, kt, io[f"y_second{i}"]) for i, (f, kt) in enumerate(((stick_breaking, 4), (ssd, 8), (rwkv, 4)))]
    weights = (io["w_out_sb_2"], io["w_out_ssd_2"], io["w_out_rw_2"])
    for g0 in range(0, D, GROUP):
        for w, kt in zip(weights, (4, 8, 4)):
            m.weights.extend(w, g0, g0 + GROUP, kt)
    m.weights.extend(io["w_o_2"], 0, D)
    x, x_done = merge(m, c, io, "merge_second", h, gates_2,
                      [(io["y_second0"], ys[0], 4, weights[0], SB_Z_ROW, lambda row: m.background.arrived(gates_2, row)),
                       (io["y_second1"], ys[1], 8, weights[1], None, None),
                       (io["y_second2"], ys[2], 4, weights[2], RW_Z_ROW, lambda row: m.rw_gate)],
                      io["w_o_2"], io["x_middle"])
    m.top = base + KD * T
    x_done = normalize(m, c, x, lambda k: x_done[k], "final_g_2", out=x)
    out = [Slot(x[:, k, :], m.sem(f"result_out{k}")) for k in range(KD)]
    m_wait(m.sp, [s.fill(m.sp, [(channels(io["result"])[:, k, :], s.view)], x_done[k]) for k, s in enumerate(out)])
    m.play()
    return m



def channel_columns(a):
    return np.ascontiguousarray(a.reshape(-1, P).T)


def pack_vectors(x):
    v = np.zeros((P, VEC_N), np.float32)

    def put(name, a):
        c0, n = VEC_AT[name]
        assert a.shape[1] == n, name
        v[0:a.shape[0], c0:c0 + n] = a

    for name in ("norm_g", "ssm_d", "glu_b", "qk_conv_b", "mh_norm_g", "q_norm_g", "norm_g_2", "conv_b_2",
                 "ssd_norm_g_2", "rw_mu_2", "rw_w0_2", "rw_a0_2", "rw_k_k_2", "rw_k_a_2", "rw_r_k_2", "rw_ln_g_2",
                 "rw_ln_b_2", "final_norm_g", "final_g_2"):
        put(name, channel_columns(x[name].reshape(-1)))
    for name in ("qk_conv_w", "conv_w_2"):
        taps = x[name][0]
        put(name, np.concatenate([channel_columns(taps[k]) for k in range(4)], axis=1))
    for name in ("kidx_norm_g", "kidx_norm_b"):
        put(name, np.concatenate([x[name].reshape(-1, 1)] * 2, axis=0))
    for name in ("igate_b", "fgate_b", "dt_bias_2", "a_log_2"):
        put(name, x[name].reshape(-1, 1))
    put("d_skip_2", np.repeat(x["d_skip_2"].reshape(1, 16), P, axis=0))
    put("ssm_a_re", channel_columns(x["ssm_a_re"].reshape(-1)))
    put("ssm_a_im", channel_columns(x["ssm_a_im"].reshape(-1)))
    put("ssm_log_dt", channel_columns(np.repeat(x["ssm_log_dt"].reshape(-1), 64)))
    return v


def lay_out(x):
    arrays = {"xT": np.ascontiguousarray(x["x"][0].T), "vectors": pack_vectors(x)}
    arrays["ssm_b"] = np.ascontiguousarray(np.stack(
        [x[n][0].reshape(16, P, 16).transpose(1, 0, 2) for n in ("ssm_b_re", "ssm_b_im")], axis=1).reshape(P, -1))
    arrays["ssm_c"] = np.ascontiguousarray(np.stack(
        [x[n][0].transpose(0, 2, 1).reshape(16, P, 16).transpose(1, 0, 2) for n in ("ssm_c_re", "ssm_c_im")],
        axis=1).reshape(P, -1))
    for name in ("w_in", "w_out", "glu_w", "w_uq", "w_qidx", "w_in_2", "w_out_sb_2", "w_out_ssd_2", "w_out_rw_2",
                 "w_o_2", "rw_w_up_2", "rw_a_up_2"):
        arrays[name] = np.ascontiguousarray(x[name][0])
    for i in range(3):
        arrays[f"w_branch{i}"] = np.ascontiguousarray(x["w_branch"][0, i])
    return arrays


def kernel(**inputs):
    import concourse.bacc as bacc
    from concourse.bass_utils import run_bass_kernel_spmd

    nc = bacc.Bacc("TRN2", target_bir_lowering=False, num_devices=1)
    arrays = lay_out({name: np.asarray(a) for name, a in inputs.items()})
    io = {name: nc.dram_tensor(f"in_{name}", a.shape, F32, kind="ExternalInput").ap() for name, a in arrays.items()}
    for name, shape in SCRATCH:
        io[name] = nc.dram_tensor(name, shape, F32, kind="Internal").ap()
    io["result"] = nc.dram_tensor("result", (D, T), F32, kind="ExternalOutput").ap()
    with ExitStack() as ctx:
        both_blocks(nc, ctx, io)
    done = run_bass_kernel_spmd(nc, [{f"in_{name}": a for name, a in arrays.items()}], core_ids=[0])
    return np.ascontiguousarray(done.results[0]["result"].T).reshape(1, T, D)
```
